# Optimizing a Trainium2 kernel written in Bass

```python
import math
import jax, jax.numpy as jnp
from jax import lax
import numpy as np

D_MODEL = 1024
BATCH = 1
SEQ = 512
DEPTH = 1
DEC_BATCH = 8
DEC_SEQ = 1
PAST_LEN = 4096
PAGE_SIZE = 128

N_META = 16
D_MIX = D_MODEL
EPS = 1e-6
GLA_HEADS = 4
GLA_DV = D_MIX // 2 // GLA_HEADS
GLA_DK = GLA_DV // 2
GLA_GATE_RANK = 16
GLA_GATE_NORM = 16.0
GLA_CHUNK = 64
MLA_HEADS = 4
MLA_NOPE = 128
MLA_ROPE = 64
MLA_V = (D_MIX - GLA_HEADS * GLA_DV) // MLA_HEADS
Q_LORA = 384
KV_LORA = 256
ROPE_THETA = 10000.0
MLA_SCALE = (MLA_NOPE + MLA_ROPE) ** -0.5
Q_BLOCK = 128
D_FF = -(-8 * D_MODEL // (3 * 256)) * 256
IN_SIZES = (GLA_HEADS * GLA_DK, GLA_HEADS * GLA_DK, GLA_HEADS * GLA_DV, GLA_GATE_RANK,
            GLA_HEADS * GLA_DV, Q_LORA, KV_LORA, MLA_ROPE)
IN_WIDTH = sum(IN_SIZES)

kernel_name = 'hymba_gla_mla_decode_step'

def _rmsnorm(x, w):
    xf = x.astype(jnp.float32)
    y = xf * lax.rsqrt(jnp.mean(xf * xf, axis=-1, keepdims=True) + EPS)
    return (y * w.astype(jnp.float32)).astype(x.dtype)

def _rope(x, pos):
    half = MLA_ROPE // 2
    inv = ROPE_THETA ** (-jnp.arange(half, dtype=jnp.float32) / half)
    ang = pos.astype(jnp.float32)[:, None] * inv[None, :]
    cos, sin = jnp.cos(ang), jnp.sin(ang)
    xf = x.astype(jnp.float32)
    x1, x2 = xf[..., :half], xf[..., half:]
    return jnp.concatenate([x1 * cos - x2 * sin, x1 * sin + x2 * cos], axis=-1).astype(x.dtype)

def _project(n, pos, w_in, w_gk, b_gk, q_norm, kv_norm, w_uq, w_ukv):
    Bn, T, _ = n.shape
    idx = np.cumsum(IN_SIZES)[:-1].tolist()
    q, k, v, gr, g, cq, ckv, kpe = jnp.split(n @ w_in, idx, axis=-1)
    heads = lambda a, d: a.reshape(Bn, T, GLA_HEADS, d).transpose(0, 2, 1, 3)
    gq = heads(q, GLA_DK) * (GLA_DK ** -0.5)
    gk = heads(k, GLA_DK)
    gv = heads(v, GLA_DV)
    lg = heads(jax.nn.log_sigmoid((gr @ w_gk + b_gk).astype(jnp.float32)) / GLA_GATE_NORM, GLA_DK)
    qh = (_rmsnorm(cq, q_norm) @ w_uq).reshape(Bn, T, MLA_HEADS, MLA_NOPE + MLA_ROPE)
    w_uk = w_ukv.reshape(KV_LORA, MLA_HEADS, MLA_NOPE + MLA_V)[..., :MLA_NOPE]
    q_lat = jnp.einsum('bthn,rhn->bhtr', qh[..., :MLA_NOPE], w_uk)
    q_pe = _rope(qh[..., MLA_NOPE:].transpose(0, 2, 1, 3), pos)
    ckv = _rmsnorm(ckv, kv_norm)
    kpe = _rope(kpe, pos)
    return (gq, gk, gv, lg, g), (q_lat, q_pe, ckv, kpe)

def _gla_chunk(S, q, k, v, lg):
    q, k, v, lg = (a.astype(jnp.float32) for a in (q, k, v, lg))
    S = S.astype(jnp.float32)
    C = q.shape[2]
    b = jnp.cumsum(lg, axis=2)
    causal = jnp.tril(jnp.ones((C, C), bool))
    diff = b[:, :, :, None, :] - b[:, :, None, :, :]
    decay = jnp.exp(jnp.where(causal[None, None, :, :, None], diff, -jnp.inf))
    A = jnp.einsum('bhtd,bhsd,bhtsd->bhts', q, k, decay)
    o = A @ v + jnp.einsum('bhtd,bhde->bhte', q * jnp.exp(b), S)
    b_last = b[:, :, -1:, :]
    S_new = jnp.exp(b_last[:, :, 0, :])[..., None] * S + jnp.einsum('bhsd,bhse->bhde', k * jnp.exp(b_last - b), v)
    return S_new, o

def _gla_prompt(q, k, v, lg):
    Bn, H, L, _ = q.shape
    S0 = jnp.zeros((Bn, H, GLA_DK, GLA_DV), jnp.float32)
    S, o_meta = _gla_chunk(S0, q[:, :, :N_META], k[:, :, :N_META], v[:, :, :N_META], lg[:, :, :N_META])
    n_chunks = (L - N_META) // GLA_CHUNK

    def chunks(a):
        return jnp.moveaxis(a[:, :, N_META:].reshape(Bn, H, n_chunks, GLA_CHUNK, a.shape[-1]), 2, 0)

    S, o = lax.scan(lambda s, xs: _gla_chunk(s, *xs), S, tuple(chunks(a) for a in (q, k, v, lg)))
    o = jnp.moveaxis(o, 0, 2).reshape(Bn, H, L - N_META, GLA_DV)
    return jnp.concatenate([o_meta, o], axis=2), S

def _latent_scores(q_lat, q_pe, ck, kp):
    s = jnp.einsum('bhtr,bkr->bhtk', q_lat, ck) + jnp.einsum('bhtp,bkp->bhtk', q_pe, kp)
    return s.astype(jnp.float32) * MLA_SCALE

def _mla_prompt(q_lat, q_pe, ckv, kpe):
    Bn, H, L, R = q_lat.shape
    n_blk = -(-L // Q_BLOCK)
    Lp = n_blk * Q_BLOCK
    padt = lambda a, ax: jnp.pad(a, [(0, Lp - L) if i == ax else (0, 0) for i in range(a.ndim)])
    q_lat, q_pe = padt(q_lat, 2), padt(q_pe, 2)
    ckv, kpe = padt(ckv, 1), padt(kpe, 1)
    key_pos = jnp.arange(Lp)

    def block(i):
        s = i * Q_BLOCK
        ql = lax.dynamic_slice_in_dim(q_lat, s, Q_BLOCK, axis=2)
        qp = lax.dynamic_slice_in_dim(q_pe, s, Q_BLOCK, axis=2)
        qpos = s + jnp.arange(Q_BLOCK)
        sc = jnp.where(key_pos[None, :] <= qpos[:, None], _latent_scores(ql, qp, ckv, kpe), -jnp.inf)
        p = jax.nn.softmax(sc, axis=-1)
        return jnp.einsum('bhtk,bkr->bhtr', p, ckv.astype(jnp.float32))

    o = lax.map(block, jnp.arange(n_blk))
    return jnp.moveaxis(o, 0, 2).reshape(Bn, H, Lp, R)[:, :, :L]

def _online_update(carry, sc, ck):
    m, l, acc = carry
    m_new = jnp.maximum(m, sc.max(-1))
    corr = jnp.exp(m - m_new)
    p = jnp.exp(sc - m_new[..., None])
    acc = acc * corr[..., None] + jnp.einsum('bhtk,bkr->bhtr', p, ck.astype(jnp.float32))
    return (m_new, l * corr + p.sum(-1), acc)

def _mla_sample(q_lat, q_pe, ck_new, kp_new, cache_ckv, cache_kpe, page_table, layer):
    Bd, H, T, R = q_lat.shape

    def page_step(carry, pages):
        ck = cache_ckv[layer, pages]
        kp = cache_kpe[layer, pages]
        return _online_update(carry, _latent_scores(q_lat, q_pe, ck, kp), ck), None

    init = (jnp.full((Bd, H, T), -jnp.inf, jnp.float32), jnp.zeros((Bd, H, T), jnp.float32),
            jnp.zeros((Bd, H, T, R), jnp.float32))
    carry, _ = lax.scan(page_step, init, page_table.T)
    causal = jnp.tril(jnp.ones((T, T), bool))
    sc = jnp.where(causal, _latent_scores(q_lat, q_pe, ck_new, kp_new), -jnp.inf)
    m, l, acc = _online_update(carry, sc, ck_new)
    return acc / l[..., None]

def _merge(o_gla, g, o_lat, gla_norm, w_ukv, w_out, dtype):
    Bn, _, T, _ = o_gla.shape
    og = _rmsnorm(o_gla, gla_norm).transpose(0, 2, 1, 3).reshape(Bn, T, GLA_HEADS * GLA_DV)
    og = og * jax.nn.silu(g.astype(jnp.float32))
    w_uv = w_ukv.reshape(KV_LORA, MLA_HEADS, MLA_NOPE + MLA_V)[..., MLA_NOPE:]
    om = jnp.einsum('bhtr,rhv->bthv', o_lat, w_uv).reshape(Bn, T, MLA_HEADS * MLA_V)
    return (jnp.concatenate([og, om.astype(jnp.float32)], axis=-1) @ w_out).astype(dtype)

def _ffn_block(h, mix, norm_ffn, w_gate, w_up, w_down):
    h = h + mix
    n = _rmsnorm(h, norm_ffn)
    return h + (jax.nn.silu(n @ w_gate) * (n @ w_up)) @ w_down

def setup_inputs(seed: int = 0) -> dict:
    key = jax.random.key(seed)
    ks = jax.random.split(key, 24)
    f32 = jnp.float32
    nrm = lambda k, shape, s=1.0: jax.random.normal(k, shape, f32) * s
    n_pages = PAST_LEN // PAGE_SIZE
    n_used = DEC_BATCH * n_pages
    n_phys = (5 * n_used + 3) // 4
    page_table = jax.random.permutation(ks[0], n_phys)[:n_used].reshape(DEC_BATCH, n_pages).astype(jnp.int32)
    return {
        'x_prompt': nrm(ks[1], (BATCH, SEQ, D_MODEL)),
        'x_sample': nrm(ks[2], (DEC_BATCH, DEC_SEQ, D_MODEL)),
        'cache_ckv': nrm(ks[3], (DEPTH, n_phys, PAGE_SIZE, KV_LORA)),
        'cache_kpe': nrm(ks[4], (DEPTH, n_phys, PAGE_SIZE, MLA_ROPE)),
        'state_gla': nrm(ks[5], (DEPTH, DEC_BATCH, GLA_HEADS, GLA_DK, GLA_DV), 0.3),
        'page_table': page_table,
        'meta_tokens': nrm(ks[6], (N_META, D_MODEL)),
        'norm_mix': 1.0 + nrm(ks[7], (DEPTH, D_MODEL), 0.05),
        'w_in': nrm(ks[8], (DEPTH, D_MODEL, IN_WIDTH), D_MODEL ** -0.5),
        'w_gk': nrm(ks[9], (DEPTH, GLA_GATE_RANK, GLA_HEADS * GLA_DK), GLA_GATE_RANK ** -0.5),
        'b_gk': nrm(ks[10], (DEPTH, GLA_HEADS * GLA_DK), 0.1),
        'gla_norm': 1.0 + nrm(ks[11], (DEPTH, GLA_DV), 0.05),
        'q_norm': 1.0 + nrm(ks[12], (DEPTH, Q_LORA), 0.05),
        'kv_norm': 1.0 + nrm(ks[13], (DEPTH, KV_LORA), 0.05),
        'w_uq': nrm(ks[14], (DEPTH, Q_LORA, MLA_HEADS * (MLA_NOPE + MLA_ROPE)), Q_LORA ** -0.5),
        'w_ukv': nrm(ks[15], (DEPTH, KV_LORA, MLA_HEADS * (MLA_NOPE + MLA_V)), KV_LORA ** -0.5),
        'w_out': nrm(ks[16], (DEPTH, D_MIX, D_MODEL), D_MIX ** -0.5),
        'norm_ffn': 1.0 + nrm(ks[17], (DEPTH, D_MODEL), 0.05),
        'w_gate': nrm(ks[18], (DEPTH, D_MODEL, D_FF), D_MODEL ** -0.5),
        'w_up': nrm(ks[19], (DEPTH, D_MODEL, D_FF), D_MODEL ** -0.5),
        'w_down': nrm(ks[20], (DEPTH, D_FF, D_MODEL), D_FF ** -0.5),
        'norm_final': 1.0 + nrm(ks[21], (D_MODEL,), 0.05),
    }

def reference(x_prompt, x_sample, cache_ckv, cache_kpe, state_gla, page_table, meta_tokens,
              norm_mix, w_in, w_gk, b_gk, gla_norm, q_norm, kv_norm, w_uq, w_ukv, w_out,
              norm_ffn, w_gate, w_up, w_down, norm_final):
    Bp = x_prompt.shape[0]
    T = x_sample.shape[1]
    past = page_table.shape[1] * PAGE_SIZE
    meta = jnp.broadcast_to(meta_tokens.astype(x_prompt.dtype)[None], (Bp, N_META, D_MODEL))
    hp = jnp.concatenate([meta, x_prompt], axis=1)
    pos_p = jnp.arange(hp.shape[1])
    pos_s = past + jnp.arange(T)
    hs = x_sample
    ckv_p, kpe_p, st_p, ckv_s, kpe_s, st_s = [], [], [], [], [], []
    for layer in range(DEPTH):
        proj_w = (w_in[layer], w_gk[layer], b_gk[layer], q_norm[layer], kv_norm[layer], w_uq[layer], w_ukv[layer])
        n = _rmsnorm(hp, norm_mix[layer])
        (gq, gk, gv, lg, g), (ql, qp, ck, kp) = _project(n, pos_p, *proj_w)
        o_gla, S = _gla_prompt(gq, gk, gv, lg)
        o_lat = _mla_prompt(ql, qp, ck, kp)
        mix = _merge(o_gla, g, o_lat, gla_norm[layer], w_ukv[layer], w_out[layer], hp.dtype)
        hp = _ffn_block(hp, mix, norm_ffn[layer], w_gate[layer], w_up[layer], w_down[layer])
        ckv_p.append(ck)
        kpe_p.append(kp)
        st_p.append(S.astype(state_gla.dtype))
        n = _rmsnorm(hs, norm_mix[layer])
        (gq, gk, gv, lg, g), (ql, qp, ck, kp) = _project(n, pos_s, *proj_w)
        S, o_gla = _gla_chunk(state_gla[layer], gq, gk, gv, lg)
        o_lat = _mla_sample(ql, qp, ck, kp, cache_ckv, cache_kpe, page_table, layer)
        mix = _merge(o_gla, g, o_lat, gla_norm[layer], w_ukv[layer], w_out[layer], hs.dtype)
        hs = _ffn_block(hs, mix, norm_ffn[layer], w_gate[layer], w_up[layer], w_down[layer])
        ckv_s.append(ck)
        kpe_s.append(kp)
        st_s.append(S.astype(state_gla.dtype))
    y_prompt = _rmsnorm(hp[:, N_META:], norm_final)
    y_sample = _rmsnorm(hs, norm_final)
    return (y_prompt, y_sample, jnp.stack(ckv_p), jnp.stack(kpe_p), jnp.stack(st_p),
            jnp.stack(ckv_s), jnp.stack(kpe_s), jnp.stack(st_s))


_drawn_inputs = setup_inputs


def setup_inputs(seed=0):
    import zlib

    import numpy as np

    out = dict(_drawn_inputs(seed))
    spreads = {}
    factors = {'cache_ckv': 2.952, 'cache_kpe': 5.653, 'q_norm': 8.0, 'gla_norm': 2.761}
    for name, (base, spread) in spreads.items():
        noise = np.random.default_rng([zlib.crc32(name.encode()), seed]).standard_normal(out[name].shape)
        drawn = base * np.exp(spread * noise) if base else spread * noise
        out[name] = __import__('jax').numpy.asarray(drawn.astype(out[name].dtype))
    for name, factor in factors.items():
        out[name] = (out[name] * factor).astype(out[name].dtype)
    return out
```

```python
from contextlib import ExitStack

import numpy as np

import concourse.bass as bass
from concourse import mybir

F32 = mybir.dt.float32
F32R = mybir.dt.float32r
I32 = mybir.dt.int32
U32 = mybir.dt.uint32
ALU = mybir.AluOpType
ACT = mybir.ActivationFunctionType
AX = mybir.AxisListType.X

P = 128
EPS = 1e-6
D = 1024
KD = D // P
NMETA = 16
SEQ = 512
NP = NMETA + SEQ
NB = 8
T = NP + NB
TH = T // 2
NT = 5
TPAD = NT * P
TT = [P, P, P, P, T - 4 * P]
PAST = 4096
PAGE = 128
NPAGES = PAST // PAGE
GH, DK, DV = 4, 64, 128
RANK = 16
MH, NOPE, ROPE = 4, 128, 64
HALF = ROPE // 2
QL, KVL = 384, 256
SCALE = float(NOPE + ROPE) ** -0.5
DFF = 2816
KF = DFF // P
C_Q, C_K, C_V, C_GR, C_G, C_CQ, C_CKV, C_KPE = 0, 256, 512, 1024, 1040, 1552, 1936, 2192
LEVELS = [64, 32, 16, 8, 4, 2, 1]
NL = len(LEVELS)
NG = P // 32
UNITS = 16
CHUNKS = NPAGES * PAGE // (P * UNITS)
NBLK = (KVL + ROPE) // 32

CC = {}
_at = 0
for _name, _n in (("ident", P), ("ones", P), ("ucum", P), ("swap", P), ("cosf", T), ("sinf", T), ("cosk", NT * ROPE),
                  ("sink", NT * ROPE), ("ucum4", 24), ("sell", 4), ("selo", 4), ("eps", 1), ("quart", 1), ("cap", P)):
    CC[_name] = (_at, _at + _n)
    _at += _n
NCONST = _at


def constants():
    c = np.zeros((P, NCONST), np.float32)

    def put(name, a):
        c[:, CC[name][0]:CC[name][1]] = a

    p = np.arange(P)
    put("ident", np.eye(P))
    put("ones", 1.0)
    put("ucum", (p[:, None] <= p[None, :]) / 16.0)
    last = np.zeros((P, 24))
    last[:16, :16] = np.triu(np.ones((16, 16))) / 16.0
    last[16:24, 16:] = np.eye(8) / 16.0
    put("ucum4", last)
    put("swap", np.eye(P)[p ^ HALF])
    pos = np.concatenate([np.arange(NP), np.full(TPAD - NP, PAST)]).astype(np.float32)
    inv = (10000.0 ** (-np.arange(HALF) / HALF)).astype(np.float32)
    ang = (pos[:, None] * inv[None, :]).astype(np.float32)
    cos, sin = np.cos(ang), np.sin(ang)
    cos2, sin2 = np.concatenate([cos, cos], 1), np.concatenate([-sin, sin], 1)
    put("cosf", np.concatenate([cos2, cos2], 1)[:T].T)
    put("sinf", np.concatenate([sin2, sin2], 1)[:T].T)
    put("cosk", cos2.reshape(NT, P, ROPE).transpose(1, 0, 2).reshape(P, -1))
    put("sink", sin2.reshape(NT, P, ROPE).transpose(1, 0, 2).reshape(P, -1))
    h = np.arange(4)
    put("sell", ((p[:, None] % 32 < 16) & (p[:, None] % 4 == h)).astype(np.float32))
    put("selo", (p[:, None] % 32 == h).astype(np.float32))
    put("eps", EPS)
    put("quart", ((p % 4) * 2)[:, None])
    put("cap", np.where(p[None, :] <= p[:, None], 3e38, -3e38))
    masks = np.zeros((P, NL + 1, P), np.int32)
    for i, s in enumerate(LEVELS):
        same = p[:, None] // (2 * s) == p[None, :] // (2 * s)
        masks[:, i] = same & (p[:, None] % (2 * s) < s) & (p[None, :] % (2 * s) >= s)
    masks[:, NL] = np.eye(P)
    pick = np.zeros((24, NB, P), np.float32)
    for b in range(NB):
        pick[16 + b, b] = 1.0
    return c, masks.reshape(P, -1), pick.reshape(24, -1)


def plan():
    n = [f"xT{k}" for k in range(KD)]
    n += [f"cq{m}" for m in range(3)]
    n += [f"tok{i}" for i in range(NT)] + ["ssq"]
    n += [f"q{m}" for m in range(2)] + [f"k{m}" for m in range(2)]
    n += [f"v{i}" for i in range(NT)]
    n += [f"g{m}" for m in range(4)]
    n += [f"ck{j}" for j in range(3)] + ["gr"]
    for hh in range(2):
        n += [f"qn{2 * hh}", f"qn{2 * hh + 1}", f"qp{hh}"]
    n += ["sw0", "sw1"]
    n += [f"kn{h}" for h in range(4)] + [f"vm{i}" for i in range(NT)] + ["wuk0", "wuk1", "qlat", "snew"]
    for u in range(NT * MH + 2):
        n += [f"S{u}"] if u < NT * MH else []
        n += [f"PT{u - 1}"] if 1 <= u <= NT * MH else []
        n += [f"OM{u - 2}"] if u >= 2 else []
    while len(n) % 4:
        n.append(f"-{len(n)}")
    n += [f"cache{i}" for i in range(4 * NB)]
    n += ["wb", "omd"]
    n += [f"lg{i}" for i in range(NT)] + [f"b{c}" for c in range(NT)]
    for lv in range(NL + 1):
        for c in range(NT):
            if c < 4 or lv == NL or LEVELS[lv] <= 8:
                n += [f"G{lv}.{c}"]
    for c in range(NT):
        n += [f"kt{c}", f"o{c}", f"s{c}"]
    n += [f"vb{b}" for b in range(NB)] + ["os"]
    n += [f"ssg{h}" for h in range(4)]
    n += [f"hT{k}" for k in range(KD)]
    n += [f"wo{m}" for m in range(KD)] + ["ssf"]
    while len(n) % 4:
        n.append(f"-{len(n)}")
    n += [f"ffn{i}" for i in range(2 * KF)]
    n += [f"dn{i}" for i in range(KD)]
    n += ["ssy"] + [f"y{i}" for i in range(NT)]
    return {name: i for i, name in enumerate(n)}


PLAN = plan()
IDLE = {v for k, v in PLAN.items() if k[0] == "-"}

BLOCKS = [[("w_in", 0, KD, C_CQ, 256)], [("w_in", 0, KD, C_CQ + 256, 128)], [("w_in", 0, KD, C_CKV, 256)],
          [("w_in", 0, KD, C_KPE, 64), ("w_in", 0, KD, C_GR, 16)],
          [("w_in", 0, KD, C_Q, 256)], [("w_in", 0, KD, C_K, 256)],
          [("w_in", 0, KD, C_V, 256)], [("w_in", 0, KD, C_V + 256, 256)],
          [("w_in", 0, KD, C_G, 256)], [("w_in", 0, KD, C_G + 256, 256)],
          *[[("w_uq", 0, 3, 384 * x + c, w) for c, w in ((0, 128), (192, 128), (128, 64), (320, 64))] for x in range(2)],
          [("w_ukv", 0, 2, 0, 1024)]]
B_UQ, B_UKV, B_OUT = 10, 12, 13
BLOCKS += [[("w_out", 0, KD, 256 * m, 256)] for m in range(4)]
B_FFN = len(BLOCKS)
B_DOWN = B_FFN + 2 * (DFF // 256)
DPARTS = [(0, 8), (8, 8), (16, 6)]


SIGNALS = ["E_done", "Qall_done", "ckhi_done", "cklo_done", "diff_done", "dn_part", "eb_done", "fe_done", "ge_done",
           "hhi_done", "hlo_done", "kt_done", "lgt_done", "m_done", "mb_done", "mixhi_done", "mixlo_done", "mm_done",
           "mr_done", "msk_loaded", "mt_done", "nhi_done", "nlo_done", "nm_done", "nmax_done", "oc_done", "og_done",
           "olat_done", "omdhi_done", "omhi_done", "ot_done", "pad_done", "pick_loaded", "pn_done", "prod_done",
           "ps_done", "pt_done", "pti_loaded", "pv_done", "qc_done", "qk_done", "qn_done", "qnhi_done", "qnlo_done",
           "qpe_done", "rk_done", "rs_done", "sc_done", "sqf_done", "sqg_done", "sqs_done", "sqy_done", "stat_clear",
           "states_loaded", "tf_done", "wdiff_done", "wexp_done", "wrow_done", "wuv_kept", "x2_loaded", "xhi_done",
           "xn_done", "yT_done", "y_half", "y_out0", "y_out1", "kc_loaded0", "kc_loaded1"]
LAST = {0: "cq1", 1: "cq2", 2: "tok4", 3: "tok4", 4: "q1", 5: "k1", 6: "v4", 7: "v4", 8: "g1", 9: "g3", 10: "qp0",
        11: "qp1", 12: "vm4", 13: "wo1", 14: "wo3", 15: "wo5", 16: "wo7", 17: "ffn1", 18: "ffn3"}

def reads(n):
    return sum(m not in IDLE for m in range(n % 4, n, 4))


def last_g(c):
    return f"G{NL}.{c}"


def last_of_level(lv):
    return f"G{lv}.{4 if lv == NL or LEVELS[lv] <= 8 else 3}"


def fills(name):
    return sum(v <= PLAN[name] and k[0] != "-" and not k.startswith("cache") for k, v in PLAN.items())


LOADS = []
for _n in range(B_DOWN + 12):
    _k = len(BLOCKS[_n]) if _n < B_FFN else 1
    LOADS.append(_k + (LOADS[_n - 2] if _n >= 2 else 0))


def hybrid_decode_kernel(nc, ins, outs):
    (x_prompt, x_sample, cache_ckv, cache_kpe, state_gla, page_table, meta_tokens, norm_mix, w_in, w_gk, b_gk,
     gla_norm, q_norm, kv_norm, w_uq, w_ukv, w_out, norm_ffn, w_gate, w_up, w_down, norm_final,
     c_all, c_masks, c_pick) = ins
    y_prompt, y_sample, ckv_p, kpe_p, gla_p, ckv_s, kpe_s, gla_s = outs
    weights = {"w_in": w_in[0], "w_uq": w_uq[0], "w_ukv": w_ukv[0], "w_out": w_out[0], "w_gate": w_gate[0],
               "w_up": w_up[0], "w_down": w_down[0]}
    with ExitStack() as ctx:
        top = [0]
        arena_bytes = 212000
        nc_base = nc.sbuf_base
        ctx.enter_context(nc.sbuf_tensor("arena", [P, arena_bytes // 4], F32))
        arena_at = -(-nc_base // 32) * 32

        def sb(name, shape, dt=F32, at=None):
            n = 4
            for d in shape[1:]:
                n *= d
            off = top[0] if at is None else at
            if at is None:
                top[0] = -(-(off + n) // 32) * 32
            assert off + n <= arena_bytes, (name, off, n)
            return nc.alloc_sbuf_tensor_at(name, shape, dt, offset=arena_at + off)

        xhi = sb("xhi", [P, KD, TPAD], F32R)
        xlo = sb("xlo", [P, KD, TPAD], F32R)
        wraw = [sb(f"wraw{i}", [P, 2048]) for i in range(2)]
        whi = [sb(f"whi{i}", [P, 2048], F32R) for i in range(2)]
        wlo = [sb(f"wlo{i}", [P, 2048], F32R) for i in range(2)]
        cst_at = top[0]
        cst = sb("cst", [P, NCONST])
        nrm = sb("nrm", [P, 3 * KD + 4])
        keep = top[0]
        hT = sb("hT", [P, KD, T])
        gq = sb("gq", [P, 2, T], at=keep)
        gk = sb("gk", [P, 2, T], at=keep + 8 * T)
        gT = sb("gT", [P, 4, T], at=keep + 16 * T)
        hid_at = top[0]
        stat = sb("stat", [P, 64])
        vtok = sb("vtok", [P, NT, 512])
        grT = sb("grT", [32, T])
        Qall = sb("Qall", [P, NB, NBLK * 32])
        wuv = sb("wuv", [P, 2, 4, 128])
        cks = sb("cks", [P, 2, NB])
        qlT = sb("qlT", [P, 2, 4, NB])
        olT = sb("olT", [P, 2 * CHUNKS * NB, 4])
        rows = sb("rows", [1, 640])
        el = sb("el", [P, 2, NT])
        eb = sb("eb", [P, 2, NB])
        wgk = sb("wgk", [32, 256])
        W0 = top[0]
        X = sb("X", [P, NT, D], at=W0)
        cq = sb("cq", [P, 3, T], at=W0)
        knT = sb("knT", [P, 4, T], at=W0)
        a = W0 + 16 * T
        qnhi = sb("qnhi", [P, 3, T], F32R, at=a)
        qnlo = sb("qnlo", [P, 3, T], F32R, at=a + 12 * T)
        vm = sb("vm", [P, NT, 512], at=a)
        a += 24 * T
        ctok = sb("ctok", [P, NT, 384], at=a)
        a += NT * 384 * 4
        kpT = sb("kpT", [P, T], at=a)
        a += 4 * T
        ckhi = sb("ckhi", [P, 2, TPAD], F32R, at=a)
        cklo = sb("cklo", [P, 2, TPAD], F32R, at=a + 8 * TPAD)
        pr = [sb(f"pr{i}", [P, NP], at=a + 4 * NP * i) for i in range(2)]
        pt = [sb(f"pt{i}", [P, NT, P], at=a + 8 * NP + 4 * NT * P * i) for i in range(2)]
        a += 16 * TPAD
        qnT = sb("qnT", [P, 4, T], at=a)
        a += 16 * T
        qpe = sb("qpe", [P, 2, T], at=a)
        a += 8 * T
        sqs = sb("sqs", [P, 3, T], at=a - 24 * T)
        rsb = sb("rsb", [P, T], at=a)
        kvn = sb("kvn", [P, KVL], at=a + 4 * T)
        a += 4 * T + 4 * KVL
        rp = sb("rp", [P, 2, ROPE], at=a)
        grt = sb("grt", [P, NT, RANK], at=a + 8 * ROPE)
        prod = sb("prod", [P, 3, 4, NB], at=a + 832)
        scr = sb("scr", [P, D], at=a + 1216)
        wukT = sb("wukT", [P, 4, 256], at=a + 1216)
        KC = [sb(f"KC{i}", [P, UNITS * KVL], at=W0 + 4 * UNITS * KVL * i) for i in range(2)]
        b0 = W0 + 8 * UNITS * KVL
        KP = [sb(f"KP{i}", [P, UNITS * ROPE], at=b0 + 4 * UNITS * ROPE * i) for i in range(2)]
        b0 += 8 * UNITS * ROPE
        KT = sb("KT", [P, UNITS, 8, 32], at=b0)
        b0 += 4 * UNITS * KVL
        KTp = sb("KTp", [P, UNITS, 2, 32], at=b0)
        idx = sb("idx", [P, NB, CHUNKS], I32, at=b0 + 4 * UNITS * ROPE)
        b1 = b0 + 4 * UNITS * ROPE + 64
        pti = sb("pti", [P, NB], I32, at=b1)
        icur = [sb(f"icur{i}", [P, 1], I32, at=b1 + 32 + 32 * i) for i in range(2)]
        b1 += 96
        Qc = sb("Qc", [P, NBLK * 32], at=b1)
        mc = sb("mc", [P, 4], at=b1 + 1280)
        b1 = cst_at + 4 * CC["cosf"][0]
        assert 4096 <= 8 * T
        Pc = sb("Pc", [P, P], at=b1)
        Pt = sb("Pt", [P, 4, 32], at=b1 + 512)
        PS = sb("PS", [P, UNITS, 32], at=b1 + 1024)
        Oc = sb("Oc", [P, KVL], at=b1 + 3072)
        wbc = sb("wbc", [P, 3 * 32], at=W0)
        olat = sb("olat", [P, 2, NB * 4], at=W0 + 512)
        otmp = sb("otmp", [P, NB * 4], at=W0 + 1024)
        a = W0
        lgs = sb("lgs", [P, NT, 256], at=a)
        a += NT * 256 * 4
        bT = sb("bT", [P, 2, T], at=a)
        a += 8 * T
        Ee = sb("Ee", [P, 2, NP], at=a)
        a += 8 * NP
        qt = sb("qt", [P, 2, NP], at=a)
        a += 8 * NP
        kt = sb("kt", [P, 2, NP], at=a)
        a += 8 * NP
        AT = sb("AT", [P, NT, 4, P], at=a)
        a += NT * 4 * P * 4
        msk = sb("msk", [P, NL + 1, P], I32, at=a)
        pick = sb("pick", [24, NB, P], at=a)
        a += 4 * P * (NL + 1)
        Sst = sb("Sst", [P, 2, P], at=a)
        a += 8 * P
        states = sb("states", [P, NB, 2, P], at=a)
        a += 8 * NB * P
        oT = sb("oT", [P, 4, T], at=a)
        a += 16 * T
        ktok = sb("ktok", [P, 2, P], at=a)
        a += 8 * P
        lgt = sb("lgt", [P, 256], at=a)
        a += 1024
        assert a <= arena_bytes, a
        sqg = [sb(f"sqg{i}", [P, T], at=W0 + 4 * T * i) for i in range(2)]
        rsg = [sb(f"rsg{i}", [P, T], at=W0 + 8 * T + 4 * T * i) for i in range(2)]
        X2 = sb("X2", [P, NT, D], at=W0)
        sqf = sb("sqf", [P, KD, T], at=W0 + 20480)
        rsf = sb("rsf", [P, T], at=W0)
        tf = [sb(f"tf{i}", [P, T], at=W0 + 4 * T * (1 + i)) for i in range(2)]
        hhi = sb("hhi", [P, KF, T], F32R, at=hid_at)
        hlo = sb("hlo", [P, KF, T], F32R, at=hid_at + 4 * KF * T)
        f0 = cst_at + 4 * CC["cosf"][0]
        fe = [sb(f"fe{i}", [P, T], at=f0 + 4 * T * i) for i in range(2)]
        sqy = sb("sqy", [P, KD, T], at=0)
        yT = sb("yT", [P, KD, T], at=4 * KD * TPAD)
        rsy = sb("rsy", [P, T], at=hid_at)
        ysb = [sb(f"ysb{i}", [P, D], at=hid_at + 4 * T + 4 * D * i) for i in range(2)]

        pairs = [ctx.enter_context(nc.psum_tensor(f"pair{i}", [P, 1024], F32)) for i in range(4)]

        def sem(name):
            return ctx.enter_context(nc.semaphore(name))

        pe_done = sem("pe_done")
        pair_free = [sem(f"pair_free{i}") for i in range(4)]
        w_loaded = [sem(f"w_loaded{i}") for i in range(2)]
        w_hi, w_lo = sem("w_hi"), sem("w_lo")
        x_loaded = [sem(f"x_loaded{i}") for i in range(NT)]
        c_loaded, n_loaded, small_loaded = sem("c_loaded"), sem("n_loaded"), sem("small_loaded")
        out_done = sem("out_done")
        dve_chain, act_chain, pool_chain = sem("dve_chain"), sem("act_chain"), sem("pool_chain")
        signals = {name: sem(name) for name in SIGNALS}

        def S(name):
            return signals[name]

        block = ctx.enter_context(nc.Block())

        def C(name, rows=P):
            return cst[0:rows, CC[name][0]:CC[name][1]]

        ident, ones = C("ident"), C("ones")

        def halves(ap):
            return ap[:, :].rearrange("p (a t) -> p a t", a=2)[:, :, 0:TH]

        def split2(ap):
            return ap.rearrange("p (a t) -> p a t", a=2)

        def block_size(n):
            return BLOCKS[n][0][2] * sum(p[4] for p in BLOCKS[n]) if n < B_FFN else 256 * KD

        def view(bufs, n, k=None):
            k = k or BLOCKS[n][0][2]
            w = sum(p[4] for p in BLOCKS[n]) if n < B_FFN else 256
            return bufs[n % 2][:, 0:k * w].rearrange("p (k n) -> p k n", n=w)

        @block.sync
        def _(sp):
            sp.dma_start(cst[:, :], c_all).then_inc(c_loaded, 16)

            def load_x(dst, sems):
                for i in range(NT):
                    if i == 0:
                        sp.dma_start(dst[0:NMETA, 0, :], meta_tokens).then_inc(sems[0], 16)
                        sp.dma_start(dst[NMETA:P, 0, :], x_prompt[0, 0:P - NMETA, :]).then_inc(sems[0], 16)
                    elif i < 4:
                        sp.dma_start(dst[:, i, :], x_prompt[0, P * i - NMETA:P * (i + 1) - NMETA, :]).then_inc(sems[i], 16)
                    else:
                        sp.dma_start(dst[0:NMETA, 4, :], x_prompt[0, SEQ - NMETA:SEQ, :]).then_inc(sems[4], 16)
                        sp.dma_start(dst[NMETA:NMETA + NB, 4, :], x_sample[:, 0, :]).then_inc(sems[4], 16)

            load_x(X, x_loaded)

            def load_block(n):
                if n >= 2:
                    sp.wait_ge(w_lo, n - 1)
                if n == B_UKV + 2:
                    sp.wait_ge(pe_done, fills("wuk1"))
                    sp.wait_ge(S("wuv_kept"), 1)
                c0 = 0
                w = sum(p[4] for p in BLOCKS[n])
                k = BLOCKS[n][0][2]
                for name, k0, kk, col, cols in BLOCKS[n]:
                    dst = wraw[n % 2][:, 0:k * w].rearrange("p (k n) -> p k n", n=w)[:, :, c0:c0 + cols]
                    src = weights[name][P * k0:P * (k0 + kk), col:col + cols].rearrange("(k p) n -> p k n", p=P)
                    sp.dma_start(dst, src).then_inc(w_loaded[n % 2], 16)
                    c0 += cols

            for n in range(B_UKV):
                load_block(n)
                if n == 7:
                    for i in range(NT):
                        sp.wait_ge(pair_free[PLAN[f"tok{i}"] % 4], reads(PLAN[f"tok{i}"]) + 1)
                        r = min(TT[i], NP - P * i)
                        sp.dma_start(ckv_p[0, 0, P * i:P * i + r, :], ctok[0:r, i, 0:KVL]).then_inc(out_done, 16)
                        sp.dma_start(kpe_p[0, 0, P * i:P * i + r, :], ctok[0:r, i, KVL:KVL + ROPE]).then_inc(out_done, 16)
                        if i == NT - 1:
                            sp.dma_start(ckv_s[0, :, 0, :], ctok[r:r + NB, i, 0:KVL]).then_inc(out_done, 16)
                            sp.dma_start(kpe_s[0, :, 0, :], ctok[r:r + NB, i, KVL:KVL + ROPE]).then_inc(out_done, 16)
            load_block(B_UKV)
            load_block(B_OUT)
            load_block(B_OUT + 1)
            sp.wait_ge(pair_free[PLAN["omd"] % 4], reads(PLAN["omd"]) + 1)
            sp.wait_ge(out_done, 16 * 12)
            sp.dma_start(msk[:, :, :].rearrange("p a b -> p (a b)"), c_masks).then_inc(S("msk_loaded"), 16)
            for b in range(NB):
                for pp in range(2):
                    sp.dma_start(states[:, b, pp, :], state_gla[0, b, 2 * pp:2 * pp + 2].rearrange("a k v -> (a k) v")
                                 ).then_inc(S("states_loaded"), 16)
            sp.wait_ge(pair_free[PLAN[f"G{NL}.4"] % 4], reads(PLAN[f"G{NL}.4"]) + 1)
            sp.dma_start(pick[:, :, :].rearrange("p a b -> p (a b)"), c_pick).then_inc(S("pick_loaded"), 16)
            sp.wait_ge(pair_free[PLAN["s4"] % 4], reads(PLAN["s4"]) + 1)
            for pp in range(2):
                sp.dma_start(gla_p[0, 0, 2 * pp:2 * pp + 2].rearrange("a k v -> (a k) v"), Sst[:, pp, :]).then_inc(out_done, 16)
            sp.wait_ge(pair_free[PLAN["vb7"] % 4], reads(PLAN["vb7"]) + 1)
            for b in range(NB):
                for pp in range(2):
                    sp.dma_start(gla_s[0, b, 2 * pp:2 * pp + 2].rearrange("a k v -> (a k) v"), states[:, b, pp, :]
                                 ).then_inc(out_done, 16)
            sp.wait_ge(out_done, 16 * (12 + 2 + 16))
            sp.wait_ge(S("mixlo_done"), 4)
            load_x(X2, [S("x2_loaded")] * NT)
            load_block(B_OUT + 2)
            load_block(B_OUT + 3)
            with sp.Fori(0, DFF // 256) as j:
                for s, name in ((0, "w_gate"), (1, "w_up")):
                    slot = (B_FFN + s) % 2
                    sp.wait_ge(w_lo, (B_FFN + s - 1) + 2 * j)
                    src = weights[name].rearrange("(k p) n -> p k n", p=P)[:, :, bass.ds(256 * j, 256)]
                    sp.dma_start(wraw[slot][:, :].rearrange("p (k n) -> p k n", n=256), src).then_inc(w_loaded[slot], 16)
            with sp.Fori(0, 2) as j:
                for cb in range(2):
                    for q, (k0, kk) in enumerate(DPARTS):
                        n = B_DOWN + 3 * cb + q
                        sp.wait_ge(w_lo, (n - 1) + 6 * j)
                        src = weights["w_down"][P * k0:P * (k0 + kk), :].rearrange("(k p) n -> p k n", p=P)[:, :, bass.ds(512 * j + 256 * cb, 256)]
                        sp.dma_start(wraw[n % 2][:, 0:256 * kk].rearrange("p (k n) -> p k n", n=256), src).then_inc(w_loaded[n % 2], 16)
            for i in range(NT):
                sp.wait_ge(pair_free[PLAN[f"y{i}"] % 4], reads(PLAN[f"y{i}"]) + 1)
                y = ysb[i % 2]
                if i == 0:
                    sp.dma_start(y_prompt[0, 0:P - NMETA, :], y[NMETA:P, :]).then_inc(S(f"y_out{i % 2}"), 16)
                elif i < 4:
                    sp.dma_start(y_prompt[0, P * i - NMETA:P * (i + 1) - NMETA, :], y[:, :]).then_inc(S(f"y_out{i % 2}"), 16)
                else:
                    sp.dma_start(y_prompt[0, SEQ - NMETA:SEQ, :], y[0:NMETA, :]).then_inc(S(f"y_out{i % 2}"), 16)
                    sp.dma_start(y_sample[:, 0, :], y[NMETA:NMETA + NB, :]).then_inc(S(f"y_out{i % 2}"), 16)
            sp.wait_ge(S("y_out0"), 16 * 4)
            sp.wait_ge(S("y_out1"), 16 * 2)
            sp.wait_ge(out_done, 16 * (12 + 2 + 16))

        @block.gpsimd
        def _(pool):
            g = nc.gpsimd
            chain = [0]

            def link(ins):
                chain[0] += 1
                ins.then_inc(pool_chain, 1)
                pool.wait_ge(pool_chain, chain[0])

            with nc.allow_non_contiguous_dma("vectors by feature"):
                for j, v in enumerate((norm_mix[0], norm_ffn[0], norm_final)):
                    pool.dma_start(nrm[:, KD * j:KD * j + KD], v.rearrange("(k p) -> p k", p=P)).then_inc(n_loaded, 16)
                pool.dma_start(nrm[:, 3 * KD:3 * KD + 3], q_norm[0].rearrange("(k p) -> p k", p=P)).then_inc(n_loaded, 16)
                pool.dma_start(nrm[:, 3 * KD + 3:3 * KD + 4], gla_norm[0].rearrange("(k p) -> p k", p=P)).then_inc(n_loaded, 16)
                link(g.memset(wgk[:, :], 0.0))
                pool.dma_start(wgk[0:RANK, :], w_gk[0]).then_inc(small_loaded, 16)
                pool.dma_start(wgk[RANK:RANK + 1, :], b_gk).then_inc(small_loaded, 16)
                pool.dma_start(kvn[:, :], kv_norm[0].partition_broadcast(P)).then_inc(small_loaded, 16)
            g.memset(xhi[:, :, T:TPAD].bitcast(F32), 0.0).then_inc(S("pad_done"), 1)
            g.memset(xlo[:, :, T:TPAD].bitcast(F32), 0.0).then_inc(S("pad_done"), 1)
            g.memset(grT[:, :], 1.0).then_inc(S("pad_done"), 1)
            link(g.memset(Qall[:, :, :], 0.0))
            pool.wait_ge(w_loaded[B_UKV % 2], 16 * LOADS[B_UKV])
            ins = g.tensor_copy(wuv[:, :, :, :], wraw[B_UKV % 2][:, :].rearrange("p (k h n) -> p k h n", k=2, h=4)[:, :, :, NOPE:256])
            ins.then_inc(S("wuv_kept"), 1)
            pool.wait_ge(S("wuv_kept"), 1)
            pool.wait_ge(pair_free[PLAN["qlat"] % 4], reads(PLAN["qlat"]) + 1)
            pool.wait_ge(S("qpe_done"), 1)
            for q in range(NG):
                for gg in range(NG):
                    for dup in range(2):
                        at = 16 * dup + 4 * gg
                        for rh in range(2):
                            c = 4 * rh + q
                            dst = Qall[32 * gg:32 * gg + 32, :, 32 * c + at:32 * c + at + 4]
                            src = qlT[32 * q:32 * q + 32, rh, :, :].rearrange("p h b -> p b h")
                            link(g.tensor_copy(dst, src))
            for aa in range(2):
                for e in range(2):
                    for gg in range(NG):
                        for dup in range(2):
                            at = 32 * (8 + e) + 16 * dup + 4 * gg + aa
                            dst = Qall[32 * gg:32 * gg + 32, :, at:at + 3:2]
                            src = qpe[64 * aa + 32 * e:64 * aa + 32 * e + 32, :, NP:T].rearrange("p q b -> p b q")
                            ins = g.tensor_copy(dst, src)
                            if (aa, e, gg, dup) < (1, 1, NG - 1, 1):
                                link(ins)
            ins.then_inc(S("Qall_done"), 1)
            pool.wait_ge(S("Qall_done"), 1)
            pool.wait_ge(pair_free[PLAN["OM19"] % 4], reads(PLAN["OM19"]) + 1)
            pool.wait_ge(out_done, 16 * 12)
            with nc.allow_non_contiguous_dma("page table"):
                for q in range(4):
                    pool.dma_start(pti[q:P:4, :], page_table.rearrange("b n -> n b")).then_inc(S("pti_loaded"), 16)
            link(g.memset(PS[:, :, :], 0.0))
            pool.wait_ge(S("pti_loaded"), 64)
            link(g.tensor_scalar(idx[:, :, 0], pti[:, :], 8.0, C("quart"), ALU.mult, ALU.add))
            link(g.tensor_scalar(idx[:, :, 1], idx[:, :, 0], 1.0, 0.0, ALU.add, ALU.add))
            ckv_rows = cache_ckv[0].rearrange("n (s k) r -> (n s) (k r)", k=UNITS)
            kpe_rows = cache_kpe[0].rearrange("n (s k) r -> (n s) (k r)", k=UNITS)

            def gather(b, e):
                if b:
                    pool.wait_ge(S("pv_done"), 2 * b - 1 + e)
                    pool.wait_ge(S("kt_done"), 2 * b - 1 + e)
                link(g.tensor_copy(icur[e][:, :], idx[:, b, e:e + 1]))
                g.indirect_dma_start(KC[e][:, :], None, ckv_rows, bass.IndirectOffsetOnAxis(icur[e][:, 0:1], 0)).then_inc(S(f"kc_loaded{e}"), 16)
                g.indirect_dma_start(KP[e][:, :], None, kpe_rows, bass.IndirectOffsetOnAxis(icur[e][:, 0:1], 0)).then_inc(S(f"kc_loaded{e}"), 16)

            for b in range(NB):
                for e in range(CHUNKS):
                    gather(b, e)

        @block.tensor
        def _(pe):
            mm = nc.tensor.matmul

            def take(name):
                n = PLAN[name]
                if n >= 4:
                    pe.wait_ge(pair_free[n % 4], reads(n))
                return pairs[n % 4]

            def evacuated(name):
                pe.wait_ge(pair_free[PLAN[name] % 4], reads(PLAN[name]) + 1)

            def use(n):
                pe.wait_ge(w_lo, n + 1)

            def done(ins):
                ins.then_inc(pe_done, 1)

            def dense(ps, h, l, wcols, k_of, hi, lo, first=True, last=True):
                ins = None
                for half in range(2):
                    out = ps[:, 512 * half:512 * half + TH]
                    tok = slice(TH * half, TH * half + TH)
                    for j, kx in enumerate(k_of):
                        mm(out, wcols(h, j), hi[:, kx, tok], start=first and j == 0, stop=False)
                        mm(out, wcols(h, j), lo[:, kx, tok], start=False, stop=False)
                        ins = mm(out, wcols(l, j), hi[:, kx, tok], start=False, stop=last and j == len(k_of) - 1)
                return ins

            def cols(c):
                return lambda ap, j: ap[:, j, c:c + P]

            def layer(name, n, c, K, hi, lo):
                done(dense(take(name), view(whi, n), view(wlo, n), cols(c), list(range(K)), hi, lo))

            def by_token(out, i, n, K, wcols, hi, lo):
                h, l = view(whi, n), view(wlo, n)
                tok = slice(P * i, P * i + P)
                ins = None
                for j in range(K):
                    mm(out, hi[:, j, tok], wcols(h, j), start=j == 0, stop=False)
                    mm(out, lo[:, j, tok], wcols(h, j), start=False, stop=False)
                    ins = mm(out, hi[:, j, tok], wcols(l, j), start=False, stop=j == K - 1)
                return ins

            def ones_sum(ps, src):
                ins = None
                for half in range(2):
                    for k, s in enumerate(src):
                        ins = mm(ps[:, 512 * half:512 * half + TH], ones, s[:, TH * half:TH * half + TH],
                                 start=k == 0, stop=k == len(src) - 1)
                return ins

            pe.wait_ge(c_loaded, 16)
            pe.wait_ge(S("xn_done"), NT)
            for k in range(KD):
                ps = take(f"xT{k}")
                for i in range(NT):
                    ins = nc.tensor.transpose(ps[:, P * i:P * i + TT[i]], X[0:TT[i], i, P * k:P * k + P],
                                              C("ident", TT[i])[:, 0:TT[i]])
                done(ins)
            pe.wait_ge(S("pad_done"), 3)
            for k in range(4, KD):
                evacuated(f"xT{k}")
            use(0)
            layer("cq0", 0, 0, KD, xhi, xlo)
            layer("cq1", 0, P, KD, xhi, xlo)
            use(1)
            layer("cq2", 1, 0, KD, xhi, xlo)
            use(3)
            for i in range(NT):
                ps = take(f"tok{i}")
                by_token(ps[:, 0:256], i, 2, KD, lambda a, j: a[:, j, :], xhi, xlo)
                done(by_token(ps[:, 256:336], i, 3, KD, lambda a, j: a[:, j, :], xhi, xlo))
            pe.wait_ge(S("sqs_done"), 3)
            done(ones_sum(take("ssq"), [sqs[:, k, :] for k in range(3)]))
            for n, name in ((4, "q"), (5, "k")):
                use(n)
                for m in range(2):
                    layer(f"{name}{m}", n, P * m, KD, xhi, xlo)
            use(7)
            for i in range(NT):
                ps = take(f"v{i}")
                by_token(ps[:, 0:256], i, 6, KD, lambda a, j: a[:, j, :], xhi, xlo)
                done(by_token(ps[:, 256:512], i, 7, KD, lambda a, j: a[:, j, :], xhi, xlo))
            for m in range(4):
                if m % 2 == 0:
                    use(8 + m // 2)
                layer(f"g{m}", 8 + m // 2, P * (m % 2), KD, xhi, xlo)
            for j in range(3):
                ps = take(f"ck{j}")
                for i in range(NT):
                    ins = nc.tensor.transpose(ps[:, P * i:P * i + TT[i]], ctok[0:TT[i], i, P * j:P * j + P],
                                              C("ident", TT[i])[:, 0:TT[i]])
                done(ins)
            ps = take("gr")
            for i in range(NT):
                ins = mm(ps[0:RANK, P * i:P * i + TT[i]], grt[0:TT[i], i, :], C("ident", TT[i])[:, 0:TT[i]], start=True, stop=True)
            done(ins)
            pe.wait_ge(S("qnlo_done"), 1)
            for hh in range(2):
                n = B_UQ + hh
                use(n)
                for x in range(2):
                    layer(f"qn{2 * hh + x}", n, P * x, 3, qnhi, qnlo)
                done(dense(take(f"qp{hh}"), view(whi, n), view(wlo, n), cols(2 * P), list(range(3)), qnhi, qnlo))
            for hh in range(2):
                ps = take(f"sw{hh}")
                evacuated(f"qp{hh}")
                for half in range(2):
                    ins = mm(ps[:, 512 * half:512 * half + TH], C("swap"), qpe[:, hh, TH * half:TH * half + TH], start=True, stop=True)
                done(ins)
            use(B_UKV)
            pe.wait_ge(S("cklo_done"), 2)
            for h in range(MH):
                layer(f"kn{h}", B_UKV, 256 * h, 2, ckhi, cklo)
            for i in range(NT):
                ps = take(f"vm{i}")
                done(by_token(ps[:, 0:512].rearrange("p (h v) -> p h v", h=4), i, B_UKV, 2,
                              lambda a, j: a[:, j, :].rearrange("p (h c) -> p h c", h=4)[:, :, NOPE:256], ckhi, cklo))
            raw = wraw[B_UKV % 2][:, :].rearrange("p (k h c) -> p k h c", k=2, h=4)
            for x in range(2):
                ps = take(f"wuk{x}")
                for y in range(2):
                    for rh in range(2):
                        o = P * (2 * y + rh)
                        ins = nc.tensor.transpose(ps[:, o:o + P], raw[:, rh, 2 * x + y, 0:NOPE], ident)
                done(ins)
            ps = take("qlat")
            evacuated("qn3")
            evacuated("wuk1")
            for rh in range(2):
                for h in range(4):
                    o = 32 * rh + 8 * h
                    ins = mm(ps[:, o:o + 8], wukT[:, h, P * rh:P * rh + P], qnT[:, h, NP:T], start=True, stop=True)
            done(ins)
            ps = take("snew")
            pe.wait_ge(S("prod_done"), 1)
            for x in range(3):
                ins = mm(ps[0:1, 0:32], ones[:, 0:1], prod[:, x, :, :].rearrange("p h b -> p (h b)"), start=x == 0, stop=x == 2)
            done(ins)
            U = NT * MH
            for u in range(U + 2):
                if u < U:
                    qb, h = divmod(u, MH)
                    a, q0, nq = h % 2, P * qb, min(P, NP - P * qb)
                    nk = min(q0 + P, NP)
                    ps = take(f"S{u}")
                    for k0, k1 in ((0, min(nk, 512)), (512, nk)):
                        if k1 > k0:
                            mm(ps[0:nq, k0:k1], qnT[:, h, q0:q0 + nq], knT[:, h, k0:k1], start=True, stop=False)
                            ins = mm(ps[0:nq, k0:k1], qpe[64 * a:64 * a + 64, h // 2, q0:q0 + nq], kpT[64 * a:64 * a + 64, k0:k1],
                                     start=False, stop=True)
                    done(ins)
                if 1 <= u <= U:
                    v = u - 1
                    qb, h = divmod(v, MH)
                    nq = min(P, NP - P * qb)
                    ps = take(f"PT{v}")
                    pe.wait_ge(S("pn_done"), v + 1)
                    for kb in range(min(qb + 1, 4)):
                        ins = nc.tensor.transpose(ps[:, P * kb:P * kb + nq], pr[v % 2][0:nq, P * kb:P * kb + P], C("ident", nq)[:, 0:nq])
                    if qb == 4:
                        ins = mm(ps[0:16, 512:528], pr[v % 2][0:16, 512:528], C("ident", 16)[:, 0:16], start=True, stop=True)
                    done(ins)
                if u >= 2:
                    v = u - 2
                    qb, h = divmod(v, MH)
                    nq = min(P, NP - P * qb)
                    ps = take(f"OM{v}")
                    evacuated(f"PT{v}")
                    for kb in range(qb + 1):
                        nk = min(P, NP - P * kb)
                        ins = mm(ps[:, 0:nq], vm[0:nk, kb, P * h:P * h + P], pt[v % 2][0:nk, kb, 0:nq], start=kb == 0, stop=kb == qb)
                    done(ins)
            base = PLAN["cache0"]
            with pe.Fori(0, NB) as b:
                for e in range(CHUNKS):
                    s_ps, o_ps = pairs[2 * e], pairs[2 * e + 1]
                    pe.wait_ge(S("kt_done"), CHUNKS * b + e + 1)
                    pe.wait_ge(pair_free[2 * e], reads(base + 2 * e) + b)
                    if e == 0:
                        pe.wait_ge(S("qc_done"), b + 1)
                    for c in range(NBLK):
                        for t in range(NG):
                            kk = KT[:, 4 * t:4 * t + 4, c, :] if c < 8 else KTp[:, 4 * t:4 * t + 4, c - 8, :]
                            ins = mm(s_ps[32 * t:32 * t + 32, 0:P], Qc[:, 32 * c:32 * c + 32], kk, start=c == 0, stop=c == NBLK - 1)
                    ins.then_inc(S("sc_done"), 1)
                    pe.wait_ge(S("m_done"), CHUNKS * b + e + 1)
                    mm(s_ps[0:1, 512:512 + P], mc[:, 0:1], ident, start=True, stop=True).then_inc(S("mt_done"), 1)
                    pe.wait_ge(S("mb_done"), CHUNKS * b + e + 1)
                    mm(s_ps[:, 768:769], rows[0:1, 0:P], ones[0:1, 0:1], start=True, stop=True).then_inc(S("mm_done"), 1)
                    pe.wait_ge(pair_free[2 * e + 1], reads(base + 2 * e + 1) + b)
                    pe.wait_ge(S("ps_done"), 2 * (CHUNKS * b + e + 1))
                    for x in range(4):
                        for t in range(NG):
                            unit = 4 * t + x
                            ins = mm(o_ps[32 * t:32 * t + 32, 0:KVL], PS[:, unit, :], KC[e][:, KVL * unit:KVL * unit + KVL],
                                     start=x == 0, stop=x == 3)
                    ins.then_inc(S("pv_done"), 1)
                    pe.wait_ge(S("oc_done"), CHUNKS * b + e + 1)
                    for rh in range(2):
                        mm(o_ps[:, 512 + 4 * rh:516 + 4 * rh], Oc[:, P * rh:P * rh + P], C("selo"), start=True, stop=True)
                    mm(o_ps[0:1, 520:524], mc[:, 2:3], C("sell"), start=True, stop=True).then_inc(S("ot_done"), 1)
            ps = take("wb")
            pe.wait_ge(S("wrow_done"), 1)
            done(mm(ps[:, 0:96], ones[0:1, :], rows[0:1, 256:352], start=True, stop=True))
            ps = take("omd")
            pe.wait_ge(S("olat_done"), 1)
            for h in range(4):
                for rh in range(2):
                    ins = mm(ps[:, 8 * h:8 * h + 8], wuv[:, rh, h, :], olat[:, rh, 8 * h:8 * h + 8], start=rh == 0, stop=rh == 1)
            done(ins)
            for i in range(NT):
                ps = take(f"lg{i}")
                if i == 0:
                    evacuated("gr")
                done(mm(ps[0:TT[i], 0:256], grT[0:RANK + 1, P * i:P * i + TT[i]], wgk[0:RANK + 1, :], start=True, stop=True))
            for c in range(NT):
                ps = take(f"b{c}")
                evacuated(f"lg{c}")
                tri = C("ucum") if c < 4 else C("ucum4", TT[4])
                for q in range(2):
                    ins = mm(ps[:, 512 * q:512 * q + TT[c]], lgs[0:TT[c], c, P * q:P * q + P], tri, start=True, stop=True)
                done(ins)
            for lv in range(NL + 1):
                qq, kk = (qt, kt) if lv < NL else (gq, gk)
                if lv < NL:
                    pe.wait_ge(S("qk_done"), lv + 1)
                for c in range(NT):
                    if f"G{lv}.{c}" in PLAN:
                        n = min(P, NP - P * c)
                        ps = take(f"G{lv}.{c}")
                        for h in (0, 2, 1, 3):
                            a, q = h % 2, h // 2
                            ins = mm(ps[0:n, 512 * a + P * q:512 * a + P * q + n], kk[64 * a:64 * a + 64, q, P * c:P * c + n],
                                     qq[64 * a:64 * a + 64, q, P * c:P * c + n], start=True, stop=True)
                        done(ins)
            pe.wait_ge(S("qk_done"), NL + 1)
            for c in range(NT):
                n = min(P, NP - P * c)
                ps = take(f"kt{c}")
                for q in range(2):
                    ins = mm(ps[0:n, P * q:P * q + P], kt[:, q, P * c:P * c + n], ident, start=True, stop=True)
                done(ins)
                ps = take(f"o{c}")
                evacuated(last_g(c))
                if c:
                    evacuated(f"s{c - 1}")
                for h in (0, 2, 1, 3):
                    a, q = h % 2, h // 2
                    out = ps[:, 512 * a + P * q:512 * a + P * q + n]
                    ins = mm(out, vtok[0:n, c, P * h:P * h + P], AT[0:n, c, 2 * a + q, 0:n], start=True, stop=c == 0)
                    if c:
                        ins = mm(out, Sst[64 * a:64 * a + 64, q, :], qt[64 * a:64 * a + 64, q, P * c:P * c + n], start=False, stop=True)
                done(ins)
                ps = take(f"s{c}")
                evacuated(f"kt{c}")
                for h in range(4):
                    a, q = h % 2, h // 2
                    ins = mm(ps[64 * a:64 * a + 64, P * q:P * q + P], ktok[0:n, q, 64 * a:64 * a + 64], vtok[0:n, c, P * h:P * h + P],
                             start=True, stop=True)
                done(ins)
            pe.wait_ge(S("pick_loaded"), 16)
            for b in range(NB):
                ps = take(f"vb{b}")
                done(mm(ps[:, 0:512], pick[:, b, :], vtok[0:24, 4, :], start=True, stop=True))
            ps = take("os")
            for b in range(NB - 4, NB):
                evacuated(f"vb{b}")
            for b in range(NB):
                for h in (0, 2, 1, 3):
                    a, q = h % 2, h // 2
                    o = 512 * a + 8 * q + b
                    ins = mm(ps[:, o:o + 1], states[64 * a:64 * a + 64, b, q, :], gq[64 * a:64 * a + 64, q, NP + b:NP + b + 1],
                             start=True, stop=True)
            done(ins)
            for h in range(4):
                ps = take(f"ssg{h}")
                pe.wait_ge(S("sqg_done"), h + 1)
                done(ones_sum(ps, [sqg[h % 2]]))
            pe.wait_ge(S("mixlo_done"), 4)
            pe.wait_ge(S("x2_loaded"), 16 * (NT + 2))
            for k in range(KD):
                ps = take(f"hT{k}")
                for i in range(NT):
                    ins = nc.tensor.transpose(ps[:, P * i:P * i + TT[i]], X2[0:TT[i], i, P * k:P * k + P],
                                              C("ident", TT[i])[:, 0:TT[i]])
                done(ins)
            for m in range(KD):
                if m % 2 == 0:
                    use(B_OUT + m // 2)
                layer(f"wo{m}", B_OUT + m // 2, P * (m % 2), KD, xhi, xlo)
            ps = take("ssf")
            pe.wait_ge(S("sqf_done"), KD)
            done(ones_sum(ps, [sqf[:, k, :] for k in range(KD)]))
            base = PLAN["ffn0"]
            pe.wait_ge(S("nlo_done"), KD)
            with pe.Fori(0, DFF // 256) as j:
                for s in range(2):
                    n = B_FFN + s
                    pe.wait_ge(w_lo, n + 1 + 2 * j)
                    for m in range(2):
                        p = 2 * s + m
                        pe.wait_ge(pair_free[p], reads(base + p) + j)
                        done(dense(pairs[p], view(whi, n, KD), view(wlo, n, KD), cols(P * m), list(range(KD)), xhi, xlo))
            base = PLAN["dn0"]
            pe.wait_ge(S("hlo_done"), KF)
            with pe.Fori(0, 2) as j:
                for cb in range(2):
                    for q, (k0, kk) in enumerate(DPARTS):
                        n = B_DOWN + 3 * cb + q
                        pe.wait_ge(w_lo, n + 1 + 6 * j)
                        for m in range(2):
                            p = 2 * cb + m
                            if q == 0:
                                pe.wait_ge(pair_free[p], reads(base + p) + j)
                            ins = dense(pairs[p], view(whi, n, kk), view(wlo, n, kk), cols(P * m), list(range(k0, k0 + kk)), hhi, hlo,
                                        first=q == 0, last=q == 2)
                            if q == 2:
                                done(ins)
                        if q < 2:
                            ins.then_inc(S("dn_part"), 1)
            ps = take("ssy")
            pe.wait_ge(S("sqy_done"), KD)
            done(ones_sum(ps, [sqy[:, k, :] for k in range(KD)]))
            pe.wait_ge(S("yT_done"), KD)
            for i in range(NT):
                ps = take(f"y{i}")
                for k in range(KD):
                    ins = mm(ps[0:TT[i], P * k:P * k + P], yT[:, k, P * i:P * i + TT[i]], ident, start=True, stop=True)
                done(ins)

        @block.scalar
        def _(act):
            f = nc.scalar.activation
            chain = [0]

            def link(ins):
                chain[0] += 1
                ins.then_inc(act_chain, 1)
                act.wait_ge(act_chain, chain[0])

            def ready(name):
                act.wait_ge(pe_done, fills(name))
                return pairs[PLAN[name] % 4]

            def free(ins, name):
                ins.then_inc(pair_free[PLAN[name] % 4], 1)

            def hi(n, size=None):
                act.wait_ge(w_loaded[n % 2], 16 * LOADS[n])
                if n >= 2:
                    act.wait_ge(pe_done, fills(LAST[n - 2]))
                size = size or block_size(n)
                f(whi[n % 2][:, 0:size], wraw[n % 2][:, 0:size], ACT.Copy).then_inc(w_hi, 1)

            def rsqrt(out, src, tmp, width):
                link(f(tmp, src, ACT.Ln, scale=1.0 / width, bias=C("eps", src.shape[0])))
                return f(out, tmp, ACT.Exp, scale=-0.5)

            act.wait_ge(S("stat_clear"), 1)
            act.wait_ge(c_loaded, 16)
            for i in range(NT):
                act.wait_ge(x_loaded[i], 32 if i in (0, 4) else 16)
                link(f(scr[0:TT[i], :], X[0:TT[i], i, :], ACT.Square, accum_out=stat[0:TT[i], i:i + 1]))
            rsqrt(stat[:, 8:8 + NT], stat[:, 0:NT], stat[:, 0:NT], D).then_inc(S("rs_done"), 1)
            hi(0)
            act.wait_ge(n_loaded, 16 * 5)
            act.wait_ge(S("pad_done"), 3)
            for k in range(KD):
                ps = ready(f"xT{k}")
                f(xhi[:, k, 0:T], ps[:, 0:T], ACT.Copy, scale=nrm[:, k:k + 1]).then_inc(S("xhi_done"), 1)
                if k == 5:
                    hi(1)
            for m in range(3):
                if m == 2:
                    hi(2)
                act.wait_ge(pair_free[PLAN[f"cq{m}"] % 4], reads(PLAN[f"cq{m}"]) + 1)
                f(sqs[:, m, :], cq[:, m, :], ACT.Square).then_inc(S("sqs_done"), 1)
            hi(3)
            for i in range(NT):
                ps = ready(f"tok{i}")
                link(f(scr[:, 0:KVL], ps[:, 0:KVL], ACT.Square, accum_out=stat[:, 16 + i:17 + i]))
                rsqrt(stat[:, 24 + i:25 + i], stat[:, 16 + i:17 + i], stat[:, 16 + i:17 + i], KVL).then_inc(S("rk_done"), 1)
            hi(4)
            ps = ready("ssq")
            link(f(split2(rsb[:, :]), halves(ps), ACT.Ln, scale=1.0 / QL, bias=C("eps")))
            ins = f(rsb[:, :], rsb[:, :], ACT.Exp, scale=-0.5)
            free(ins, "ssq")
            hi(5)
            act.wait_ge(S("qn_done"), 1)
            f(qnhi[:, :, :], cq[:, :, :], ACT.Copy).then_inc(S("qnhi_done"), 1)
            for m in range(2):
                free(f(split2(gq[:, m, :]), halves(ready(f"q{m}")), ACT.Copy, scale=DK ** -0.5), f"q{m}")
            hi(6)
            for m in range(2):
                free(f(split2(gk[:, m, :]), halves(ready(f"k{m}")), ACT.Copy), f"k{m}")
            hi(7)
            for i in range(NT):
                free(f(vtok[:, i, :], ready(f"v{i}")[:, 0:512], ACT.Copy), f"v{i}")
            hi(8)
            hi(9)
            for m in range(4):
                f(split2(gT[:, m, :]), halves(ready(f"g{m}")), ACT.Exp, scale=-1.0).then_inc(S("ge_done"), 1)
                if m == 2:
                    hi(10)
            hi(11)
            for j in range(2):
                f(ckhi[:, j, 0:T], ready(f"ck{j}")[:, 0:T], ACT.Copy).then_inc(S("ckhi_done"), 1)
            for hh in range(2):
                for x in range(2):
                    free(f(split2(qnT[:, 2 * hh + x, :]), halves(ready(f"qn{2 * hh + x}")), ACT.Copy), f"qn{2 * hh + x}")
                free(f(split2(qpe[:, hh, :]), halves(ready(f"qp{hh}")), ACT.Copy), f"qp{hh}")
                hi(12 + hh)
            for h in range(MH):
                free(f(split2(knT[:, h, :]), halves(ready(f"kn{h}")), ACT.Copy), f"kn{h}")
            for x in range(2):
                free(f(wukT[:, 2 * x:2 * x + 2, :].rearrange("p a b -> p (a b)"), ready(f"wuk{x}")[:, 0:512], ACT.Copy), f"wuk{x}")
            hi(14)
            U = NT * MH
            for u in range(U + 2):
                if u < U:
                    qb = u // MH
                    nq, nk = min(P, NP - P * qb), min(P * qb + P, NP)
                    s = 32 + 4 * (u % 2)
                    ps = ready(f"S{u}")
                    act.wait_ge(S("nmax_done"), u + 1)
                    if u >= 2:
                        act.wait_ge(pe_done, fills(f"PT{u - 2}"))
                    free(f(pr[u % 2][0:nq, 0:nk], ps[0:nq, 0:nk], ACT.Exp, scale=SCALE, bias=stat[0:nq, s + 1:s + 2],
                           accum_out=stat[0:nq, s + 2:s + 3]), f"S{u}")
                if 1 <= u <= U:
                    v = u - 1
                    qb = v // MH
                    nq = min(P, NP - P * qb)
                    ps = ready(f"PT{v}")
                    if v >= 2:
                        act.wait_ge(pe_done, fills(f"OM{v - 2}"))
                    nb = min(qb + 1, 4)
                    ins = f(pt[v % 2][:, 0:nb, 0:nq], ps[:, 0:P * nb].rearrange("p (k q) -> p k q", q=P)[:, :, 0:nq], ACT.Copy)
                    if qb == 4:
                        ins = f(pt[v % 2][0:16, 4, 0:16], ps[0:16, 512:528], ACT.Copy)
                    free(ins, f"PT{v}")
                if u >= 2:
                    v = u - 2
                    qb, h = divmod(v, MH)
                    nq = min(P, NP - P * qb)
                    f(xhi[:, 4 + h, P * qb:P * qb + nq], ready(f"OM{v}")[:, 0:nq], ACT.Copy).then_inc(S("omhi_done"), 1)
            act.wait_ge(S("Qall_done"), 1)
            with act.Fori(0, NB) as b:
                f(Qc[:, :], Qall[:, bass.ds(b, 1), :].rearrange("p a n -> p (a n)"), ACT.Copy).then_inc(S("qc_done"), 1)
                for e in range(CHUNKS):
                    s_ps, o_ps = pairs[2 * e], pairs[2 * e + 1]
                    act.wait_ge(S("mm_done"), CHUNKS * b + e + 1)
                    f(mc[:, 1:2], s_ps[:, 768:769], ACT.Copy, scale=-SCALE).then_inc(S("nm_done"), 1)
                    act.wait_ge(S("nm_done"), CHUNKS * b + e + 1)
                    f(Pc[:, :], s_ps[:, 0:P], ACT.Exp, scale=SCALE, bias=mc[:, 1:2], accum_out=mc[:, 2:3]).then_inc(pair_free[2 * e], 1)
                    act.wait_ge(S("pt_done"), CHUNKS * b + e + 1)
                    for t in (0, 1):
                        for gg in range(NG):
                            ins = f(PS[32 * gg:32 * gg + 32, 4 * t:4 * t + 4, 0:4], Pt[32 * t:32 * t + 32, :, 4 * gg:4 * gg + 4], ACT.Copy)
                    ins.then_inc(S("ps_done"), 1)
                    act.wait_ge(S("pv_done"), CHUNKS * b + e + 1)
                    f(Oc[:, :], o_ps[:, 0:KVL], ACT.Copy).then_inc(S("oc_done"), 1)
            act.wait_ge(S("wdiff_done"), 1)
            f(rows[0:1, 256:352], rows[0:1, 256:352], ACT.Exp, scale=SCALE).then_inc(S("wexp_done"), 1)
            f(xhi[:, 4:8, NP:T], ready("omd")[:, 0:32].rearrange("p (h b) -> p h b", h=4), ACT.Copy).then_inc(S("omdhi_done"), 1)
            for i in range(NT):
                ps = ready(f"lg{i}")
                r = TT[i]
                if i:
                    act.wait_ge(pair_free[PLAN[f"lg{i - 1}"] % 4], reads(PLAN[f"lg{i - 1}"]) + 1)
                else:
                    act.wait_ge(pair_free[PLAN["omd"] % 4], reads(PLAN["omd"]) + 1)
                link(f(lgt[0:r, :], ps[0:r, 0:256], ACT.Abs))
                link(f(lgt[0:r, :], lgt[0:r, :], ACT.Exp, scale=-1.0))
                f(lgt[0:r, :], lgt[0:r, :], ACT.Ln, bias=1.0).then_inc(S("lgt_done"), 1)
            for c in range(NT):
                ps = ready(f"b{c}")
                free(f(bT[:, :, P * c:P * c + TT[c]], ps[:, :].rearrange("p (q t) -> p q t", q=2)[:, :, 0:TT[c]], ACT.Copy), f"b{c}")
            for lv in range(NL):
                n = 512 if LEVELS[lv] > 8 else NP
                act.wait_ge(S("diff_done"), lv + 1)
                f(Ee[:, :, 0:n], Ee[:, :, 0:n], ACT.Exp).then_inc(S("E_done"), 1)
            act.wait_ge(S("qk_done"), NL)
            f(Ee[:, :, :], bT[:, :, 0:NP], ACT.Exp).then_inc(S("E_done"), 1)
            f(eb[:, :, :], bT[:, :, NP:T], ACT.Exp).then_inc(S("eb_done"), 1)
            act.wait_ge(S("diff_done"), NL + 1)
            f(Ee[:, :, :], Ee[:, :, :], ACT.Exp).then_inc(S("E_done"), 1)
            f(el[:, :, 0:4], bT[:, :, P - 1:4 * P:P], ACT.Exp)
            f(el[:, :, 4:5], bT[:, :, NP - 1:NP], ACT.Exp).then_inc(S("eb_done"), 1)
            for c in range(NT):
                n = min(P, NP - P * c)
                ps = ready(f"kt{c}")
                if c:
                    act.wait_ge(pe_done, fills(f"s{c - 1}"))
                free(f(ktok[0:n, :, :], ps[0:n, 0:256].rearrange("p (q d) -> p q d", q=2), ACT.Copy), f"kt{c}")
                ps = ready(f"o{c}")
                free(f(oT[:, :, P * c:P * c + n].rearrange("p (q a) t -> p a q t", a=2),
                       ps[:, :].rearrange("p (a q t) -> p a q t", a=2, q=4)[:, :, 0:2, 0:n], ACT.Copy), f"o{c}")
            ps = ready("os")
            ins = f(oT[:, :, NP:T].rearrange("p (q a) t -> p a q t", a=2),
                    ps[:, :].rearrange("p (a q t) -> p a q t", a=2, q=64)[:, :, 0:2, :], ACT.Copy)
            free(ins, "os")
            act.wait_ge(pair_free[PLAN["os"] % 4], reads(PLAN["os"]) + 1)
            for h in range(4 + 1):
                if h < 4:
                    if h >= 2:
                        act.wait_ge(pe_done, fills(f"ssg{h - 2}"))
                    f(sqg[h % 2][:, :], oT[:, h, :], ACT.Square).then_inc(S("sqg_done"), 1)
                if h >= 1:
                    v = h - 1
                    if v >= 2:
                        act.wait_ge(S("mixlo_done"), v - 1)
                    link(f(split2(rsg[v % 2][:, :]), halves(ready(f"ssg{v}")), ACT.Ln, scale=1.0 / DV, bias=C("eps")))
                    free(f(rsg[v % 2][:, :], rsg[v % 2][:, :], ACT.Exp, scale=-0.5), f"ssg{v}")
                    act.wait_ge(S("og_done"), v + 1)
                    f(xhi[:, v, 0:T], oT[:, v, :], ACT.Copy).then_inc(S("mixhi_done"), 1)
            for k in range(KD):
                free(f(hT[:, k, :], ready(f"hT{k}")[:, 0:T], ACT.Copy), f"hT{k}")
            for m in range(KD):
                if m in (2, 4, 6):
                    hi(14 + m // 2)
                act.wait_ge(pair_free[PLAN[f"wo{m}"] % 4], reads(PLAN[f"wo{m}"]) + 1)
                f(sqf[:, m, :], hT[:, m, :], ACT.Square).then_inc(S("sqf_done"), 1)
            hi(18)
            ps = ready("ssf")
            link(f(split2(rsf[:, :]), halves(ps), ACT.Ln, scale=1.0 / D, bias=C("eps")))
            free(f(rsf[:, :], rsf[:, :], ACT.Exp, scale=-0.5), "ssf")
            for k in range(KD):
                act.wait_ge(S("tf_done"), k + 1)
                f(xhi[:, k, 0:T], tf[k % 2][:, :], ACT.Copy).then_inc(S("nhi_done"), 1)
            base = PLAN["ffn0"]
            with act.Fori(0, DFF // 256) as j:
                for m in range(2):
                    act.wait_ge(pe_done, fills("ffn0") + 4 * j + m)
                    act.wait_ge(w_lo, B_FFN + 2 + 2 * j)
                    f(split2(fe[m][:, :]), halves(pairs[m]), ACT.Exp, scale=-1.0).then_inc(S("fe_done"), 1)
                for s in range(2):
                    if s == 1:
                        for m in range(2):
                            act.wait_ge(pair_free[2 + m], reads(base + 2 + m) + 1 + j)
                            f(hhi[:, bass.ds(2 * j + m, 1), :].rearrange("p a t -> p (a t)"), fe[m][:, :], ACT.Copy).then_inc(S("hhi_done"), 1)
                    n = B_FFN + s
                    act.wait_ge(pe_done, fills("ffn0") + 4 * j + 2 * s + 1)
                    act.wait_ge(w_loaded[n % 2], 16 * (LOADS[n] + 1) + 16 * j)
                    f(whi[n % 2][:, :], wraw[n % 2][:, :], ACT.Copy).then_inc(w_hi, 1)
            for cb in range(4):
                for q in range(3):
                    n = B_DOWN + 3 * cb + q + 2
                    if n < B_DOWN + 12:
                        if q < 2:
                            act.wait_ge(S("dn_part"), 2 * cb + q + 1)
                        else:
                            act.wait_ge(pe_done, fills(f"dn{2 * cb + 1}"))
                        act.wait_ge(w_loaded[n % 2], 16 * LOADS[n])
                        size = 256 * DPARTS[(q + 2) % 3][1]
                        f(whi[n % 2][:, 0:size], wraw[n % 2][:, 0:size], ACT.Copy).then_inc(w_hi, 1)
                for m in (2 * cb, 2 * cb + 1):
                    act.wait_ge(pair_free[PLAN[f"dn{m}"] % 4], reads(PLAN[f"dn{m}"]) + 1)
                    if m == 0:
                        act.wait_ge(pe_done, fills("dn0"))
                    f(sqy[:, m, :], hT[:, m, :], ACT.Square).then_inc(S("sqy_done"), 1)
            ps = ready("ssy")
            link(f(split2(rsy[:, :]), halves(ps), ACT.Ln, scale=1.0 / D, bias=C("eps")))
            free(f(rsy[:, :], rsy[:, :], ACT.Exp, scale=-0.5), "ssy")
            for i in range(NT):
                if i >= 2:
                    act.wait_ge(S(f"y_out{i % 2}"), 16 * (i // 2))
                f(ysb[i % 2][0:TT[i], 0:512], ready(f"y{i}")[0:TT[i], 0:512], ACT.Copy).then_inc(S("y_half"), 1)

        @block.vector
        def _(dve):
            v_ = nc.vector
            tt, ts, stt = v_.tensor_tensor, v_.tensor_scalar, v_.scalar_tensor_tensor
            chain = [0]

            def link(ins):
                chain[0] += 1
                ins.then_inc(dve_chain, 1)
                dve.wait_ge(dve_chain, chain[0])

            def ready(name):
                dve.wait_ge(pe_done, fills(name))
                return pairs[PLAN[name] % 4]

            def free(ins, name):
                ins.then_inc(pair_free[PLAN[name] % 4], 1)

            def lo(n):
                dve.wait_ge(w_hi, n + 1)
                size = block_size(n)
                tt(wlo[n % 2][:, 0:size], wraw[n % 2][:, 0:size], whi[n % 2][:, 0:size].bitcast(F32), ALU.subtract).then_inc(w_lo, 1)

            def rest(out, value, high):
                return tt(out, value, high.bitcast(F32), ALU.subtract)

            v_.memset(stat[:, :], 1.0).then_inc(S("stat_clear"), 1)
            dve.wait_ge(S("rs_done"), 1)
            for i in range(NT):
                ts(X[0:TT[i], i, :], X[0:TT[i], i, :], stat[0:TT[i], 8 + i:9 + i], None, ALU.mult).then_inc(S("xn_done"), 1)
            lo(0)
            dve.wait_ge(n_loaded, 16 * 5)
            for k in range(KD):
                dve.wait_ge(S("xhi_done"), k + 1)
                ps = ready(f"xT{k}")
                free(stt(xlo[:, k, 0:T], ps[:, 0:T], nrm[:, k:k + 1], xhi[:, k, 0:T].bitcast(F32), ALU.mult, ALU.subtract), f"xT{k}")
            lo(1)
            v_.memset(ckhi[:, :, T:TPAD].bitcast(F32), 0.0)
            v_.memset(cklo[:, :, T:TPAD].bitcast(F32), 0.0)
            for m in range(3):
                if m == 2:
                    lo(2)
                free(v_.tensor_copy(split2(cq[:, m, :]), halves(ready(f"cq{m}"))), f"cq{m}")
            lo(3)
            dve.wait_ge(small_loaded, 16 * 3)
            for i in range(NT):
                ps = ready(f"tok{i}")
                dve.wait_ge(S("rk_done"), i + 1)
                cos, sin = C("cosk")[:, ROPE * i:ROPE * i + ROPE], C("sink")[:, ROPE * i:ROPE * i + ROPE]
                tt(rp[:, 0, :], ps[:, 256:320], cos, ALU.mult)
                tt(rp[:, 1, 0:HALF], ps[:, 256 + HALF:320], sin[:, 0:HALF], ALU.mult)
                link(tt(rp[:, 1, HALF:ROPE], ps[:, 256:256 + HALF], sin[:, HALF:ROPE], ALU.mult))
                v_.tensor_copy(grt[:, i, :], ps[:, 320:336])
                tt(ctok[:, i, 256:320], rp[:, 0, :], rp[:, 1, :], ALU.add)
                link(tt(ctok[:, i, 320:384], rp[:, 0, :], rp[:, 1, :], ALU.add))
                free(stt(ctok[:, i, 0:KVL], ps[:, 0:KVL], stat[:, 24 + i:25 + i], kvn[:, :], ALU.mult, ALU.mult), f"tok{i}")
            lo(4)
            dve.wait_ge(pair_free[PLAN["ssq"] % 4], reads(PLAN["ssq"]) + 1)
            for m in range(3):
                ins = stt(cq[:, m, :], cq[:, m, :], nrm[:, 3 * KD + m:3 * KD + m + 1], rsb[:, :], ALU.mult, ALU.mult)
            ins.then_inc(S("qn_done"), 1)
            lo(5)
            dve.wait_ge(S("qnhi_done"), 1)
            rest(qnlo[:, :, :], cq[:, :, :], qnhi[:, :, :]).then_inc(S("qnlo_done"), 1)
            for n in (6, 7, 8, 9):
                lo(n)
            for m in range(4):
                dve.wait_ge(S("ge_done"), m + 1)
                link(ts(gT[:, m, :], gT[:, m, :], 1.0, None, ALU.add))
                link(v_.reciprocal(gT[:, m, :], gT[:, m, :]))
                free(tt(split2(gT[:, m, :]), split2(gT[:, m, :]), halves(ready(f"g{m}")), ALU.mult), f"g{m}")
                if m == 3:
                    lo(10)
            for j in range(3):
                ps = ready(f"ck{j}")
                if j < 2:
                    dve.wait_ge(S("ckhi_done"), j + 1)
                    rest(cklo[:, j, 0:T], ps[:, 0:T], ckhi[:, j, 0:T]).then_inc(S("cklo_done"), 1)
                    free(v_.tensor_copy(cks[:, j, :], ps[:, NP:T]), f"ck{j}")
                else:
                    free(v_.tensor_copy(kpT[:, :], ps[:, 0:T]), f"ck{j}")
            dve.wait_ge(S("pad_done"), 3)
            free(v_.tensor_copy(grT[0:RANK, :], ready("gr")[0:RANK, 0:T]), "gr")
            lo(11)
            lo(12)
            lo(13)
            for hh in range(2):
                ps = ready(f"sw{hh}")
                free(tt(split2(rsb[:, :]), halves(ps), split2(C("sinf")), ALU.mult), f"sw{hh}")
                link(tt(qpe[:, hh, :], qpe[:, hh, :], C("cosf"), ALU.mult))
                dve.wait_ge(pair_free[PLAN[f"sw{hh}"] % 4], reads(PLAN[f"sw{hh}"]) + 1)
                ins = tt(qpe[:, hh, :], qpe[:, hh, :], rsb[:, :], ALU.add)
                if hh == 0:
                    link(ins)
            ins.then_inc(S("qpe_done"), 1)
            for i in range(NT):
                free(v_.tensor_copy(vm[:, i, :], ready(f"vm{i}")[:, 0:512]), f"vm{i}")
            ps = ready("qlat")
            v_.tensor_copy(qlT[:, :, :, :], ps[:, 0:64].rearrange("p (r h b) -> p r h b", r=2, h=4)).then_inc(pair_free[PLAN["qlat"] % 4], 1)
            dve.wait_ge(pair_free[PLAN["qlat"] % 4], reads(PLAN["qlat"]) + 1)
            for rh in range(2):
                tt(prod[:, rh, :, :], qlT[:, rh, :, :], cks[:, rh:rh + 1, :].broadcast_to([P, 4, NB]), ALU.mult)
            dve.wait_ge(S("qpe_done"), 1)
            link(v_.memset(prod[:, 2, :, :], 0.0))
            for a in range(2):
                r = slice(64 * a, 64 * a + 64)
                ins = tt(prod[r, 2, a:4:2, :], qpe[r, :, NP:T], kpT[r, NP:T].unsqueeze(1).broadcast_to([64, 2, NB]), ALU.mult)
            ins.then_inc(S("prod_done"), 1)
            free(v_.tensor_copy(rows[0:1, 352:384], ready("snew")[0:1, 0:32]), "snew")
            lo(14)
            U = NT * MH
            for u in range(U + 2):
                if u < U:
                    qb = u // MH
                    q0, nq, nk = P * qb, min(P, NP - P * qb), min(P * qb + P, NP)
                    s = 32 + 4 * (u % 2)
                    ps = ready(f"S{u}")
                    link(tt(ps[0:nq, q0:nk], ps[0:nq, q0:nk], C("cap", nq)[:, 0:nq], ALU.min))
                    link(v_.reduce_max(stat[0:nq, s:s + 1], ps[0:nq, 0:nk], AX))
                    ts(stat[0:nq, s + 1:s + 2], stat[0:nq, s:s + 1], -SCALE, None, ALU.mult).then_inc(S("nmax_done"), 1)
                    dve.wait_ge(pair_free[PLAN[f"S{u}"] % 4], reads(PLAN[f"S{u}"]) + 1)
                    link(v_.reciprocal(stat[0:nq, s + 3:s + 4], stat[0:nq, s + 2:s + 3]))
                    ts(pr[u % 2][0:nq, 0:nk], pr[u % 2][0:nq, 0:nk], stat[0:nq, s + 3:s + 4], None, ALU.mult).then_inc(S("pn_done"), 1)
                if u >= 2:
                    v = u - 2
                    qb, h = divmod(v, MH)
                    nq = min(P, NP - P * qb)
                    dve.wait_ge(S("omhi_done"), v + 1)
                    ins = rest(xlo[:, 4 + h, P * qb:P * qb + nq], ready(f"OM{v}")[:, 0:nq], xhi[:, 4 + h, P * qb:P * qb + nq])
                    free(ins, f"OM{v}")
            with dve.Fori(0, NB) as b:
                for e in range(CHUNKS):
                    s_ps, o_ps = pairs[2 * e], pairs[2 * e + 1]
                    n = CHUNKS * b + e
                    dve.wait_ge(S(f"kc_loaded{e}"), 32 + 32 * b)
                    v_.transpose(KT[:, :, :, :].rearrange("p u c j -> p (u c j)").bitcast(U32), KC[e][:, :].bitcast(U32))
                    v_.transpose(KTp[:, :, :, :].rearrange("p u c j -> p (u c j)").bitcast(U32), KP[e][:, :].bitcast(U32)).then_inc(S("kt_done"), 1)
                    dve.wait_ge(S("sc_done"), n + 1)
                    v_.reduce_max(mc[:, 0:1], s_ps[:, 0:P], AX).then_inc(S("m_done"), 1)
                    dve.wait_ge(S("mt_done"), n + 1)
                    v_.reduce_max(rows[0:1, 128:132], s_ps[0:1, 512:512 + P].rearrange("o (x h) -> o h x", h=4), AX).then_inc(S("mr_done"), 1)
                    dve.wait_ge(S("mr_done"), n + 1)
                    v_.tensor_copy(rows[0:1, bass.ds(384 + 8 * b + 4 * e, 4)], rows[0:1, 128:132])
                    v_.tensor_copy(rows[0:1, 0:P].rearrange("o (x h) -> o x h", h=4),
                                   rows[0:1, 128:132].unsqueeze(1).broadcast_to([1, 32, 4])).then_inc(S("mb_done"), 1)
                    dve.wait_ge(pair_free[2 * e], reads(PLAN["cache0"] + 2 * e) + 1 + b)
                    v_.transpose(Pt[:, :, :].rearrange("p u j -> p (u j)").bitcast(U32), Pc[:, :].bitcast(U32)).then_inc(S("pt_done"), 1)
                    dve.wait_ge(S("pt_done"), n + 1)
                    for t in (2, 3):
                        for gg in range(NG):
                            ins = v_.tensor_copy(PS[32 * gg:32 * gg + 32, 4 * t:4 * t + 4, 0:4], Pt[32 * t:32 * t + 32, :, 4 * gg:4 * gg + 4])
                    ins.then_inc(S("ps_done"), 1)
                    dve.wait_ge(S("ot_done"), n + 1)
                    for rh in range(2):
                        v_.tensor_copy(olT[:, bass.ds(2 * NB * rh + 2 * b + e, 1), :].rearrange("p a h -> p (a h)"), o_ps[:, 512 + 4 * rh:516 + 4 * rh])
                    v_.tensor_copy(rows[0:1, bass.ds(448 + 8 * b + 4 * e, 4)], o_ps[0:1, 520:524]).then_inc(pair_free[2 * e + 1], 1)
            last = PLAN["cache31"]
            dve.wait_ge(pair_free[last % 4], reads(last) + 1)

            def by(o):
                return rows[0:1, o:o + 64].rearrange("o (b e h) -> o e h b", e=2, h=4)

            M, L, W = by(384), by(448), rows[0:1, 256:352].rearrange("o (e h b) -> o e h b", e=3, h=4)
            sn = rows[0:1, 352:384].rearrange("o (h b) -> o h b", h=4)
            mx = rows[0:1, 160:192].rearrange("o (h b) -> o h b", h=4)
            tw = rows[0:1, 192:256].rearrange("o (e h b) -> o e h b", e=2, h=4)
            link(tt(mx, M[:, 0], M[:, 1], ALU.max))
            link(tt(mx, mx, sn, ALU.max))
            for e in range(2):
                tt(W[:, e], M[:, e], mx, ALU.subtract)
            tt(W[:, 2], sn, mx, ALU.subtract).then_inc(S("wdiff_done"), 1)
            dve.wait_ge(S("wexp_done"), 1)
            for e in range(2):
                ins = tt(tw[:, e], W[:, e], L[:, e], ALU.mult)
            link(ins)
            link(tt(mx, tw[:, 0], tw[:, 1], ALU.add))
            link(tt(mx, mx, W[:, 2], ALU.add))
            link(v_.reciprocal(mx, mx))
            for e in range(3):
                ins = tt(W[:, e], W[:, e], mx, ALU.mult)
            ins.then_inc(S("wrow_done"), 1)
            free(v_.tensor_copy(wbc[:, :], ready("wb")[:, 0:96]), "wb")
            dve.wait_ge(pair_free[PLAN["wb"] % 4], reads(PLAN["wb"]) + 1)
            wv = wbc[:, :].rearrange("p (e h b) -> p e h b", e=3, h=4)
            for rh in range(2):
                o = olT[:, 2 * NB * rh:2 * NB * rh + 2 * NB, :].rearrange("p (b e) h -> p e h b", e=2)
                out = olat[:, rh, :].rearrange("p (h b) -> p h b", h=4)
                tmp = otmp[:, :].rearrange("p (h b) -> p h b", h=4)
                link(tt(out, o[:, 0], wv[:, 0], ALU.mult))
                link(tt(tmp, o[:, 1], wv[:, 1], ALU.mult))
                link(tt(out, out, tmp, ALU.add))
                link(tt(tmp, cks[:, rh:rh + 1, :].broadcast_to([P, 4, NB]), wv[:, 2], ALU.mult))
                ins = tt(out, out, tmp, ALU.add)
                if rh == 0:
                    link(ins)
            ins.then_inc(S("olat_done"), 1)
            dve.wait_ge(S("omdhi_done"), 1)
            ps = ready("omd")
            rest(xlo[:, 4:8, NP:T], ps[:, 0:32].rearrange("p (h b) -> p h b", h=4), xhi[:, 4:8, NP:T]).then_inc(pair_free[PLAN["omd"] % 4], 1)
            for i in range(NT):
                dve.wait_ge(S("lgt_done"), i + 1)
                r = TT[i]
                free(stt(lgs[0:r, i, :], ready(f"lg{i}")[0:r, 0:256], 0.0, lgt[0:r, :], ALU.min, ALU.subtract), f"lg{i}")
            v_.memset(AT[:, :, :, :], 0.0)
            dve.wait_ge(S("msk_loaded"), 16)
            for c in range(NT):
                dve.wait_ge(pair_free[PLAN[f"b{c}"] % 4], reads(PLAN[f"b{c}"]) + 1)
            for lv in range(NL + 1):
                if lv < NL:
                    s = LEVELS[lv]
                    n = 512 if s > 8 else NP
                    nb = n // (2 * s)
                    if lv:
                        dve.wait_ge(S("E_done"), lv)
                    for q in range(2):
                        bb = bT[:, q, 0:n].rearrange("p (n a s) -> p n a s", a=2, s=s)
                        ee = Ee[:, q, 0:n].rearrange("p (n a s) -> p n a s", a=2, s=s)
                        mid = bb[:, :, 0, s - 1:s].broadcast_to([P, nb, s])
                        tt(ee[:, :, 1, :], bb[:, :, 1, :], mid, ALU.subtract)
                        ins = tt(ee[:, :, 0, :], mid, bb[:, :, 0, :], ALU.subtract)
                    ins.then_inc(S("diff_done"), 1)
                    dve.wait_ge(S("E_done"), lv + 1)
                    if lv:
                        dve.wait_ge(pe_done, fills(last_of_level(lv - 1)))
                    tt(qt[:, :, 0:n], gq[:, :, 0:n], Ee[:, :, 0:n], ALU.mult)
                    tt(kt[:, :, 0:n], gk[:, :, 0:n], Ee[:, :, 0:n], ALU.mult).then_inc(S("qk_done"), 1)
                for c in range(NT):
                    if f"G{lv}.{c}" in PLAN:
                        n = min(P, NP - P * c)
                        ps = ready(f"G{lv}.{c}")
                        data = ps[0:n, :].rearrange("p (a q t) -> p a q t", a=2, q=4)[:, :, 0:2, 0:n]
                        out = AT[0:n, c, :, 0:n].rearrange("p (a q) t -> p a q t", a=2)
                        mask = msk[0:n, lv:lv + 1, 0:n].unsqueeze(1).broadcast_to([n, 2, 2, n])
                        free(v_.copy_predicated(out, mask.bitcast(U32), data), f"G{lv}.{c}")
            dve.wait_ge(pair_free[PLAN[f"G{NL}.4"] % 4], reads(PLAN[f"G{NL}.4"]) + 1)
            dve.wait_ge(pe_done, fills(last_of_level(NL - 1)))
            dve.wait_ge(S("qk_done"), NL)
            dve.wait_ge(S("E_done"), NL + 1)
            link(tt(qt[:, :, :], gq[:, :, 0:NP], Ee[:, :, :], ALU.mult))
            for c in range(NT):
                n = min(P, NP - P * c)
                e = P * c + n
                ins = tt(Ee[:, :, P * c:e], bT[:, :, e - 1:e].broadcast_to([P, 2, n]), bT[:, :, P * c:e], ALU.subtract)
            ins.then_inc(S("diff_done"), 1)
            dve.wait_ge(S("E_done"), NL + 2)
            tt(kt[:, :, :], gk[:, :, 0:NP], Ee[:, :, :], ALU.mult).then_inc(S("qk_done"), 1)
            dve.wait_ge(S("eb_done"), 2)
            for c in range(NT):
                ps = ready(f"s{c}")
                if c == 0:
                    ins = v_.tensor_copy(Sst[:, :, :], ps[:, 0:256].rearrange("p (q v) -> p q v", q=2))
                else:
                    dve.wait_ge(pair_free[PLAN[f"s{c - 1}"] % 4], reads(PLAN[f"s{c - 1}"]) + 1)
                    for q in range(2):
                        ins = stt(Sst[:, q, :], Sst[:, q, :], el[:, q, c:c + 1], ps[:, P * q:P * q + P], ALU.mult, ALU.add)
                free(ins, f"s{c}")
            dve.wait_ge(S("states_loaded"), 16 * 2 * NB)
            for b in range(NB):
                for q in range(2):
                    ins = ts(states[:, b, q, :], states[:, b, q, :], eb[:, q, b:b + 1], None, ALU.mult)
            link(ins)
            for b in range(NB):
                ps = ready(f"vb{b}")
                for h in range(4):
                    a, q = h % 2, h // 2
                    r = slice(64 * a, 64 * a + 64)
                    ins = stt(states[r, b, q, :], ps[r, P * h:P * h + P], gk[r, q, NP + b:NP + b + 1], states[r, b, q, :], ALU.mult, ALU.add)
                free(ins, f"vb{b}")
            for h in range(4):
                dve.wait_ge(pair_free[PLAN[f"ssg{h}"] % 4], reads(PLAN[f"ssg{h}"]) + 1)
                link(stt(oT[:, h, :], oT[:, h, :], nrm[:, 3 * KD + 3:3 * KD + 4], rsg[h % 2][:, :], ALU.mult, ALU.mult))
                tt(oT[:, h, :], oT[:, h, :], gT[:, h, :], ALU.mult).then_inc(S("og_done"), 1)
                dve.wait_ge(S("mixhi_done"), h + 1)
                rest(xlo[:, h, 0:T], oT[:, h, :], xhi[:, h, 0:T]).then_inc(S("mixlo_done"), 1)
            for m in range(KD):
                if m in (2, 4, 6):
                    lo(14 + m // 2)
                ps = ready(f"wo{m}")
                dve.wait_ge(pair_free[PLAN[f"hT{m}"] % 4], reads(PLAN[f"hT{m}"]) + 1)
                free(tt(split2(hT[:, m, :]), split2(hT[:, m, :]), halves(ps), ALU.add), f"wo{m}")
            lo(18)
            dve.wait_ge(pair_free[PLAN["ssf"] % 4], reads(PLAN["ssf"]) + 1)
            for k in range(KD + 1):
                if k < KD:
                    if k >= 2:
                        dve.wait_ge(S("nlo_done"), k - 1)
                    stt(tf[k % 2][:, :], hT[:, k, :], nrm[:, KD + k:KD + k + 1], rsf[:, :], ALU.mult, ALU.mult).then_inc(S("tf_done"), 1)
                if k:
                    dve.wait_ge(S("nhi_done"), k)
                    rest(xlo[:, k - 1, 0:T], tf[(k - 1) % 2][:, :], xhi[:, k - 1, 0:T]).then_inc(S("nlo_done"), 1)
            base = PLAN["ffn0"]
            per = 4
            c0 = chain[0]
            with dve.Fori(0, DFF // 256) as j:
                for m in range(2):
                    dve.wait_ge(S("fe_done"), 2 * j + m + 1)
                    ts(fe[m][:, :], fe[m][:, :], 1.0, None, ALU.add).then_inc(dve_chain, 1)
                    dve.wait_ge(dve_chain, c0 + per * j + 2 * m + 1)
                    v_.reciprocal(fe[m][:, :], fe[m][:, :]).then_inc(dve_chain, 1)
                    dve.wait_ge(dve_chain, c0 + per * j + 2 * m + 2)
                    tt(split2(fe[m][:, :]), split2(fe[m][:, :]), halves(pairs[m]), ALU.mult).then_inc(pair_free[m], 1)
                for s in range(2):
                    if s == 1:
                        for m in range(2):
                            dve.wait_ge(pe_done, fills("ffn0") + 4 * j + 2 + m)
                            dve.wait_ge(pair_free[m], reads(base + m) + 1 + j)
                            tt(split2(fe[m][:, :]), split2(fe[m][:, :]), halves(pairs[2 + m]), ALU.mult).then_inc(pair_free[2 + m], 1)
                            dve.wait_ge(S("hhi_done"), 2 * j + m + 1)
                            rest(hlo[:, bass.ds(2 * j + m, 1), :].rearrange("p a t -> p (a t)"), fe[m][:, :],
                                 hhi[:, bass.ds(2 * j + m, 1), :].rearrange("p a t -> p (a t)")).then_inc(S("hlo_done"), 1)
                    n = B_FFN + s
                    dve.wait_ge(w_hi, n + 3 + 2 * j)
                    tt(wlo[n % 2][:, :], wraw[n % 2][:, :], whi[n % 2][:, :].bitcast(F32), ALU.subtract).then_inc(w_lo, 1)
            chain[0] = c0 + per * (DFF // 256)
            for cb in range(4):
                for q in range(3):
                    n = B_DOWN + 3 * cb + q + 2
                    if n < B_DOWN + 12:
                        dve.wait_ge(w_hi, n + 1)
                        size = 256 * DPARTS[(q + 2) % 3][1]
                        tt(wlo[n % 2][:, 0:size], wraw[n % 2][:, 0:size], whi[n % 2][:, 0:size].bitcast(F32), ALU.subtract).then_inc(w_lo, 1)
                for m in (2 * cb, 2 * cb + 1):
                    free(tt(split2(hT[:, m, :]), split2(hT[:, m, :]), halves(ready(f"dn{m}")), ALU.add), f"dn{m}")
            dve.wait_ge(pair_free[PLAN["ssy"] % 4], reads(PLAN["ssy"]) + 1)
            for k in range(KD):
                stt(yT[:, k, :], hT[:, k, :], nrm[:, 2 * KD + k:2 * KD + k + 1], rsy[:, :], ALU.mult, ALU.mult).then_inc(S("yT_done"), 1)
            for i in range(NT):
                dve.wait_ge(S("y_half"), i + 1)
                ps = ready(f"y{i}")
                free(v_.tensor_copy(ysb[i % 2][0:TT[i], 512:D], ps[0:TT[i], 512:D]), f"y{i}")


_INS = ["x_prompt", "x_sample", "cache_ckv", "cache_kpe", "state_gla", "page_table", "meta_tokens", "norm_mix", "w_in",
        "w_gk", "b_gk", "gla_norm", "q_norm", "kv_norm", "w_uq", "w_ukv", "w_out", "norm_ffn", "w_gate", "w_up", "w_down",
        "norm_final"]
_OUTS = [(1, SEQ, D), (NB, 1, D), (1, 1, NP, KVL), (1, 1, NP, ROPE), (1, 1, GH, DK, DV), (1, NB, 1, KVL), (1, NB, 1, ROPE),
         (1, NB, GH, DK, DV)]


def kernel(**inputs):
    import concourse.bacc as bacc
    from concourse.bass_utils import run_bass_kernel_spmd

    nc = bacc.Bacc("TRN2", target_bir_lowering=False, num_devices=1)
    arrays, ins = {}, []
    shaped = dict(zip(("c_all", "c_masks", "c_pick"), constants()))
    for name in _INS + list(shaped):
        a = np.ascontiguousarray(inputs[name] if name in inputs else shaped[name])
        arrays[f"in_{name}"] = a
        ins.append(nc.dram_tensor(f"in_{name}", a.shape, mybir.dt.from_np(a.dtype), kind="ExternalInput").ap())
    outs = [nc.dram_tensor(f"out_{i}", s, F32, kind="ExternalOutput").ap() for i, s in enumerate(_OUTS)]
    hybrid_decode_kernel(nc, ins, outs)
    r = run_bass_kernel_spmd(nc, [arrays], core_ids=[0])
    return tuple(r.results[0][f"out_{i}"] for i in range(len(_OUTS)))
```

```python
from contextlib import ExitStack

import numpy as np

import concourse.bass as bass
from concourse import mybir

F32 = mybir.dt.float32
F32R = mybir.dt.float32r
I32 = mybir.dt.int32
U32 = mybir.dt.uint32
ALU = mybir.AluOpType
ACT = mybir.ActivationFunctionType
AX = mybir.AxisListType.X

P = 128
EPS = 1e-6
D = 1024
KD = D // P
NMETA = 16
SEQ = 512
NP = NMETA + SEQ
NB = 8
T = NP + NB
TH = T // 2
NT = 5
TPAD = NT * P
TT = [P, P, P, P, T - 4 * P]
PAST = 4096
PAGE = 128
NPAGES = PAST // PAGE
GH, DK, DV = 4, 64, 128
RANK = 16
MH, NOPE, ROPE = 4, 128, 64
HALF = ROPE // 2
QL, KVL = 384, 256
SCALE = float(NOPE + ROPE) ** -0.5
DFF = 2816
KF = DFF // P
C_Q, C_K, C_V, C_GR, C_G, C_CQ, C_CKV, C_KPE = 0, 256, 512, 1024, 1040, 1552, 1936, 2192
LEVELS = [64, 32, 16, 8, 4, 2, 1]
NL = len(LEVELS)
NG = P // 32
UNITS = 16
CHUNKS = NPAGES * PAGE // (P * UNITS)
NBLK = (KVL + ROPE) // 32

CC = {}
_at = 0
for _name, _n in (("ident", P), ("ones", P), ("ucum", P), ("swap", P), ("cosf", T), ("sinf", T), ("cosk", NT * ROPE),
                  ("sink", NT * ROPE), ("ucum4", 24), ("sell", 4), ("selo", 4), ("eps", 1), ("quart", 1), ("cap", P)):
    CC[_name] = (_at, _at + _n)
    _at += _n
NCONST = _at


def constants():
    c = np.zeros((P, NCONST), np.float32)

    def put(name, a):
        c[:, CC[name][0]:CC[name][1]] = a

    p = np.arange(P)
    put("ident", np.eye(P))
    put("ones", 1.0)
    put("ucum", (p[:, None] <= p[None, :]) / 16.0)
    last = np.zeros((P, 24))
    last[:16, :16] = np.triu(np.ones((16, 16))) / 16.0
    last[16:24, 16:] = np.eye(8) / 16.0
    put("ucum4", last)
    put("swap", np.eye(P)[p ^ HALF])
    pos = np.concatenate([np.arange(NP), np.full(TPAD - NP, PAST)]).astype(np.float32)
    inv = (10000.0 ** (-np.arange(HALF) / HALF)).astype(np.float32)
    ang = (pos[:, None] * inv[None, :]).astype(np.float32)
    cos, sin = np.cos(ang), np.sin(ang)
    cos2, sin2 = np.concatenate([cos, cos], 1), np.concatenate([-sin, sin], 1)
    put("cosf", np.concatenate([cos2, cos2], 1)[:T].T)
    put("sinf", np.concatenate([sin2, sin2], 1)[:T].T)
    put("cosk", cos2.reshape(NT, P, ROPE).transpose(1, 0, 2).reshape(P, -1))
    put("sink", sin2.reshape(NT, P, ROPE).transpose(1, 0, 2).reshape(P, -1))
    h = np.arange(4)
    put("sell", ((p[:, None] % 32 < 16) & (p[:, None] % 4 == h)).astype(np.float32))
    put("selo", ((p[:, None] % 32 >= 16) & (p[:, None] % 4 == h)).astype(np.float32))
    put("eps", EPS)
    put("quart", ((p % 4) * 2)[:, None])
    put("cap", np.where(p[None, :] <= p[:, None], 3e38, -3e38))
    masks = np.zeros((P, NL + 1, P), np.int32)
    for i, s in enumerate(LEVELS):
        same = p[:, None] // (2 * s) == p[None, :] // (2 * s)
        masks[:, i] = same & (p[:, None] % (2 * s) < s) & (p[None, :] % (2 * s) >= s)
    masks[:, NL] = np.eye(P)
    pick = np.zeros((24, NB, P), np.float32)
    for b in range(NB):
        pick[16 + b, b] = 1.0
    return c, masks.reshape(P, -1), pick.reshape(24, -1)


def plan():
    n = [f"xT{k}" for k in range(KD)]
    n += [f"cq{m}" for m in range(3)]
    n += [f"tok{i}" for i in range(NT)] + ["ssq"]
    n += [f"q{m}" for m in range(2)] + [f"k{m}" for m in range(2)]
    n += [f"v{i}" for i in range(NT)]
    n += [f"g{m}" for m in range(4)]
    n += [f"ck{j}" for j in range(3)] + ["gr"]
    for hh in range(2):
        n += [f"qn{2 * hh}", f"qn{2 * hh + 1}", f"qp{hh}"]
    n += ["sw0", "sw1"]
    n += [f"kn{h}" for h in range(4)] + [f"vm{i}" for i in range(NT)] + ["wuk0", "wuk1", "qlat", "snew"]
    for u in range(NT * MH + 2):
        n += [f"S{u}"] if u < NT * MH else []
        n += [f"PT{u - 1}"] if 1 <= u <= NT * MH else []
        n += [f"OM{u - 2}"] if u >= 2 else []
    while len(n) % 4:
        n.append(f"-{len(n)}")
    n += [f"cache{i}" if i % 2 == 0 or i < 2 * NB else f"-cache{i}" for i in range(4 * NB)]
    n += ["mt", "mx", "den", "rb", "osum", "ol", "omd"]
    n += [f"lg{i}" for i in range(NT)] + [f"b{c}" for c in range(NT)]
    for lv in range(NL + 1):
        for c in range(NT):
            if c < 4 or lv == NL or LEVELS[lv] <= 8:
                n += [f"G{lv}.{c}"]
        n += [f"vb{lv}"]
    n += ["os"]
    for c in range(NT + 1):
        n += [f"kt{c}", f"s{c}"] if c < NT else []
        n += [f"o{c - 1}"] if c else []
    n += [f"ssg{h}" for h in range(4)]
    n += [f"wo{m}" for m in range(4)] + [f"hT{m}" for m in range(4)]
    for m in range(4, KD):
        n += [f"wo{m}", f"hT{m}"]
    n += ["ssf"]
    while len(n) % 4:
        n.append(f"-{len(n)}")
    n += [f"ffn{i}" for i in range(2 * KF)]
    n += [f"dn{i}" for i in range(KD)]
    n += ["ssy"] + [f"y{i}" for i in range(NT)]
    return {name: i for i, name in enumerate(n)}


PLAN = plan()
IDLE = {v for k, v in PLAN.items() if k[0] == "-"}

BLOCKS = [[("w_in", 0, KD, C_CQ, 256)], [("w_in", 0, KD, C_CQ + 256, 128)], [("w_in", 0, KD, C_CKV, 256)],
          [("w_in", 0, KD, C_KPE, 64), ("w_in", 0, KD, C_GR, 16)],
          [("w_in", 0, KD, C_Q, 256)], [("w_in", 0, KD, C_K, 256)],
          [("w_in", 0, KD, C_V, 256)], [("w_in", 0, KD, C_V + 256, 256)],
          [("w_in", 0, KD, C_G, 256)], [("w_in", 0, KD, C_G + 256, 256)],
          *[[("w_uq", 0, 3, 384 * x + c, w) for c, w in ((0, 128), (192, 128), (128, 64), (320, 64))] for x in range(2)],
          [("w_ukv", 0, 2, 0, 1024)]]
B_UQ, B_UKV, B_OUT = 10, 12, 13
BLOCKS += [[("w_out", 0, KD, 256 * m, 256)] for m in range(4)]
B_FFN = len(BLOCKS)
B_DOWN = B_FFN + 2 * (DFF // 256)
DPARTS = [(0, 8), (8, 8), (16, 6)]


SIGNALS = ["E_done", "Qall_done", "ckhi_done", "cklo_done", "diff_done", "dn_part", "eb_done", "fe_done", "ge_done",
           "hhi_done", "hlo_done", "kt_done", "lgt_done", "mixhi_done", "mixlo_done", "msk_loaded", "nhi_done", "nlo_done", "nm_done", "m_done", "mc_done", "ml_done", "nmax_done", "og_done",
           "omdhi_done", "omhi_done", "mexp_done", "d2_done", "lw_done", "rexp_done", "selw_done", "pad_done", "pick_loaded", "pn_done", "prod_done",
           "ps_done", "ps_clear", "pt_done", "pti_loaded", "pv_done", "qc_done", "qk_done", "qn_done", "qnhi_done", "qnlo_done",
           "qpe_done", "rk_done", "rs_done", "sc_done", "exp_done", "sqf_done", "sqg_done", "sqs_done", "sqy_done", "stat_clear",
           "states_loaded", "tf_done", "wexp_done", "wuv_kept", "x2_loaded", "decay_done", "gated", "xhi_done",
           "xn_done", "yT_done", "y_half", "y_out0", "y_out1"]
SIGNALS += [f"kc_loaded{i}" for i in range(4)]
LAST = {0: "cq1", 1: "cq2", 2: "tok4", 3: "tok4", 4: "q1", 5: "k1", 6: "v4", 7: "v4", 8: "g1", 9: "g3", 10: "qp0",
        11: "qp1", 12: "vm4", 13: "wo1", 14: "wo3", 15: "wo5", 16: "wo7", 17: "ffn1", 18: "ffn3"}

def reads(n):
    return sum(m not in IDLE for m in range(n % 4, n, 4))


def last_g(c):
    return f"G{NL}.{c}"


def last_of_level(lv):
    return f"G{lv}.{4 if lv == NL or LEVELS[lv] <= 8 else 3}"


def fills(name):
    return sum(v <= PLAN[name] and k[0] != "-" and not k.startswith("cache") for k, v in PLAN.items())


LOADS = []
for _n in range(B_DOWN + 12):
    _k = len(BLOCKS[_n]) if _n < B_FFN else 1
    LOADS.append(_k + (LOADS[_n - 2] if _n >= 2 else 0))


def hybrid_decode_kernel(nc, ins, outs):
    (x_prompt, x_sample, cache_ckv, cache_kpe, state_gla, page_table, meta_tokens, norm_mix, w_in, w_gk, b_gk,
     gla_norm, q_norm, kv_norm, w_uq, w_ukv, w_out, norm_ffn, w_gate, w_up, w_down, norm_final,
     c_all, c_masks, c_pick) = ins
    y_prompt, y_sample, ckv_p, kpe_p, gla_p, ckv_s, kpe_s, gla_s = outs
    weights = {"w_in": w_in[0], "w_uq": w_uq[0], "w_ukv": w_ukv[0], "w_out": w_out[0], "w_gate": w_gate[0],
               "w_up": w_up[0], "w_down": w_down[0]}
    with ExitStack() as ctx:
        top = [0]
        arena_bytes = 212000
        nc_base = nc.sbuf_base
        ctx.enter_context(nc.sbuf_tensor("arena", [P, arena_bytes // 4], F32))
        arena_at = -(-nc_base // 32) * 32

        def sb(name, shape, dt=F32, at=None):
            n = 4
            for d in shape[1:]:
                n *= d
            off = top[0] if at is None else at
            if at is None:
                top[0] = -(-(off + n) // 32) * 32
            assert off + n <= arena_bytes, (name, off, n)
            return nc.alloc_sbuf_tensor_at(name, shape, dt, offset=arena_at + off)

        xhi = sb("xhi", [P, KD, TPAD], F32R)
        xlo = sb("xlo", [P, KD, TPAD], F32R)
        wraw = [sb(f"wraw{i}", [P, 2048]) for i in range(2)]
        whi_at = top[0]
        whi = [sb(f"whi{i}", [P, 2048], F32R) for i in range(2)]
        wlo = [sb(f"wlo{i}", [P, 2048], F32R) for i in range(2)]
        cst_at = top[0]
        cst = sb("cst", [P, NCONST])
        nrm = sb("nrm", [P, 3 * KD + 4])
        keep = top[0]
        hT = sb("hT", [P, KD, T])
        gq = sb("gq", [P, 2, T], at=keep)
        gk = sb("gk", [P, 2, T], at=keep + 8 * T)
        gT = sb("gT", [P, 4, T], at=keep + 16 * T)
        hid_at = top[0]
        stat = sb("stat", [P, 64])
        vtok = sb("vtok", [P, NT, 512])
        grT = sb("grT", [32, T])
        x2_at = top[0]
        Qall = sb("Qall", [P, NB, NBLK * 32])
        wuv = sb("wuv", [P, 2, 4, 128])
        cks = sb("cks", [P, 2, NB])
        qlT = sb("qlT", [P, 2, 4, NB])
        fin_at = top[0]
        fin = sb("fin", [P, 640])
        el_at = top[0]
        el = sb("el", [P, 2, NT])
        eb = sb("eb", [P, 2, NB])
        wgk = sb("wgk", [32, 256])
        W0 = top[0]
        X = sb("X", [P, NT, D], at=W0)
        cq = sb("cq", [P, 3, T], at=W0)
        knT = sb("knT", [P, 4, T], at=W0)
        a = W0 + 16 * T
        qnhi = sb("qnhi", [P, 3, T], F32R, at=a)
        qnlo = sb("qnlo", [P, 3, T], F32R, at=a + 12 * T)
        vm = sb("vm", [P, NT, 512], at=a)
        a += 24 * T
        ctok = sb("ctok", [P, NT, 384], at=a)
        a += NT * 384 * 4
        kpT = sb("kpT", [P, T], at=a)
        a += 4 * T
        ckhi = sb("ckhi", [P, 2, TPAD], F32R, at=a)
        cklo = sb("cklo", [P, 2, TPAD], F32R, at=a + 8 * TPAD)
        pr = [sb(f"pr{i}", [P, NP], at=a + 4 * NP * i) for i in range(2)]
        pt = [sb(f"pt{i}", [P, NT, P], at=a + 8 * NP + 4 * NT * P * i) for i in range(2)]
        a += 16 * TPAD
        qnT = sb("qnT", [P, 4, T], at=a)
        a += 16 * T
        qpe = sb("qpe", [P, 2, T], at=a)
        a += 8 * T
        sqs = sb("sqs", [P, 3, T], at=a - 24 * T)
        rsb = sb("rsb", [P, T], at=a)
        kvn = sb("kvn", [P, KVL], at=a + 4 * T)
        a += 4 * T + 4 * KVL
        rp = sb("rp", [P, 2, ROPE], at=a)
        grt = sb("grt", [P, NT, RANK], at=a + 8 * ROPE)
        prod = sb("prod", [P, 3, 4, NB], at=a + 832)
        scr = sb("scr", [P, D], at=a + 1216)
        wukT = sb("wukT", [P, 4, 256], at=a + 1216)
        KC = [sb(f"KC{i}", [P, UNITS * KVL], at=whi_at + 16384 * i if i < 2 else W0 + 16384 * (i - 2)) for i in range(4)]
        KP = [sb(f"KP{i}", [P, UNITS * ROPE], at=4 * KD * TPAD + 4096 * i if i < 2 else W0 + 32768 + 4096 * (i - 2))
              for i in range(4)]
        b0 = W0 + 40960
        KT = sb("KT", [P, UNITS, 8, 32], at=b0)
        KTp = sb("KTp", [P, UNITS, 2, 32], at=b0 + 16384)
        assert b0 + 20480 <= arena_bytes
        Oall = sb("Oall", [P, NB, KVL], at=0)
        b1 = cst_at + 4 * CC["cosf"][0]
        assert 6400 <= 8 * T + 8 * NT * ROPE
        PS = [sb(f"PS{i}", [P, UNITS, 32], at=b1 + 2048 * i) for i in range(2)]
        Pc = sb("Pc", [P, P], at=b1 + 4096)
        Pt = sb("Pt", [P, 4, 32], at=b1 + 4608)
        Qc = [sb("Qc0", [P, NBLK * 32], at=b1 + 5120), sb("Qc1", [P, NBLK * 32], at=4 * NB * KVL)]
        sn8, mx8, w8, den8, r8, wn8 = (fin[0:NB, 4 * i:4 * i + 4] for i in range(6))
        mexp, rexp, wx8 = fin[0:NB, 24:152], fin[0:NB, 324:452], fin[0:NB, 152:184]
        Mc, Lc, Wc = (fin[:, o:o + 16].rearrange("p (e b) -> p e b", e=2) for o in (184, 200, 216))
        wvb, ML, mc = fin[:, 232:264], fin[:, 264:312], fin[:, 312:324]
        idx = sb("idx", [P, NB, CHUNKS], I32, at=fin_at + 4 * 456)
        pti = sb("pti", [P, NB], I32, at=fin_at + 4 * 472)
        icur = [sb(f"icur{i}", [P, 1], I32, at=fin_at + 32 * (60 + i)) for i in range(4)]
        selw = sb("selw", [P, NB, 32], at=W0)
        osb = sb("osb", [P, 2, KVL], at=W0 + 1024)
        olat = sb("olat", [P, 2, NB * 4], at=W0 + 3072)
        otmp = sb("otmp", [P, 2, NB * 4], at=W0 + 3328)
        a = W0
        lgs = sb("lgs", [P, NT, 256], at=a)
        a += NT * 256 * 4
        bT = sb("bT", [P, 2, T], at=a)
        a += 8 * T
        Ee = [sb(f"Ee{i}", [P, 2, NP], at=a + 8 * NP * i) for i in range(2)]
        qt = [sb(f"qt{i}", [P, 2, NP], at=a + 8 * NP * (2, 4)[i]) for i in range(2)]
        kt = [sb(f"kt{i}", [P, 2, NP], at=a + 8 * NP * (5, 3)[i]) for i in range(2)]
        oT = sb("oT", [P, 4, T], at=a)
        lgt = sb("lgt", [P, 256], at=a)
        a += 48 * NP
        at_at = a
        AT = sb("AT", [P, NT, 4, P], at=a)
        a += NT * 4 * P * 4
        msk = sb("msk", [P, NL + 1, P], I32, at=a)
        a += 4 * P * (NL + 1)
        Sst = [sb("Sst0", [P, 2, P], at=a), sb("Sst1", [P, 2, P], at=cst_at + 4 * CC["cosf"][0] + 4096)]
        a += 8 * P
        states = sb("states", [P, NB, 2, P], at=a)
        a += 8 * NB * P
        ktok = sb("ktok", [P, 2, P], at=a)
        a += 8 * P
        pick = sb("pick", [24, NB, P], at=cst_at + 4 * CC["cosf"][0])
        X2 = [sb(f"X2_{i}", [P, D], at=x2_at + 4 * D * i if i < 4 else a) for i in range(NT)]
        assert x2_at + 16 * D <= el_at
        sqg = [sb(f"sqg{i}", [P, T], at=W0 + 4 * T * i) for i in range(4)]
        rsg = [sb(f"rsg{i}", [P, T], at=at_at + 4 * T * i) for i in range(4)]
        sqf = sb("sqf", [P, KD, T], at=W0 + 20480)
        rsf = sb("rsf", [P, T], at=W0)
        tf = [sb(f"tf{i}", [P, T], at=W0 + 4 * T * (1 + i)) for i in range(2)]
        hhi = sb("hhi", [P, KF, T], F32R, at=hid_at)
        hlo = sb("hlo", [P, KF, T], F32R, at=hid_at + 4 * KF * T)
        f0 = cst_at + 4 * CC["cosf"][0]
        fe = [sb(f"fe{i}", [P, T], at=f0 + 4 * T * i) for i in range(2)]
        sqy = sb("sqy", [P, KD, T], at=0)
        yT = sb("yT", [P, KD, T], at=4 * KD * TPAD)
        rsy = sb("rsy", [P, T], at=hid_at)
        ysb = [sb(f"ysb{i}", [P, D], at=hid_at + 4 * T + 4 * D * i) for i in range(2)]

        pairs = [ctx.enter_context(nc.psum_tensor(f"pair{i}", [P, 1024], F32)) for i in range(4)]

        def sem(name):
            return ctx.enter_context(nc.semaphore(name))

        pe_done = sem("pe_done")
        pair_free = [sem(f"pair_free{i}") for i in range(4)]
        w_loaded = [sem(f"w_loaded{i}") for i in range(2)]
        w_hi, w_lo = sem("w_hi"), sem("w_lo")
        x_loaded = [sem(f"x_loaded{i}") for i in range(NT)]
        c_loaded, n_loaded, small_loaded = sem("c_loaded"), sem("n_loaded"), sem("small_loaded")
        out_done = sem("out_done")
        dve_chain, act_chain, pool_chain = sem("dve_chain"), sem("act_chain"), sem("pool_chain")
        signals = {name: sem(name) for name in SIGNALS}

        def S(name):
            return signals[name]

        block = ctx.enter_context(nc.Block())

        def C(name, rows=P):
            return cst[0:rows, CC[name][0]:CC[name][1]]

        ident, ones = C("ident"), C("ones")

        def halves(ap):
            return ap[:, :].rearrange("p (a t) -> p a t", a=2)[:, :, 0:TH]

        def split2(ap):
            return ap.rearrange("p (a t) -> p a t", a=2)

        def block_size(n):
            return BLOCKS[n][0][2] * sum(p[4] for p in BLOCKS[n]) if n < B_FFN else 256 * KD

        def view(bufs, n, k=None):
            k = k or BLOCKS[n][0][2]
            w = sum(p[4] for p in BLOCKS[n]) if n < B_FFN else 256
            return bufs[n % 2][:, 0:k * w].rearrange("p (k n) -> p k n", n=w)

        @block.sync
        def _(sp):
            sp.dma_start(cst[:, :], c_all).then_inc(c_loaded, 16)

            def load_x(dst, sems):
                for i in range(NT):
                    if i == 0:
                        sp.dma_start(dst[0][0:NMETA, :], meta_tokens).then_inc(sems[0], 16)
                        sp.dma_start(dst[0][NMETA:P, :], x_prompt[0, 0:P - NMETA, :]).then_inc(sems[0], 16)
                    elif i < 4:
                        sp.dma_start(dst[i], x_prompt[0, P * i - NMETA:P * (i + 1) - NMETA, :]).then_inc(sems[i], 16)
                    else:
                        sp.dma_start(dst[4][0:NMETA, :], x_prompt[0, SEQ - NMETA:SEQ, :]).then_inc(sems[4], 16)
                        sp.dma_start(dst[4][NMETA:NMETA + NB, :], x_sample[:, 0, :]).then_inc(sems[4], 16)

            load_x([X[:, i, :] for i in range(NT)], x_loaded)

            def load_block(n):
                if n >= 2:
                    sp.wait_ge(w_lo, n - 1)
                if n == B_UKV + 2:
                    sp.wait_ge(pe_done, fills("wuk1"))
                    sp.wait_ge(S("wuv_kept"), 1)
                c0 = 0
                w = sum(p[4] for p in BLOCKS[n])
                k = BLOCKS[n][0][2]
                for name, k0, kk, col, cols in BLOCKS[n]:
                    dst = wraw[n % 2][:, 0:k * w].rearrange("p (k n) -> p k n", n=w)[:, :, c0:c0 + cols]
                    src = weights[name][P * k0:P * (k0 + kk), col:col + cols].rearrange("(k p) n -> p k n", p=P)
                    sp.dma_start(dst, src).then_inc(w_loaded[n % 2], 16)
                    c0 += cols

            for n in range(B_UKV):
                load_block(n)
                if n == 7:
                    for i in range(NT):
                        sp.wait_ge(pair_free[PLAN[f"tok{i}"] % 4], reads(PLAN[f"tok{i}"]) + 1)
                        r = min(TT[i], NP - P * i)
                        sp.dma_start(ckv_p[0, 0, P * i:P * i + r, :], ctok[0:r, i, 0:KVL]).then_inc(out_done, 16)
                        sp.dma_start(kpe_p[0, 0, P * i:P * i + r, :], ctok[0:r, i, KVL:KVL + ROPE]).then_inc(out_done, 16)
                        if i == NT - 1:
                            sp.dma_start(ckv_s[0, :, 0, :], ctok[r:r + NB, i, 0:KVL]).then_inc(out_done, 16)
                            sp.dma_start(kpe_s[0, :, 0, :], ctok[r:r + NB, i, KVL:KVL + ROPE]).then_inc(out_done, 16)
            load_block(B_UKV)
            load_block(B_OUT)
            load_block(B_OUT + 1)
            sp.wait_ge(pair_free[PLAN["omd"] % 4], reads(PLAN["omd"]) + 1)
            sp.wait_ge(out_done, 16 * 12)
            sp.dma_start(msk[:, :, :].rearrange("p a b -> p (a b)"), c_masks).then_inc(S("msk_loaded"), 16)
            for b in range(NB):
                for pp in range(2):
                    sp.dma_start(states[:, b, pp, :], state_gla[0, b, 2 * pp:2 * pp + 2].rearrange("a k v -> (a k) v")
                                 ).then_inc(S("states_loaded"), 16)
            sp.dma_start(pick[:, :, :].rearrange("p a b -> p (a b)"), c_pick).then_inc(S("pick_loaded"), 16)
            load_x([t[:, :] for t in X2], [S("x2_loaded")] * NT)
            sp.wait_ge(pair_free[PLAN["vb7"] % 4], reads(PLAN["vb7"]) + 1)
            for b in range(NB):
                for pp in range(2):
                    sp.dma_start(gla_s[0, b, 2 * pp:2 * pp + 2].rearrange("a k v -> (a k) v"), states[:, b, pp, :]
                                 ).then_inc(out_done, 16)
            sp.wait_ge(pair_free[PLAN["s4"] % 4], reads(PLAN["s4"]) + 1)
            for pp in range(2):
                sp.dma_start(gla_p[0, 0, 2 * pp:2 * pp + 2].rearrange("a k v -> (a k) v"), Sst[(NT - 1) % 2][:, pp, :]).then_inc(out_done, 16)
            load_block(B_OUT + 2)
            load_block(B_OUT + 3)
            with sp.Fori(0, DFF // 256) as j:
                for s, name in ((0, "w_gate"), (1, "w_up")):
                    slot = (B_FFN + s) % 2
                    sp.wait_ge(w_lo, (B_FFN + s - 1) + 2 * j)
                    src = weights[name].rearrange("(k p) n -> p k n", p=P)[:, :, bass.ds(256 * j, 256)]
                    sp.dma_start(wraw[slot][:, :].rearrange("p (k n) -> p k n", n=256), src).then_inc(w_loaded[slot], 16)
            with sp.Fori(0, 2) as j:
                for cb in range(2):
                    for q, (k0, kk) in enumerate(DPARTS):
                        n = B_DOWN + 3 * cb + q
                        sp.wait_ge(w_lo, (n - 1) + 6 * j)
                        src = weights["w_down"][P * k0:P * (k0 + kk), :].rearrange("(k p) n -> p k n", p=P)[:, :, bass.ds(512 * j + 256 * cb, 256)]
                        sp.dma_start(wraw[n % 2][:, 0:256 * kk].rearrange("p (k n) -> p k n", n=256), src).then_inc(w_loaded[n % 2], 16)
            for i in range(NT):
                sp.wait_ge(pair_free[PLAN[f"y{i}"] % 4], reads(PLAN[f"y{i}"]) + 1)
                y = ysb[i % 2]
                if i == 0:
                    sp.dma_start(y_prompt[0, 0:P - NMETA, :], y[NMETA:P, :]).then_inc(S(f"y_out{i % 2}"), 16)
                elif i < 4:
                    sp.dma_start(y_prompt[0, P * i - NMETA:P * (i + 1) - NMETA, :], y[:, :]).then_inc(S(f"y_out{i % 2}"), 16)
                else:
                    sp.dma_start(y_prompt[0, SEQ - NMETA:SEQ, :], y[0:NMETA, :]).then_inc(S(f"y_out{i % 2}"), 16)
                    sp.dma_start(y_sample[:, 0, :], y[NMETA:NMETA + NB, :]).then_inc(S(f"y_out{i % 2}"), 16)
            sp.wait_ge(S("y_out0"), 16 * 4)
            sp.wait_ge(S("y_out1"), 16 * 2)
            sp.wait_ge(out_done, 16 * (12 + 2 + 16))

        @block.gpsimd
        def _(pool):
            g = nc.gpsimd
            chain = [0]

            def link(ins):
                chain[0] += 1
                ins.then_inc(pool_chain, 1)
                pool.wait_ge(pool_chain, chain[0])

            with nc.allow_non_contiguous_dma("vectors by feature"):
                for j, v in enumerate((norm_mix[0], norm_ffn[0], norm_final)):
                    pool.dma_start(nrm[:, KD * j:KD * j + KD], v.rearrange("(k p) -> p k", p=P)).then_inc(n_loaded, 16)
                pool.dma_start(nrm[:, 3 * KD:3 * KD + 3], q_norm[0].rearrange("(k p) -> p k", p=P)).then_inc(n_loaded, 16)
                pool.dma_start(nrm[:, 3 * KD + 3:3 * KD + 4], gla_norm[0].rearrange("(k p) -> p k", p=P)).then_inc(n_loaded, 16)
                link(g.memset(wgk[:, :], 0.0))
                pool.dma_start(wgk[0:RANK, :], w_gk[0]).then_inc(small_loaded, 16)
                pool.dma_start(wgk[RANK:RANK + 1, :], b_gk).then_inc(small_loaded, 16)
                pool.dma_start(kvn[:, :], kv_norm[0].partition_broadcast(P)).then_inc(small_loaded, 16)
            g.memset(xhi[:, :, T:TPAD].bitcast(F32), 0.0).then_inc(S("pad_done"), 1)
            g.memset(xlo[:, :, T:TPAD].bitcast(F32), 0.0).then_inc(S("pad_done"), 1)
            g.memset(grT[:, :], 1.0).then_inc(S("pad_done"), 1)
            link(g.memset(Qall[:, :, :], 0.0))
            pool.wait_ge(w_loaded[B_UKV % 2], 16 * LOADS[B_UKV])
            ins = g.tensor_copy(wuv[:, :, :, :], wraw[B_UKV % 2][:, :].rearrange("p (k h n) -> p k h n", k=2, h=4)[:, :, :, NOPE:256])
            ins.then_inc(S("wuv_kept"), 1)
            pool.wait_ge(S("wuv_kept"), 1)
            pool.wait_ge(pair_free[PLAN["qlat"] % 4], reads(PLAN["qlat"]) + 1)
            pool.wait_ge(S("qpe_done"), 1)
            for q in range(NG):
                for gg in range(NG):
                    for dup in range(2):
                        at = 16 * dup + 4 * gg
                        for rh in range(2):
                            c = 4 * rh + q
                            dst = Qall[32 * gg:32 * gg + 32, :, 32 * c + at:32 * c + at + 4]
                            src = qlT[32 * q:32 * q + 32, rh, :, :].rearrange("p h b -> p b h")
                            link(g.tensor_copy(dst, src))
            for aa in range(2):
                for e in range(2):
                    for gg in range(NG):
                        for dup in range(2):
                            at = 32 * (8 + e) + 16 * dup + 4 * gg + aa
                            dst = Qall[32 * gg:32 * gg + 32, :, at:at + 3:2]
                            src = qpe[64 * aa + 32 * e:64 * aa + 32 * e + 32, :, NP:T].rearrange("p q b -> p b q")
                            ins = g.tensor_copy(dst, src)
                            if (aa, e, gg, dup) < (1, 1, NG - 1, 1):
                                link(ins)
            ins.then_inc(S("Qall_done"), 1)
            pool.wait_ge(S("Qall_done"), 1)
            with nc.allow_non_contiguous_dma("page table"):
                for q in range(4):
                    pool.dma_start(pti[q:P:4, :], page_table.rearrange("b n -> n b")).then_inc(S("pti_loaded"), 16)
            g.memset(PS[0][:, :, :], 0.0).then_inc(S("ps_clear"), 1)
            g.memset(PS[1][:, :, :], 0.0).then_inc(S("ps_clear"), 1)
            pool.wait_ge(S("pti_loaded"), 64)
            link(g.tensor_scalar(idx[:, :, 0], pti[:, :], 8.0, C("quart"), ALU.mult, ALU.add))
            link(g.tensor_scalar(idx[:, :, 1], idx[:, :, 0], 1.0, 0.0, ALU.add, ALU.add))
            ckv_rows = cache_ckv[0].rearrange("n (s k) r -> (n s) (k r)", k=UNITS)
            kpe_rows = cache_kpe[0].rearrange("n (s k) r -> (n s) (k r)", k=UNITS)
            for n in range(CHUNKS * NB):
                x = n % 4
                if n == 0:
                    pool.wait_ge(pe_done, fills("vm4"))
                if n == 2:
                    pool.wait_ge(pair_free[PLAN["OM19"] % 4], reads(PLAN["OM19"]) + 1)
                    pool.wait_ge(out_done, 16 * 12)
                if n >= 4:
                    pool.wait_ge(S("pv_done"), n - 3)
                    pool.wait_ge(S("kt_done"), n - 3)
                link(g.tensor_copy(icur[x][:, :], idx[:, n // 2, n % 2:n % 2 + 1]))
                g.indirect_dma_start(KC[x][:, :], None, ckv_rows, bass.IndirectOffsetOnAxis(icur[x][:, 0:1], 0)).then_inc(S(f"kc_loaded{x}"), 16)
                g.indirect_dma_start(KP[x][:, :], None, kpe_rows, bass.IndirectOffsetOnAxis(icur[x][:, 0:1], 0)).then_inc(S(f"kc_loaded{x}"), 16)

        @block.tensor
        def _(pe):
            mm = nc.tensor.matmul

            def take(name):
                n = PLAN[name]
                if n >= 4:
                    pe.wait_ge(pair_free[n % 4], reads(n))
                return pairs[n % 4]

            def evacuated(name):
                pe.wait_ge(pair_free[PLAN[name] % 4], reads(PLAN[name]) + 1)

            def use(n):
                pe.wait_ge(w_lo, n + 1)

            def done(ins):
                ins.then_inc(pe_done, 1)

            def dense(ps, h, l, wcols, k_of, hi, lo, first=True, last=True):
                ins = None
                for half in range(2):
                    out = ps[:, 512 * half:512 * half + TH]
                    tok = slice(TH * half, TH * half + TH)
                    for j, kx in enumerate(k_of):
                        mm(out, wcols(h, j), hi[:, kx, tok], start=first and j == 0, stop=False)
                        mm(out, wcols(h, j), lo[:, kx, tok], start=False, stop=False)
                        ins = mm(out, wcols(l, j), hi[:, kx, tok], start=False, stop=last and j == len(k_of) - 1)
                return ins

            def cols(c):
                return lambda ap, j: ap[:, j, c:c + P]

            def layer(name, n, c, K, hi, lo):
                done(dense(take(name), view(whi, n), view(wlo, n), cols(c), list(range(K)), hi, lo))

            def by_token(out, i, n, K, wcols, hi, lo):
                h, l = view(whi, n), view(wlo, n)
                tok = slice(P * i, P * i + P)
                ins = None
                for j in range(K):
                    mm(out, hi[:, j, tok], wcols(h, j), start=j == 0, stop=False)
                    mm(out, lo[:, j, tok], wcols(h, j), start=False, stop=False)
                    ins = mm(out, hi[:, j, tok], wcols(l, j), start=False, stop=j == K - 1)
                return ins

            def ones_sum(ps, src):
                ins = None
                for half in range(2):
                    for k, s in enumerate(src):
                        ins = mm(ps[:, 512 * half:512 * half + TH], ones, s[:, TH * half:TH * half + TH],
                                 start=k == 0, stop=k == len(src) - 1)
                return ins

            pe.wait_ge(c_loaded, 16)
            pe.wait_ge(S("xn_done"), NT)
            for k in range(KD):
                ps = take(f"xT{k}")
                for i in range(NT):
                    ins = nc.tensor.transpose(ps[:, P * i:P * i + TT[i]], X[0:TT[i], i, P * k:P * k + P],
                                              C("ident", TT[i])[:, 0:TT[i]])
                done(ins)
            pe.wait_ge(S("pad_done"), 3)
            for k in range(4, KD):
                evacuated(f"xT{k}")
            use(0)
            layer("cq0", 0, 0, KD, xhi, xlo)
            layer("cq1", 0, P, KD, xhi, xlo)
            use(1)
            layer("cq2", 1, 0, KD, xhi, xlo)
            use(3)
            for i in range(NT):
                ps = take(f"tok{i}")
                by_token(ps[:, 0:256], i, 2, KD, lambda a, j: a[:, j, :], xhi, xlo)
                done(by_token(ps[:, 256:336], i, 3, KD, lambda a, j: a[:, j, :], xhi, xlo))
            pe.wait_ge(S("sqs_done"), 3)
            done(ones_sum(take("ssq"), [sqs[:, k, :] for k in range(3)]))
            for n, name in ((4, "q"), (5, "k")):
                use(n)
                for m in range(2):
                    layer(f"{name}{m}", n, P * m, KD, xhi, xlo)
            use(7)
            for i in range(NT):
                ps = take(f"v{i}")
                by_token(ps[:, 0:256], i, 6, KD, lambda a, j: a[:, j, :], xhi, xlo)
                done(by_token(ps[:, 256:512], i, 7, KD, lambda a, j: a[:, j, :], xhi, xlo))
            for m in range(4):
                if m % 2 == 0:
                    use(8 + m // 2)
                layer(f"g{m}", 8 + m // 2, P * (m % 2), KD, xhi, xlo)
            for j in range(3):
                ps = take(f"ck{j}")
                for i in range(NT):
                    ins = nc.tensor.transpose(ps[:, P * i:P * i + TT[i]], ctok[0:TT[i], i, P * j:P * j + P],
                                              C("ident", TT[i])[:, 0:TT[i]])
                done(ins)
            ps = take("gr")
            for i in range(NT):
                ins = mm(ps[0:RANK, P * i:P * i + TT[i]], grt[0:TT[i], i, :], C("ident", TT[i])[:, 0:TT[i]], start=True, stop=True)
            done(ins)
            pe.wait_ge(S("qnlo_done"), 1)
            for hh in range(2):
                n = B_UQ + hh
                use(n)
                for x in range(2):
                    layer(f"qn{2 * hh + x}", n, P * x, 3, qnhi, qnlo)
                done(dense(take(f"qp{hh}"), view(whi, n), view(wlo, n), cols(2 * P), list(range(3)), qnhi, qnlo))
            for hh in range(2):
                ps = take(f"sw{hh}")
                evacuated(f"qp{hh}")
                for half in range(2):
                    ins = mm(ps[:, 512 * half:512 * half + TH], C("swap"), qpe[:, hh, TH * half:TH * half + TH], start=True, stop=True)
                done(ins)
            use(B_UKV)
            pe.wait_ge(S("cklo_done"), 2)
            for h in range(MH):
                layer(f"kn{h}", B_UKV, 256 * h, 2, ckhi, cklo)
            for i in range(NT):
                ps = take(f"vm{i}")
                done(by_token(ps[:, 0:512].rearrange("p (h v) -> p h v", h=4), i, B_UKV, 2,
                              lambda a, j: a[:, j, :].rearrange("p (h c) -> p h c", h=4)[:, :, NOPE:256], ckhi, cklo))
            raw = wraw[B_UKV % 2][:, :].rearrange("p (k h c) -> p k h c", k=2, h=4)
            for x in range(2):
                ps = take(f"wuk{x}")
                for y in range(2):
                    for rh in range(2):
                        o = P * (2 * y + rh)
                        ins = nc.tensor.transpose(ps[:, o:o + P], raw[:, rh, 2 * x + y, 0:NOPE], ident)
                done(ins)
            ps = take("qlat")
            evacuated("qn3")
            evacuated("wuk1")
            for rh in range(2):
                for h in range(4):
                    o = 32 * rh + 8 * h
                    ins = mm(ps[:, o:o + 8], wukT[:, h, P * rh:P * rh + P], qnT[:, h, NP:T], start=True, stop=True)
            done(ins)
            ps = take("snew")
            pe.wait_ge(S("prod_done"), 1)
            for h in range(4):
                for x in range(3):
                    ins = mm(ps[0:NB, h:h + 1], prod[:, x, h, :], ones[:, 0:1], start=x == 0, stop=x == 2)
            done(ins)
            U = NT * MH
            for u in range(U + 2):
                if u < U:
                    qb, h = divmod(u, MH)
                    a, q0, nq = h % 2, P * qb, min(P, NP - P * qb)
                    nk = min(q0 + P, NP)
                    ps = take(f"S{u}")
                    for k0, k1 in ((0, min(nk, 512)), (512, nk)):
                        if k1 > k0:
                            mm(ps[0:nq, k0:k1], qnT[:, h, q0:q0 + nq], knT[:, h, k0:k1], start=True, stop=False)
                            ins = mm(ps[0:nq, k0:k1], qpe[64 * a:64 * a + 64, h // 2, q0:q0 + nq], kpT[64 * a:64 * a + 64, k0:k1],
                                     start=False, stop=True)
                    done(ins)
                if 1 <= u <= U:
                    v = u - 1
                    qb, h = divmod(v, MH)
                    nq = min(P, NP - P * qb)
                    ps = take(f"PT{v}")
                    pe.wait_ge(S("pn_done"), v + 1)
                    for kb in range(min(qb + 1, 4)):
                        ins = nc.tensor.transpose(ps[:, P * kb:P * kb + nq], pr[v % 2][0:nq, P * kb:P * kb + P], C("ident", nq)[:, 0:nq])
                    if qb == 4:
                        ins = mm(ps[0:16, 512:528], pr[v % 2][0:16, 512:528], C("ident", 16)[:, 0:16], start=True, stop=True)
                    done(ins)
                if u >= 2:
                    v = u - 2
                    qb, h = divmod(v, MH)
                    nq = min(P, NP - P * qb)
                    ps = take(f"OM{v}")
                    evacuated(f"PT{v}")
                    for kb in range(qb + 1):
                        nk = min(P, NP - P * kb)
                        ins = mm(ps[:, 0:nq], vm[0:nk, kb, P * h:P * h + P], pt[v % 2][0:nk, kb, 0:nq], start=kb == 0, stop=kb == qb)
                    done(ins)
            base = PLAN["cache0"]

            def cache_scores(j, x):
                p = 2 * (x % 2)
                pe.wait_ge(S("kt_done"), 4 * j + x + 1)
                pe.wait_ge(pair_free[p], reads(base + p) + 2 * j + x // 2)
                if x % 2 == 0:
                    pe.wait_ge(S("qc_done"), 2 * j + x // 2 + 1)
                for c in range(NBLK):
                    for t in range(NG):
                        kk = KT[:, 4 * t:4 * t + 4, c, :] if c < 8 else KTp[:, 4 * t:4 * t + 4, c - 8, :]
                        ins = mm(pairs[p][32 * t:32 * t + 32, 0:P], Qc[x // 2][:, 32 * c:32 * c + 32], kk, start=c == 0, stop=c == NBLK - 1)
                ins.then_inc(S("sc_done"), 1)

            def cache_values(j, x):
                p = 1 + 2 * (x // 2)
                if x % 2 == 0:
                    pe.wait_ge(pair_free[p], reads(base + p) + j)
                pe.wait_ge(S("ps_done"), 2 * (4 * j + x + 1))
                for y in range(4):
                    for t in range(NG):
                        unit = 4 * t + y
                        ins = mm(pairs[p][32 * t:32 * t + 32, 0:KVL], PS[x % 2][:, unit, :], KC[x][:, KVL * unit:KVL * unit + KVL],
                                 start=x % 2 == 0 and y == 0, stop=x % 2 == 1 and y == 3)
                ins.then_inc(S("pv_done"), 1)

            cache_scores(0, 0)
            with pe.Fori(0, NB // 2 - 1) as j:
                for x in range(4):
                    cache_scores(j + (x + 1) // 4, (x + 1) % 4)
                    cache_values(j, x)
            for x in range(4):
                if x < 3:
                    cache_scores(NB // 2 - 1, x + 1)
                cache_values(NB // 2 - 1, x)
            ps = take("mt")
            pe.wait_ge(S("mc_done"), 1)
            for e in range(2):
                ins = mm(ps[0:NB, P * e:P * e + P], Mc[:, e, :], ident, start=True, stop=True)
            done(ins)
            ps = take("mx")
            pe.wait_ge(S("mexp_done"), 1)
            done(mm(ps[:, 0:NB], mexp, C("ident", NB)[:, 0:NB], start=True, stop=True))
            ps = take("den")
            pe.wait_ge(S("lw_done"), 1)
            for e in range(2):
                ins = mm(ps[0:NB, 0:4], Lc[:, e, :], C("sell"), start=e == 0, stop=e == 1)
            done(ins)
            ps = take("rb")
            pe.wait_ge(S("rexp_done"), 1)
            mm(ps[:, 0:NB], rexp, C("ident", NB)[:, 0:NB], start=True, stop=True)
            done(mm(ps[:, 512:544], C("ones", NB), wx8, start=True, stop=True))
            ps = take("osum")
            pe.wait_ge(S("selw_done"), 1)
            for b in range(NB):
                r, o = 32 * (b % 4), 512 * (b // 4)
                ins = mm(ps[r:r + 32, o:o + KVL], selw[:, b, :], Oall[:, b, :], start=True, stop=True)
            done(ins)
            ps = take("ol")
            evacuated("osum")
            for y in range(2):
                for rh in range(2):
                    o = 512 * y + P * rh
                    ins = nc.tensor.transpose(ps[:, o:o + P], osb[:, y, P * rh:P * rh + P], ident)
            done(ins)
            ps = take("omd")
            evacuated("ol")
            for h in range(4):
                for rh in range(2):
                    ins = mm(ps[:, 8 * h:8 * h + 8], wuv[:, rh, h, :], olat[:, rh, 8 * h:8 * h + 8], start=rh == 0, stop=rh == 1)
            done(ins)
            for i in range(NT):
                ps = take(f"lg{i}")
                if i == 0:
                    evacuated("gr")
                done(mm(ps[0:TT[i], 0:256], grT[0:RANK + 1, P * i:P * i + TT[i]], wgk[0:RANK + 1, :], start=True, stop=True))
            for c in range(NT):
                ps = take(f"b{c}")
                evacuated(f"lg{c}")
                tri = C("ucum") if c < 4 else C("ucum4", TT[4])
                for q in range(2):
                    ins = mm(ps[:, 512 * q:512 * q + TT[c]], lgs[0:TT[c], c, P * q:P * q + P], tri, start=True, stop=True)
                done(ins)
            for lv in range(NL + 1):
                qq, kk = (qt[lv % 2], kt[lv % 2]) if lv < NL else (gq, gk)
                if lv < NL:
                    pe.wait_ge(S("qk_done"), lv + 1)
                for c in range(NT):
                    if f"G{lv}.{c}" in PLAN:
                        n = min(P, NP - P * c)
                        ps = take(f"G{lv}.{c}")
                        for h in (0, 2, 1, 3):
                            a, q = h % 2, h // 2
                            ins = mm(ps[0:n, 512 * a + P * q:512 * a + P * q + n], kk[64 * a:64 * a + 64, q, P * c:P * c + n],
                                     qq[64 * a:64 * a + 64, q, P * c:P * c + n], start=True, stop=True)
                        done(ins)
                ps = take(f"vb{lv}")
                if lv == 0:
                    pe.wait_ge(S("pick_loaded"), 16)
                done(mm(ps[:, 0:512], pick[:, lv, :], vtok[0:24, 4, :], start=True, stop=True))
            ps = take("os")
            for b in range(NB - 4, NB):
                evacuated(f"vb{b}")
            for b in range(NB):
                for h in (0, 2, 1, 3):
                    a, q = h % 2, h // 2
                    o = 512 * a + 8 * q + b
                    ins = mm(ps[:, o:o + 1], states[64 * a:64 * a + 64, b, q, :], gq[64 * a:64 * a + 64, q, NP + b:NP + b + 1],
                             start=True, stop=True)
            done(ins)
            qe, ke = qt[NL % 2], kt[(NL + 1) % 2]
            pe.wait_ge(S("qk_done"), NL + 1)
            for c in range(NT + 1):
                if c < NT:
                    n = min(P, NP - P * c)
                    ps = take(f"kt{c}")
                    for q in range(2):
                        ins = mm(ps[0:n, P * q:P * q + P], ke[:, q, P * c:P * c + n], ident, start=True, stop=True)
                    done(ins)
                    ps = take(f"s{c}")
                    evacuated(f"kt{c}")
                    for h in range(4):
                        a, q = h % 2, h // 2
                        ins = mm(ps[64 * a:64 * a + 64, P * q:P * q + P], ktok[0:n, q, 64 * a:64 * a + 64], vtok[0:n, c, P * h:P * h + P],
                                 start=True, stop=True)
                    done(ins)
                if c:
                    v = c - 1
                    n = min(P, NP - P * v)
                    ps = take(f"o{v}")
                    if v == 0:
                        evacuated(last_g(NT - 1))
                    else:
                        evacuated(f"s{v - 1}")
                    for h in (0, 2, 1, 3):
                        a, q = h % 2, h // 2
                        out = ps[:, 512 * a + P * q:512 * a + P * q + n]
                        ins = mm(out, vtok[0:n, v, P * h:P * h + P], AT[0:n, v, 2 * a + q, 0:n], start=True, stop=v == 0)
                        if v:
                            ins = mm(out, Sst[(v - 1) % 2][64 * a:64 * a + 64, q, :], qe[64 * a:64 * a + 64, q, P * v:P * v + n], start=False, stop=True)
                    done(ins)
            for h in range(4):
                ps = take(f"ssg{h}")
                pe.wait_ge(S("sqg_done"), h + 1)
                done(ones_sum(ps, [sqg[h]]))
            def out_proj(m, part):
                n = B_OUT + m // 2
                h, l = view(whi, n), view(wlo, n)
                k0 = 4 if part == 0 else 0
                cut = lambda ap, j: ap[:, k0 + j, P * (m % 2):P * (m % 2) + P]
                return dense(pairs[PLAN[f"wo{m}"] % 4], h, l, cut, list(range(k0, k0 + 4)), xhi, xlo, first=part == 0, last=part == 1)

            def residual(m):
                ps = take(f"hT{m}")
                for i in range(NT):
                    ins = nc.tensor.transpose(ps[:, P * i:P * i + TT[i]], X2[i][0:TT[i], P * m:P * m + P], C("ident", TT[i])[:, 0:TT[i]])
                done(ins)

            for m in range(4):
                if m % 2 == 0:
                    use(B_OUT + m // 2)
                take(f"wo{m}")
                out_proj(m, 0)
            pe.wait_ge(S("mixlo_done"), 4)
            for m in range(4):
                done(out_proj(m, 1))
            pe.wait_ge(S("x2_loaded"), 16 * (NT + 2))
            for m in range(4):
                residual(m)
            for m in range(4, KD):
                if m % 2 == 0:
                    use(B_OUT + m // 2)
                take(f"wo{m}")
                out_proj(m, 0)
                done(out_proj(m, 1))
                residual(m)
            ps = take("ssf")
            pe.wait_ge(S("sqf_done"), KD)
            done(ones_sum(ps, [sqf[:, k, :] for k in range(KD)]))
            base = PLAN["ffn0"]
            pe.wait_ge(S("nlo_done"), KD)
            with pe.Fori(0, DFF // 256) as j:
                for s in range(2):
                    n = B_FFN + s
                    pe.wait_ge(w_lo, n + 1 + 2 * j)
                    for m in range(2):
                        p = 2 * s + m
                        pe.wait_ge(pair_free[p], reads(base + p) + j)
                        done(dense(pairs[p], view(whi, n, KD), view(wlo, n, KD), cols(P * m), list(range(KD)), xhi, xlo))
            base = PLAN["dn0"]
            pe.wait_ge(S("hlo_done"), KF)
            with pe.Fori(0, 2) as j:
                for cb in range(2):
                    for q, (k0, kk) in enumerate(DPARTS):
                        n = B_DOWN + 3 * cb + q
                        pe.wait_ge(w_lo, n + 1 + 6 * j)
                        for m in range(2):
                            p = 2 * cb + m
                            if q == 0:
                                pe.wait_ge(pair_free[p], reads(base + p) + j)
                            ins = dense(pairs[p], view(whi, n, kk), view(wlo, n, kk), cols(P * m), list(range(k0, k0 + kk)), hhi, hlo,
                                        first=q == 0, last=q == 2)
                            if q == 2:
                                done(ins)
                        if q < 2:
                            ins.then_inc(S("dn_part"), 1)
            ps = take("ssy")
            pe.wait_ge(S("sqy_done"), KD)
            done(ones_sum(ps, [sqy[:, k, :] for k in range(KD)]))
            pe.wait_ge(S("yT_done"), KD)
            for i in range(NT):
                ps = take(f"y{i}")
                for k in range(KD):
                    ins = mm(ps[0:TT[i], P * k:P * k + P], yT[:, k, P * i:P * i + TT[i]], ident, start=True, stop=True)
                done(ins)

        @block.scalar
        def _(act):
            f = nc.scalar.activation
            chain = [0]

            def link(ins):
                chain[0] += 1
                ins.then_inc(act_chain, 1)
                act.wait_ge(act_chain, chain[0])

            def ready(name):
                act.wait_ge(pe_done, fills(name))
                return pairs[PLAN[name] % 4]

            def free(ins, name):
                ins.then_inc(pair_free[PLAN[name] % 4], 1)

            def hi(n, size=None):
                act.wait_ge(w_loaded[n % 2], 16 * LOADS[n])
                if n >= 2:
                    act.wait_ge(pe_done, fills(LAST[n - 2]))
                size = size or block_size(n)
                f(whi[n % 2][:, 0:size], wraw[n % 2][:, 0:size], ACT.Copy).then_inc(w_hi, 1)

            def rsqrt(out, src, tmp, width):
                link(f(tmp, src, ACT.Ln, scale=1.0 / width, bias=C("eps", src.shape[0])))
                return f(out, tmp, ACT.Exp, scale=-0.5)

            act.wait_ge(S("stat_clear"), 1)
            act.wait_ge(c_loaded, 16)
            for i in range(NT):
                act.wait_ge(x_loaded[i], 32 if i in (0, 4) else 16)
                link(f(scr[0:TT[i], :], X[0:TT[i], i, :], ACT.Square, accum_out=stat[0:TT[i], i:i + 1]))
            rsqrt(stat[:, 8:8 + NT], stat[:, 0:NT], stat[:, 0:NT], D).then_inc(S("rs_done"), 1)
            hi(0)
            act.wait_ge(n_loaded, 16 * 5)
            act.wait_ge(S("pad_done"), 3)
            for k in range(KD):
                ps = ready(f"xT{k}")
                f(xhi[:, k, 0:T], ps[:, 0:T], ACT.Copy, scale=nrm[:, k:k + 1]).then_inc(S("xhi_done"), 1)
                if k == 5:
                    hi(1)
            for m in range(3):
                if m == 2:
                    hi(2)
                act.wait_ge(pair_free[PLAN[f"cq{m}"] % 4], reads(PLAN[f"cq{m}"]) + 1)
                f(sqs[:, m, :], cq[:, m, :], ACT.Square).then_inc(S("sqs_done"), 1)
            hi(3)
            for i in range(NT):
                ps = ready(f"tok{i}")
                link(f(scr[:, 0:KVL], ps[:, 0:KVL], ACT.Square, accum_out=stat[:, 16 + i:17 + i]))
                rsqrt(stat[:, 24 + i:25 + i], stat[:, 16 + i:17 + i], stat[:, 16 + i:17 + i], KVL).then_inc(S("rk_done"), 1)
            hi(4)
            ps = ready("ssq")
            link(f(split2(rsb[:, :]), halves(ps), ACT.Ln, scale=1.0 / QL, bias=C("eps")))
            ins = f(rsb[:, :], rsb[:, :], ACT.Exp, scale=-0.5)
            free(ins, "ssq")
            hi(5)
            act.wait_ge(S("qn_done"), 1)
            f(qnhi[:, :, :], cq[:, :, :], ACT.Copy).then_inc(S("qnhi_done"), 1)
            for m in range(2):
                free(f(split2(gq[:, m, :]), halves(ready(f"q{m}")), ACT.Copy, scale=DK ** -0.5), f"q{m}")
            hi(6)
            for m in range(2):
                free(f(split2(gk[:, m, :]), halves(ready(f"k{m}")), ACT.Copy), f"k{m}")
            hi(7)
            for i in range(NT):
                free(f(vtok[:, i, :], ready(f"v{i}")[:, 0:512], ACT.Copy), f"v{i}")
            hi(8)
            hi(9)
            for m in range(4):
                f(split2(gT[:, m, :]), halves(ready(f"g{m}")), ACT.Exp, scale=-1.0).then_inc(S("ge_done"), 1)
                if m == 2:
                    hi(10)
            hi(11)
            for j in range(2):
                f(ckhi[:, j, 0:T], ready(f"ck{j}")[:, 0:T], ACT.Copy).then_inc(S("ckhi_done"), 1)
            for hh in range(2):
                for x in range(2):
                    free(f(split2(qnT[:, 2 * hh + x, :]), halves(ready(f"qn{2 * hh + x}")), ACT.Copy), f"qn{2 * hh + x}")
                free(f(split2(qpe[:, hh, :]), halves(ready(f"qp{hh}")), ACT.Copy), f"qp{hh}")
                if hh == 0:
                    hi(12)
            for h in range(MH):
                free(f(split2(knT[:, h, :]), halves(ready(f"kn{h}")), ACT.Copy), f"kn{h}")
            for x in range(2):
                free(f(wukT[:, 2 * x:2 * x + 2, :].rearrange("p a b -> p (a b)"), ready(f"wuk{x}")[:, 0:512], ACT.Copy), f"wuk{x}")
            U = NT * MH
            for u in range(U + 2):
                if u < U:
                    qb = u // MH
                    nq, nk = min(P, NP - P * qb), min(P * qb + P, NP)
                    s = 32 + 4 * (u % 2)
                    ps = ready(f"S{u}")
                    act.wait_ge(S("nmax_done"), u + 1)
                    if u >= 2:
                        act.wait_ge(pe_done, fills(f"PT{u - 2}"))
                    free(f(pr[u % 2][0:nq, 0:nk], ps[0:nq, 0:nk], ACT.Exp, scale=SCALE, bias=stat[0:nq, s + 1:s + 2],
                           accum_out=stat[0:nq, s + 2:s + 3]), f"S{u}")
                if 1 <= u <= U:
                    v = u - 1
                    qb = v // MH
                    nq = min(P, NP - P * qb)
                    ps = ready(f"PT{v}")
                    if v >= 2:
                        act.wait_ge(pe_done, fills(f"OM{v - 2}"))
                    nb = min(qb + 1, 4)
                    ins = f(pt[v % 2][:, 0:nb, 0:nq], ps[:, 0:P * nb].rearrange("p (k q) -> p k q", q=P)[:, :, 0:nq], ACT.Copy)
                    if qb == 4:
                        ins = f(pt[v % 2][0:16, 4, 0:16], ps[0:16, 512:528], ACT.Copy)
                    free(ins, f"PT{v}")
                if u >= 2:
                    v = u - 2
                    qb, h = divmod(v, MH)
                    nq = min(P, NP - P * qb)
                    f(xhi[:, 4 + h, P * qb:P * qb + nq], ready(f"OM{v}")[:, 0:nq], ACT.Copy).then_inc(S("omhi_done"), 1)
            act.wait_ge(S("Qall_done"), 1)
            act.wait_ge(S("ps_clear"), 2)

            def queries(b, x):
                f(Qc[x][:, :], Qall[:, bass.ds(b, 1), :].rearrange("p a n -> p (a n)"), ACT.Copy).then_inc(S("qc_done"), 1)

            def cache_softmax(j, x, more=True):
                n = 4 * j + x
                act.wait_ge(S("nm_done"), n + 1)
                f(Pc[:, :], pairs[2 * (x % 2)][:, 0:P], ACT.Exp, scale=SCALE, bias=mc[:, 4 + x:5 + x],
                  accum_out=mc[:, 8 + x:9 + x]).then_inc(pair_free[2 * (x % 2)], 1)
                if x % 2 == 0 and more:
                    queries(2 * j + x // 2 + 1, (x // 2 + 1) % 2)
                act.wait_ge(S("pt_done"), n + 1)
                for t in (0, 1):
                    for gg in range(NG):
                        at = 16 * (x % 2) + 4 * gg
                        ins = f(PS[x % 2][32 * gg:32 * gg + 32, 4 * t:4 * t + 4, at:at + 4], Pt[32 * t:32 * t + 32, :, 4 * gg:4 * gg + 4], ACT.Copy)
                ins.then_inc(S("ps_done"), 1)
                if x % 2 == 1:
                    act.wait_ge(S("pv_done"), n + 1)
                    p = 1 + 2 * (x // 2)
                    f(Oall[:, bass.ds(2 * j + x // 2, 1), :].rearrange("p a n -> p (a n)"), pairs[p][:, 0:KVL], ACT.Copy).then_inc(pair_free[p], 1)

            queries(0, 0)
            with act.Fori(0, NB // 2 - 1) as j:
                for x in range(4):
                    cache_softmax(j, x)
            for x in range(4):
                cache_softmax(NB // 2 - 1, x, more=x < 2)
            act.wait_ge(S("d2_done"), 1)
            f(w8, w8, ACT.Exp, scale=SCALE).then_inc(S("wexp_done"), 1)
            act.wait_ge(pair_free[PLAN["mx"] % 4], reads(PLAN["mx"]) + 1)
            f(Wc, Wc, ACT.Exp, scale=SCALE).then_inc(S("wexp_done"), 1)
            hi(13)
            hi(14)
            f(xhi[:, 4:8, NP:T], ready("omd")[:, 0:32].rearrange("p (h b) -> p h b", h=4), ACT.Copy).then_inc(S("omdhi_done"), 1)
            for i in range(NT):
                ps = ready(f"lg{i}")
                r = TT[i]
                if i:
                    act.wait_ge(pair_free[PLAN[f"lg{i - 1}"] % 4], reads(PLAN[f"lg{i - 1}"]) + 1)
                else:
                    act.wait_ge(pair_free[PLAN["omd"] % 4], reads(PLAN["omd"]) + 1)
                link(f(lgt[0:r, :], ps[0:r, 0:256], ACT.Abs))
                link(f(lgt[0:r, :], lgt[0:r, :], ACT.Exp, scale=-1.0))
                f(lgt[0:r, :], lgt[0:r, :], ACT.Ln, bias=1.0).then_inc(S("lgt_done"), 1)
            for c in range(NT):
                ps = ready(f"b{c}")
                free(f(bT[:, :, P * c:P * c + TT[c]], ps[:, :].rearrange("p (q t) -> p q t", q=2)[:, :, 0:TT[c]], ACT.Copy), f"b{c}")
            for c in range(NT):
                act.wait_ge(pair_free[PLAN[f"b{c}"] % 4], reads(PLAN[f"b{c}"]) + 1)
            f(eb[:, :, :], bT[:, :, NP:T], ACT.Exp).then_inc(S("eb_done"), 1)
            f(el[:, :, 0:4], bT[:, :, P - 1:4 * P:P], ACT.Exp)
            f(el[:, :, 4:5], bT[:, :, NP - 1:NP], ACT.Exp).then_inc(S("eb_done"), 1)
            for lv in range(NL):
                n = 512 if LEVELS[lv] > 8 else NP
                act.wait_ge(S("diff_done"), lv + 1)
                f(Ee[lv % 2][:, :, 0:n], Ee[lv % 2][:, :, 0:n], ACT.Exp).then_inc(S("E_done"), 1)
                if lv == 1:
                    act.wait_ge(S("eb_done"), 2)
                    act.wait_ge(S("states_loaded"), 16 * 2 * NB)
                    for b in range(NB):
                        for q in range(2):
                            ins = f(states[:, b, q, :], states[:, b, q, :], ACT.Copy, scale=eb[:, q, b:b + 1])
                    ins.then_inc(S("decay_done"), 1)
            act.wait_ge(S("qk_done"), NL - 1)
            f(Ee[NL % 2][:, :, :], bT[:, :, 0:NP], ACT.Exp).then_inc(S("E_done"), 1)
            act.wait_ge(S("diff_done"), NL + 1)
            f(Ee[(NL + 1) % 2][:, :, :], Ee[(NL + 1) % 2][:, :, :], ACT.Exp).then_inc(S("E_done"), 1)
            act.wait_ge(S("qk_done"), NL + 1)
            ps = ready("os")
            ins = f(oT[:, :, NP:T].rearrange("p (q a) t -> p a q t", a=2),
                    ps[:, :].rearrange("p (a q t) -> p a q t", a=2, q=64)[:, :, 0:2, :], ACT.Copy)
            free(ins, "os")
            for c in range(NT + 1):
                if c < NT:
                    n = min(P, NP - P * c)
                    ps = ready(f"kt{c}")
                    if c:
                        act.wait_ge(pe_done, fills(f"s{c - 1}"))
                    free(f(ktok[0:n, :, :], ps[0:n, 0:256].rearrange("p (q d) -> p q d", q=2), ACT.Copy), f"kt{c}")
                if c:
                    v = c - 1
                    n = min(P, NP - P * v)
                    ps = ready(f"o{v}")
                    free(f(oT[:, :, P * v:P * v + n].rearrange("p (q a) t -> p a q t", a=2),
                           ps[:, :].rearrange("p (a q t) -> p a q t", a=2, q=4)[:, :, 0:2, 0:n], ACT.Copy), f"o{v}")
            act.wait_ge(pair_free[PLAN["o4"] % 4], reads(PLAN["o4"]) + 1)
            act.wait_ge(pair_free[PLAN["os"] % 4], reads(PLAN["os"]) + 1)
            for h in range(4):
                f(sqg[h][:, :], oT[:, h, :], ACT.Square).then_inc(S("sqg_done"), 1)
            for h in range(4):
                link(f(split2(rsg[h][:, :]), halves(ready(f"ssg{h}")), ACT.Ln, scale=1.0 / DV, bias=C("eps")))
                free(f(rsg[h][:, :], rsg[h][:, :], ACT.Exp, scale=-0.5), f"ssg{h}")
            for h in range(4):
                act.wait_ge(S("og_done"), h + 1)
                f(xhi[:, h, 0:T], oT[:, h, :], ACT.Copy).then_inc(S("mixhi_done"), 1)
            act.wait_ge(S("mixlo_done"), 4)

            def take_out(m):
                free(f(split2(hT[:, m, :]), halves(ready(f"wo{m}")), ACT.Copy), f"wo{m}")

            def square(m):
                act.wait_ge(pair_free[PLAN[f"hT{m}"] % 4], reads(PLAN[f"hT{m}"]) + 1)
                f(sqf[:, m, :], hT[:, m, :], ACT.Square).then_inc(S("sqf_done"), 1)

            for m in range(4):
                take_out(m)
            hi(15)
            hi(16)
            for m in range(4):
                square(m)
            for m in range(4, KD):
                take_out(m)
                if m == 6:
                    hi(17)
                square(m)
            hi(18)
            ps = ready("ssf")
            link(f(split2(rsf[:, :]), halves(ps), ACT.Ln, scale=1.0 / D, bias=C("eps")))
            free(f(rsf[:, :], rsf[:, :], ACT.Exp, scale=-0.5), "ssf")
            for k in range(KD):
                act.wait_ge(S("tf_done"), k + 1)
                f(xhi[:, k, 0:T], tf[k % 2][:, :], ACT.Copy).then_inc(S("nhi_done"), 1)
            act.wait_ge(out_done, 16 * (12 + 2 + 16))
            base = PLAN["ffn0"]
            with act.Fori(0, DFF // 256) as j:
                for m in range(2):
                    act.wait_ge(pe_done, fills("ffn0") + 4 * j + m)
                    act.wait_ge(w_lo, B_FFN + 2 + 2 * j)
                    f(split2(fe[m][:, :]), halves(pairs[m]), ACT.Exp, scale=-1.0).then_inc(S("fe_done"), 1)
                for s in range(2):
                    if s == 1:
                        for m in range(2):
                            act.wait_ge(pair_free[2 + m], reads(base + 2 + m) + 1 + j)
                            f(hhi[:, bass.ds(2 * j + m, 1), :].rearrange("p a t -> p (a t)"), fe[m][:, :], ACT.Copy).then_inc(S("hhi_done"), 1)
                    n = B_FFN + s
                    act.wait_ge(pe_done, fills("ffn0") + 4 * j + 2 * s + 1)
                    act.wait_ge(w_loaded[n % 2], 16 * (LOADS[n] + 1) + 16 * j)
                    f(whi[n % 2][:, :], wraw[n % 2][:, :], ACT.Copy).then_inc(w_hi, 1)
            for cb in range(4):
                for q in range(3):
                    n = B_DOWN + 3 * cb + q + 2
                    if n < B_DOWN + 12:
                        if q < 2:
                            act.wait_ge(S("dn_part"), 2 * cb + q + 1)
                        else:
                            act.wait_ge(pe_done, fills(f"dn{2 * cb + 1}"))
                        act.wait_ge(w_loaded[n % 2], 16 * LOADS[n])
                        size = 256 * DPARTS[(q + 2) % 3][1]
                        f(whi[n % 2][:, 0:size], wraw[n % 2][:, 0:size], ACT.Copy).then_inc(w_hi, 1)
                for m in (2 * cb, 2 * cb + 1):
                    act.wait_ge(pair_free[PLAN[f"dn{m}"] % 4], reads(PLAN[f"dn{m}"]) + 1)
                    if m == 0:
                        act.wait_ge(pe_done, fills("dn0"))
                    f(sqy[:, m, :], hT[:, m, :], ACT.Square).then_inc(S("sqy_done"), 1)
            ps = ready("ssy")
            link(f(split2(rsy[:, :]), halves(ps), ACT.Ln, scale=1.0 / D, bias=C("eps")))
            free(f(rsy[:, :], rsy[:, :], ACT.Exp, scale=-0.5), "ssy")
            for i in range(NT):
                if i >= 2:
                    act.wait_ge(S(f"y_out{i % 2}"), 16 * (i // 2))
                f(ysb[i % 2][0:TT[i], 0:512], ready(f"y{i}")[0:TT[i], 0:512], ACT.Copy).then_inc(S("y_half"), 1)

        @block.vector
        def _(dve):
            v_ = nc.vector
            tt, ts, stt = v_.tensor_tensor, v_.tensor_scalar, v_.scalar_tensor_tensor
            chain = [0]

            def link(ins):
                chain[0] += 1
                ins.then_inc(dve_chain, 1)
                dve.wait_ge(dve_chain, chain[0])

            def ready(name):
                dve.wait_ge(pe_done, fills(name))
                return pairs[PLAN[name] % 4]

            def free(ins, name):
                ins.then_inc(pair_free[PLAN[name] % 4], 1)

            def lo(n):
                dve.wait_ge(w_hi, n + 1)
                size = block_size(n)
                tt(wlo[n % 2][:, 0:size], wraw[n % 2][:, 0:size], whi[n % 2][:, 0:size].bitcast(F32), ALU.subtract).then_inc(w_lo, 1)

            def rest(out, value, high):
                return tt(out, value, high.bitcast(F32), ALU.subtract)

            v_.memset(stat[:, :], 1.0).then_inc(S("stat_clear"), 1)
            dve.wait_ge(S("rs_done"), 1)
            for i in range(NT):
                ts(X[0:TT[i], i, :], X[0:TT[i], i, :], stat[0:TT[i], 8 + i:9 + i], None, ALU.mult).then_inc(S("xn_done"), 1)
            lo(0)
            dve.wait_ge(n_loaded, 16 * 5)
            for k in range(KD):
                dve.wait_ge(S("xhi_done"), k + 1)
                ps = ready(f"xT{k}")
                free(stt(xlo[:, k, 0:T], ps[:, 0:T], nrm[:, k:k + 1], xhi[:, k, 0:T].bitcast(F32), ALU.mult, ALU.subtract), f"xT{k}")
            lo(1)
            v_.memset(ckhi[:, :, T:TPAD].bitcast(F32), 0.0)
            v_.memset(cklo[:, :, T:TPAD].bitcast(F32), 0.0)
            for m in range(3):
                if m == 2:
                    lo(2)
                free(v_.tensor_copy(split2(cq[:, m, :]), halves(ready(f"cq{m}"))), f"cq{m}")
            lo(3)
            dve.wait_ge(small_loaded, 16 * 3)
            for i in range(NT):
                ps = ready(f"tok{i}")
                dve.wait_ge(S("rk_done"), i + 1)
                cos, sin = C("cosk")[:, ROPE * i:ROPE * i + ROPE], C("sink")[:, ROPE * i:ROPE * i + ROPE]
                tt(rp[:, 0, :], ps[:, 256:320], cos, ALU.mult)
                tt(rp[:, 1, 0:HALF], ps[:, 256 + HALF:320], sin[:, 0:HALF], ALU.mult)
                link(tt(rp[:, 1, HALF:ROPE], ps[:, 256:256 + HALF], sin[:, HALF:ROPE], ALU.mult))
                v_.tensor_copy(grt[:, i, :], ps[:, 320:336])
                tt(ctok[:, i, 256:320], rp[:, 0, :], rp[:, 1, :], ALU.add)
                link(tt(ctok[:, i, 320:384], rp[:, 0, :], rp[:, 1, :], ALU.add))
                free(stt(ctok[:, i, 0:KVL], ps[:, 0:KVL], stat[:, 24 + i:25 + i], kvn[:, :], ALU.mult, ALU.mult), f"tok{i}")
            lo(4)
            dve.wait_ge(pair_free[PLAN["ssq"] % 4], reads(PLAN["ssq"]) + 1)
            for m in range(3):
                ins = stt(cq[:, m, :], cq[:, m, :], nrm[:, 3 * KD + m:3 * KD + m + 1], rsb[:, :], ALU.mult, ALU.mult)
            ins.then_inc(S("qn_done"), 1)
            lo(5)
            dve.wait_ge(S("qnhi_done"), 1)
            rest(qnlo[:, :, :], cq[:, :, :], qnhi[:, :, :]).then_inc(S("qnlo_done"), 1)
            for n in (6, 7, 8, 9):
                lo(n)
            for m in range(4):
                dve.wait_ge(S("ge_done"), m + 1)
                link(ts(gT[:, m, :], gT[:, m, :], 1.0, None, ALU.add))
                link(v_.reciprocal(gT[:, m, :], gT[:, m, :]))
                free(tt(split2(gT[:, m, :]), split2(gT[:, m, :]), halves(ready(f"g{m}")), ALU.mult), f"g{m}")
                if m == 3:
                    lo(10)
            for j in range(3):
                ps = ready(f"ck{j}")
                if j < 2:
                    dve.wait_ge(S("ckhi_done"), j + 1)
                    rest(cklo[:, j, 0:T], ps[:, 0:T], ckhi[:, j, 0:T]).then_inc(S("cklo_done"), 1)
                    free(v_.tensor_copy(cks[:, j, :], ps[:, NP:T]), f"ck{j}")
                else:
                    free(v_.tensor_copy(kpT[:, :], ps[:, 0:T]), f"ck{j}")
            dve.wait_ge(S("pad_done"), 3)
            free(v_.tensor_copy(grT[0:RANK, :], ready("gr")[0:RANK, 0:T]), "gr")
            lo(11)
            lo(12)
            for hh in range(2):
                ps = ready(f"sw{hh}")
                free(tt(split2(rsb[:, :]), halves(ps), split2(C("sinf")), ALU.mult), f"sw{hh}")
                link(tt(qpe[:, hh, :], qpe[:, hh, :], C("cosf"), ALU.mult))
                dve.wait_ge(pair_free[PLAN[f"sw{hh}"] % 4], reads(PLAN[f"sw{hh}"]) + 1)
                ins = tt(qpe[:, hh, :], qpe[:, hh, :], rsb[:, :], ALU.add)
                if hh == 0:
                    link(ins)
            ins.then_inc(S("qpe_done"), 1)
            for i in range(NT):
                free(v_.tensor_copy(vm[:, i, :], ready(f"vm{i}")[:, 0:512]), f"vm{i}")
            ps = ready("qlat")
            v_.tensor_copy(qlT[:, :, :, :], ps[:, 0:64].rearrange("p (r h b) -> p r h b", r=2, h=4)).then_inc(pair_free[PLAN["qlat"] % 4], 1)
            dve.wait_ge(pair_free[PLAN["qlat"] % 4], reads(PLAN["qlat"]) + 1)
            for rh in range(2):
                tt(prod[:, rh, :, :], qlT[:, rh, :, :], cks[:, rh:rh + 1, :].broadcast_to([P, 4, NB]), ALU.mult)
            dve.wait_ge(S("qpe_done"), 1)
            link(v_.memset(prod[:, 2, :, :], 0.0))
            for a in range(2):
                r = slice(64 * a, 64 * a + 64)
                ins = tt(prod[r, 2, a:4:2, :], qpe[r, :, NP:T], kpT[r, NP:T].unsqueeze(1).broadcast_to([64, 2, NB]), ALU.mult)
            ins.then_inc(S("prod_done"), 1)
            free(v_.tensor_copy(sn8, ready("snew")[0:NB, 0:4]), "snew")
            U = NT * MH
            for u in range(U + 2):
                if u < U:
                    qb = u // MH
                    q0, nq, nk = P * qb, min(P, NP - P * qb), min(P * qb + P, NP)
                    s = 32 + 4 * (u % 2)
                    ps = ready(f"S{u}")
                    link(tt(ps[0:nq, q0:nk], ps[0:nq, q0:nk], C("cap", nq)[:, 0:nq], ALU.min))
                    link(v_.reduce_max(stat[0:nq, s:s + 1], ps[0:nq, 0:nk], AX))
                    ts(stat[0:nq, s + 1:s + 2], stat[0:nq, s:s + 1], -SCALE, None, ALU.mult).then_inc(S("nmax_done"), 1)
                    dve.wait_ge(pair_free[PLAN[f"S{u}"] % 4], reads(PLAN[f"S{u}"]) + 1)
                    link(v_.reciprocal(stat[0:nq, s + 3:s + 4], stat[0:nq, s + 2:s + 3]))
                    ts(pr[u % 2][0:nq, 0:nk], pr[u % 2][0:nq, 0:nk], stat[0:nq, s + 3:s + 4], None, ALU.mult).then_inc(S("pn_done"), 1)
                if u >= 2:
                    v = u - 2
                    qb, h = divmod(v, MH)
                    nq = min(P, NP - P * qb)
                    dve.wait_ge(S("omhi_done"), v + 1)
                    ins = rest(xlo[:, 4 + h, P * qb:P * qb + nq], ready(f"OM{v}")[:, 0:nq], xhi[:, 4 + h, P * qb:P * qb + nq])
                    free(ins, f"OM{v}")
            dve.wait_ge(out_done, 16 * 12)
            dve.wait_ge(S("ps_clear"), 2)

            def cache_keys(j, x):
                dve.wait_ge(S(f"kc_loaded{x}"), 32 + 32 * j)
                v_.transpose(KT[:, :, :, :].rearrange("p u c j -> p (u c j)").bitcast(U32), KC[x][:, :].bitcast(U32))
                v_.transpose(KTp[:, :, :, :].rearrange("p u c j -> p (u c j)").bitcast(U32), KP[x][:, :].bitcast(U32)).then_inc(S("kt_done"), 1)

            def cache_max(j, x):
                n = 4 * j + x
                dve.wait_ge(S("sc_done"), n + 1)
                v_.reduce_max(mc[:, x:x + 1], pairs[2 * (x % 2)][:, 0:P], AX).then_inc(S("m_done"), 1)
                dve.wait_ge(S("m_done"), n + 1)
                ts(mc[:, 4 + x:5 + x], mc[:, x:x + 1], -SCALE, None, ALU.mult).then_inc(S("nm_done"), 1)

            def cache_probs(j, x):
                n = 4 * j + x
                p = 2 * (x % 2)
                dve.wait_ge(pair_free[p], reads(PLAN["cache0"] + p) + 2 * j + x // 2 + 1)
                dve.wait_ge(S("ps_done"), 2 * n) if not isinstance(n, int) or n > 0 else None
                v_.transpose(Pt[:, :, :].rearrange("p u j -> p (u j)").bitcast(U32), Pc[:, :].bitcast(U32)).then_inc(S("pt_done"), 1)
                dve.wait_ge(S("pt_done"), n + 1)
                for t in (2, 3):
                    for gg in range(NG):
                        at = 16 * (x % 2) + 4 * gg
                        ins = v_.tensor_copy(PS[x % 2][32 * gg:32 * gg + 32, 4 * t:4 * t + 4, at:at + 4], Pt[32 * t:32 * t + 32, :, 4 * gg:4 * gg + 4])
                ins.then_inc(S("ps_done"), 1)
                if x == 3:
                    v_.tensor_copy(ML[:, bass.ds(12 * j, 12)], mc).then_inc(S("ml_done"), 1)
                    dve.wait_ge(S("ml_done"), j + 1)

            cache_keys(0, 0)
            cache_max(0, 0)
            with dve.Fori(0, NB // 2 - 1) as j:
                for x in range(4):
                    cache_keys(j + (x + 1) // 4, (x + 1) % 4)
                    cache_probs(j, x)
                    cache_max(j + (x + 1) // 4, (x + 1) % 4)
            for x in range(4):
                if x < 3:
                    cache_keys(NB // 2 - 1, x + 1)
                cache_probs(NB // 2 - 1, x)
                if x < 3:
                    cache_max(NB // 2 - 1, x + 1)
            dve.wait_ge(S("pv_done"), CHUNKS * NB)
            v_.memset(selw[:, :, :], 0.0)
            mlv = ML.rearrange("p (j k b e) -> p k e j b", j=NB // 2, k=3, b=2)
            for e in range(2):
                v_.tensor_copy(Mc[:, e, :].rearrange("p (j b) -> p j b", b=2), mlv[:, 0, e])
                ins = v_.tensor_copy(Lc[:, e, :].rearrange("p (j b) -> p j b", b=2), mlv[:, 2, e])
            ins.then_inc(S("mc_done"), 1)
            free(v_.reduce_max(mx8, ready("mt")[0:NB, 0:2 * P].rearrange("p (x h) -> p h x", h=4), AX), "mt")
            dve.wait_ge(pair_free[PLAN["mt"] % 4], reads(PLAN["mt"]) + 1)
            link(tt(mx8, mx8, sn8, ALU.max))
            tt(w8, sn8, mx8, ALU.subtract).then_inc(S("d2_done"), 1)
            v_.tensor_copy(mexp.rearrange("p (x h) -> p x h", h=4), mx8.unsqueeze(1).broadcast_to([NB, 32, 4])).then_inc(S("mexp_done"), 1)
            dve.wait_ge(S("mexp_done"), 1)
            ready("mx")
            free(tt(Wc, Mc, pairs[PLAN["mx"] % 4][:, 0:NB].unsqueeze(1).broadcast_to([P, 2, NB]), ALU.subtract), "mx")
            dve.wait_ge(pair_free[PLAN["mx"] % 4], reads(PLAN["mx"]) + 1)
            dve.wait_ge(S("wexp_done"), 2)
            tt(Lc, Lc, Wc, ALU.mult).then_inc(S("lw_done"), 1)
            free(tt(den8, ready("den")[0:NB, 0:4], w8, ALU.add), "den")
            dve.wait_ge(pair_free[PLAN["den"] % 4], reads(PLAN["den"]) + 1)
            link(v_.reciprocal(r8, den8))
            link(tt(wn8, w8, r8, ALU.mult))
            v_.tensor_copy(rexp.rearrange("p (x h) -> p x h", h=4), r8.unsqueeze(1).broadcast_to([NB, 32, 4]))
            tt(wx8.rearrange("p (h b) -> p h b", h=4), wn8.unsqueeze(2).broadcast_to([NB, 4, NB]),
               C("ident", NB)[:, 0:NB].unsqueeze(1).broadcast_to([NB, 4, NB]), ALU.mult).then_inc(S("rexp_done"), 1)
            ps = ready("rb")
            link(tt(Wc, Wc, ps[:, 0:NB].unsqueeze(1).broadcast_to([P, 2, NB]), ALU.mult))
            for e, sel in ((0, "sell"), (1, "selo")):
                o = selw[:, :, 0:4] if e == 0 else otmp[:, 0, :].rearrange("p (b h) -> p b h", h=4)
                ins = tt(o, Wc[:, e, :].unsqueeze(2).broadcast_to([P, NB, 4]), C(sel).unsqueeze(1).broadcast_to([P, NB, 4]), ALU.mult)
            link(ins)
            tt(selw[:, :, 0:4], selw[:, :, 0:4], otmp[:, 0, :].rearrange("p (b h) -> p b h", h=4), ALU.add).then_inc(S("selw_done"), 1)
            free(v_.tensor_copy(wvb, ps[:, 512:544]), "rb")
            free(v_.tensor_copy(osb[:, :, :], split2(ready("osum")[:, :])[:, :, 0:KVL]), "osum")
            dve.wait_ge(S("selw_done"), 1)
            dve.wait_ge(pair_free[PLAN["rb"] % 4], reads(PLAN["rb"]) + 1)
            for rh in range(2):
                ins = tt(otmp[:, rh, :].rearrange("p (h b) -> p h b", h=4), cks[:, rh:rh + 1, :].broadcast_to([P, 4, NB]),
                         wvb.rearrange("p (h b) -> p h b", h=4), ALU.mult)
            link(ins)
            ps = ready("ol")
            for rh in range(2):
                for y in range(2):
                    o = 512 * y + P * rh
                    src = ps[:, o:o + P].rearrange("p (b h) -> p h b", b=4)[:, 0:4, :]
                    ins = tt(olat[:, rh, :].rearrange("p (h b) -> p h b", h=4)[:, :, 4 * y:4 * y + 4], src,
                             otmp[:, rh, :].rearrange("p (h b) -> p h b", h=4)[:, :, 4 * y:4 * y + 4], ALU.add)
            free(ins, "ol")
            dve.wait_ge(S("omdhi_done"), 1)
            ps = ready("omd")
            rest(xlo[:, 4:8, NP:T], ps[:, 0:32].rearrange("p (h b) -> p h b", h=4), xhi[:, 4:8, NP:T]).then_inc(pair_free[PLAN["omd"] % 4], 1)
            for i in range(NT):
                dve.wait_ge(S("lgt_done"), i + 1)
                r = TT[i]
                free(stt(lgs[0:r, i, :], ready(f"lg{i}")[0:r, 0:256], 0.0, lgt[0:r, :], ALU.min, ALU.subtract), f"lg{i}")
            lo(13)
            lo(14)
            v_.memset(AT[:, :, :, :], 0.0)
            dve.wait_ge(S("msk_loaded"), 16)
            for c in range(NT):
                dve.wait_ge(pair_free[PLAN[f"b{c}"] % 4], reads(PLAN[f"b{c}"]) + 1)

            def differences(lv):
                s = LEVELS[lv]
                n = 512 if s > 8 else NP
                nb = n // (2 * s)
                if lv >= 2:
                    dve.wait_ge(S("qk_done"), lv - 1)
                for q in range(2):
                    bb = bT[:, q, 0:n].rearrange("p (n a s) -> p n a s", a=2, s=s)
                    ee = Ee[lv % 2][:, q, 0:n].rearrange("p (n a s) -> p n a s", a=2, s=s)
                    mid = bb[:, :, 0, s - 1:s].broadcast_to([P, nb, s])
                    tt(ee[:, :, 1, :], bb[:, :, 1, :], mid, ALU.subtract)
                    ins = tt(ee[:, :, 0, :], mid, bb[:, :, 0, :], ALU.subtract)
                ins.then_inc(S("diff_done"), 1)

            def keep_scores(lv):
                for c in range(NT):
                    if f"G{lv}.{c}" in PLAN:
                        n = min(P, NP - P * c)
                        ps = ready(f"G{lv}.{c}")
                        data = ps[0:n, :].rearrange("p (a q t) -> p a q t", a=2, q=4)[:, :, 0:2, 0:n]
                        out = AT[0:n, c, :, 0:n].rearrange("p (a q) t -> p a q t", a=2)
                        mask = msk[0:n, lv:lv + 1, 0:n].unsqueeze(1).broadcast_to([n, 2, 2, n])
                        free(v_.copy_predicated(out, mask.bitcast(U32), data), f"G{lv}.{c}")
                if lv == 0:
                    dve.wait_ge(S("decay_done"), 1)
                ps = ready(f"vb{lv}")
                for h in range(4):
                    a, q = h % 2, h // 2
                    r = slice(64 * a, 64 * a + 64)
                    ins = stt(states[r, lv, q, :], ps[r, P * h:P * h + P], gk[r, q, NP + lv:NP + lv + 1], states[r, lv, q, :], ALU.mult, ALU.add)
                free(ins, f"vb{lv}")

            differences(0)
            for lv in range(NL):
                n = 512 if LEVELS[lv] > 8 else NP
                if lv + 1 < NL:
                    differences(lv + 1)
                dve.wait_ge(S("E_done"), lv + 1)
                if lv >= 2:
                    dve.wait_ge(pe_done, fills(last_of_level(lv - 2)))
                tt(qt[lv % 2][:, :, 0:n], gq[:, :, 0:n], Ee[lv % 2][:, :, 0:n], ALU.mult)
                tt(kt[lv % 2][:, :, 0:n], gk[:, :, 0:n], Ee[lv % 2][:, :, 0:n], ALU.mult).then_inc(S("qk_done"), 1)
                if lv:
                    keep_scores(lv - 1)
            dve.wait_ge(S("qk_done"), NL)
            for c in range(NT):
                n = min(P, NP - P * c)
                e = P * c + n
                ins = tt(Ee[(NL + 1) % 2][:, :, P * c:e], bT[:, :, e - 1:e].broadcast_to([P, 2, n]), bT[:, :, P * c:e], ALU.subtract)
            ins.then_inc(S("diff_done"), 1)
            dve.wait_ge(S("E_done"), NL + 1)
            tt(qt[NL % 2][:, :, :], gq[:, :, 0:NP], Ee[NL % 2][:, :, :], ALU.mult)
            keep_scores(NL - 1)
            dve.wait_ge(S("E_done"), NL + 2)
            dve.wait_ge(pe_done, fills(last_of_level(NL - 1)))
            tt(kt[(NL + 1) % 2][:, :, :], gk[:, :, 0:NP], Ee[(NL + 1) % 2][:, :, :], ALU.mult).then_inc(S("qk_done"), 1)
            keep_scores(NL)
            dve.wait_ge(S("eb_done"), 2)
            for c in range(NT):
                ps = ready(f"s{c}")
                if c == 0:
                    free(v_.tensor_copy(Sst[0][:, :, :], ps[:, 0:256].rearrange("p (q v) -> p q v", q=2)), f"s{c}")
                    continue
                if c >= 2:
                    dve.wait_ge(pe_done, fills(f"o{c - 1}"))
                dve.wait_ge(pair_free[PLAN[f"s{c - 1}"] % 4], reads(PLAN[f"s{c - 1}"]) + 1)
                for q in range(2):
                    ins = stt(Sst[c % 2][:, q, :], Sst[(c - 1) % 2][:, q, :], el[:, q, c:c + 1], ps[:, P * q:P * q + P], ALU.mult, ALU.add)
                free(ins, f"s{c}")
            for h in range(4):
                dve.wait_ge(S("sqg_done"), h + 1)
                stt(oT[:, h, :], oT[:, h, :], nrm[:, 3 * KD + 3:3 * KD + 4], gT[:, h, :], ALU.mult, ALU.mult).then_inc(S("gated"), 1)
            for h in range(4 + 1):
                if h < 4:
                    dve.wait_ge(pair_free[PLAN[f"ssg{h}"] % 4], reads(PLAN[f"ssg{h}"]) + 1)
                    dve.wait_ge(S("gated"), h + 1)
                    tt(oT[:, h, :], oT[:, h, :], rsg[h][:, :], ALU.mult).then_inc(S("og_done"), 1)
                if h:
                    dve.wait_ge(S("mixhi_done"), h)
                    rest(xlo[:, h - 1, 0:T], oT[:, h - 1, :], xhi[:, h - 1, 0:T]).then_inc(S("mixlo_done"), 1)
            lo(15)
            lo(16)
            for m in range(KD):
                if m == 6:
                    lo(17)
                ps = ready(f"hT{m}")
                dve.wait_ge(pair_free[PLAN[f"wo{m}"] % 4], reads(PLAN[f"wo{m}"]) + 1)
                free(tt(hT[:, m, :], hT[:, m, :], ps[:, 0:T], ALU.add), f"hT{m}")
            lo(18)
            dve.wait_ge(pair_free[PLAN["ssf"] % 4], reads(PLAN["ssf"]) + 1)
            for k in range(KD + 1):
                if k < KD:
                    if k >= 2:
                        dve.wait_ge(S("nlo_done"), k - 1)
                    stt(tf[k % 2][:, :], hT[:, k, :], nrm[:, KD + k:KD + k + 1], rsf[:, :], ALU.mult, ALU.mult).then_inc(S("tf_done"), 1)
                if k:
                    dve.wait_ge(S("nhi_done"), k)
                    rest(xlo[:, k - 1, 0:T], tf[(k - 1) % 2][:, :], xhi[:, k - 1, 0:T]).then_inc(S("nlo_done"), 1)
            dve.wait_ge(out_done, 16 * (12 + 2 + 16))
            base = PLAN["ffn0"]
            per = 4
            c0 = chain[0]
            with dve.Fori(0, DFF // 256) as j:
                for m in range(2):
                    dve.wait_ge(S("fe_done"), 2 * j + m + 1)
                    ts(fe[m][:, :], fe[m][:, :], 1.0, None, ALU.add).then_inc(dve_chain, 1)
                    dve.wait_ge(dve_chain, c0 + per * j + 2 * m + 1)
                    v_.reciprocal(fe[m][:, :], fe[m][:, :]).then_inc(dve_chain, 1)
                    dve.wait_ge(dve_chain, c0 + per * j + 2 * m + 2)
                    tt(split2(fe[m][:, :]), split2(fe[m][:, :]), halves(pairs[m]), ALU.mult).then_inc(pair_free[m], 1)
                for s in range(2):
                    if s == 1:
                        for m in range(2):
                            dve.wait_ge(pe_done, fills("ffn0") + 4 * j + 2 + m)
                            dve.wait_ge(pair_free[m], reads(base + m) + 1 + j)
                            tt(split2(fe[m][:, :]), split2(fe[m][:, :]), halves(pairs[2 + m]), ALU.mult).then_inc(pair_free[2 + m], 1)
                            dve.wait_ge(S("hhi_done"), 2 * j + m + 1)
                            rest(hlo[:, bass.ds(2 * j + m, 1), :].rearrange("p a t -> p (a t)"), fe[m][:, :],
                                 hhi[:, bass.ds(2 * j + m, 1), :].rearrange("p a t -> p (a t)")).then_inc(S("hlo_done"), 1)
                    n = B_FFN + s
                    dve.wait_ge(w_hi, n + 3 + 2 * j)
                    tt(wlo[n % 2][:, :], wraw[n % 2][:, :], whi[n % 2][:, :].bitcast(F32), ALU.subtract).then_inc(w_lo, 1)
            chain[0] = c0 + per * (DFF // 256)
            for cb in range(4):
                for q in range(3):
                    n = B_DOWN + 3 * cb + q + 2
                    if n < B_DOWN + 12:
                        dve.wait_ge(w_hi, n + 1)
                        size = 256 * DPARTS[(q + 2) % 3][1]
                        tt(wlo[n % 2][:, 0:size], wraw[n % 2][:, 0:size], whi[n % 2][:, 0:size].bitcast(F32), ALU.subtract).then_inc(w_lo, 1)
                for m in (2 * cb, 2 * cb + 1):
                    free(tt(split2(hT[:, m, :]), split2(hT[:, m, :]), halves(ready(f"dn{m}")), ALU.add), f"dn{m}")
            dve.wait_ge(pair_free[PLAN["ssy"] % 4], reads(PLAN["ssy"]) + 1)
            for k in range(KD):
                stt(yT[:, k, :], hT[:, k, :], nrm[:, 2 * KD + k:2 * KD + k + 1], rsy[:, :], ALU.mult, ALU.mult).then_inc(S("yT_done"), 1)
            for i in range(NT):
                dve.wait_ge(S("y_half"), i + 1)
                ps = ready(f"y{i}")
                free(v_.tensor_copy(ysb[i % 2][0:TT[i], 512:D], ps[0:TT[i], 512:D]), f"y{i}")


_INS = ["x_prompt", "x_sample", "cache_ckv", "cache_kpe", "state_gla", "page_table", "meta_tokens", "norm_mix", "w_in",
        "w_gk", "b_gk", "gla_norm", "q_norm", "kv_norm", "w_uq", "w_ukv", "w_out", "norm_ffn", "w_gate", "w_up", "w_down",
        "norm_final"]
_OUTS = [(1, SEQ, D), (NB, 1, D), (1, 1, NP, KVL), (1, 1, NP, ROPE), (1, 1, GH, DK, DV), (1, NB, 1, KVL), (1, NB, 1, ROPE),
         (1, NB, GH, DK, DV)]


def kernel(**inputs):
    import concourse.bacc as bacc
    from concourse.bass_utils import run_bass_kernel_spmd

    nc = bacc.Bacc("TRN2", target_bir_lowering=False, num_devices=1)
    arrays, ins = {}, []
    shaped = dict(zip(("c_all", "c_masks", "c_pick"), constants()))
    for name in _INS + list(shaped):
        a = np.ascontiguousarray(inputs[name] if name in inputs else shaped[name])
        arrays[f"in_{name}"] = a
        ins.append(nc.dram_tensor(f"in_{name}", a.shape, mybir.dt.from_np(a.dtype), kind="ExternalInput").ap())
    outs = [nc.dram_tensor(f"out_{i}", s, F32, kind="ExternalOutput").ap() for i, s in enumerate(_OUTS)]
    hybrid_decode_kernel(nc, ins, outs)
    r = run_bass_kernel_spmd(nc, [arrays], core_ids=[0])
    return tuple(r.results[0][f"out_{i}"] for i in range(len(_OUTS)))
```

```python
from contextlib import ExitStack

import numpy as np

import concourse.bass as bass
from concourse import mybir

F32 = mybir.dt.float32
F32R = mybir.dt.float32r
I32 = mybir.dt.int32
U32 = mybir.dt.uint32
ALU = mybir.AluOpType
ACT = mybir.ActivationFunctionType
AX = mybir.AxisListType.X

P = 128
EPS = 1e-6
D = 1024
KD = D // P
NMETA = 16
SEQ = 512
NP = NMETA + SEQ
NB = 8
T = NP + NB
TH = T // 2
NT = 5
TPAD = NT * P
TT = [P, P, P, P, T - 4 * P]
PAST = 4096
PAGE = 128
NPAGES = PAST // PAGE
GH, DK, DV = 4, 64, 128
RANK = 16
MH, NOPE, ROPE = 4, 128, 64
HALF = ROPE // 2
QL, KVL = 384, 256
SCALE = float(NOPE + ROPE) ** -0.5
DFF = 2816
KF = DFF // P
C_Q, C_K, C_V, C_GR, C_G, C_CQ, C_CKV, C_KPE = 0, 256, 512, 1024, 1040, 1552, 1936, 2192
LEVELS = [64, 32, 16, 8, 4, 2, 1]
NL = len(LEVELS)
NEW_STATES = [[0], [1], [2], [3], [4], [5], [6, 7], []]
NG = P // 32
UNITS = 16
CHUNKS = NPAGES * PAGE // (P * UNITS)
NBLK = (KVL + ROPE) // 32

CC = {}
_at = 0
for _name, _n in (("ident", P), ("ones", P), ("ucum", P), ("swap", P), ("cosf", T), ("sinf", T), ("cosk", NT * ROPE),
                  ("sink", NT * ROPE), ("ucum4", 24), ("sell", 4), ("selo", 4), ("eps", 1), ("quart", 1), ("cap", P)):
    CC[_name] = (_at, _at + _n)
    _at += _n
NCONST = _at


def constants():
    c = np.zeros((P, NCONST), np.float32)

    def put(name, a):
        c[:, CC[name][0]:CC[name][1]] = a

    p = np.arange(P)
    put("ident", np.eye(P))
    put("ones", 1.0)
    put("ucum", (p[:, None] <= p[None, :]) / 16.0)
    last = np.zeros((P, 24))
    last[:16, :16] = np.triu(np.ones((16, 16))) / 16.0
    last[16:24, 16:] = np.eye(8) / 16.0
    put("ucum4", last)
    put("swap", np.eye(P)[p ^ HALF])
    pos = np.concatenate([np.arange(NP), np.full(TPAD - NP, PAST)]).astype(np.float32)
    inv = (10000.0 ** (-np.arange(HALF) / HALF)).astype(np.float32)
    ang = (pos[:, None] * inv[None, :]).astype(np.float32)
    cos, sin = np.cos(ang), np.sin(ang)
    cos2, sin2 = np.concatenate([cos, cos], 1), np.concatenate([-sin, sin], 1)
    put("cosf", np.concatenate([cos2, cos2], 1)[:T].T)
    put("sinf", np.concatenate([sin2, sin2], 1)[:T].T)
    put("cosk", cos2.reshape(NT, P, ROPE).transpose(1, 0, 2).reshape(P, -1))
    put("sink", sin2.reshape(NT, P, ROPE).transpose(1, 0, 2).reshape(P, -1))
    h = np.arange(4)
    put("sell", ((p[:, None] % 32 < 16) & (p[:, None] % 4 == h)).astype(np.float32))
    put("selo", ((p[:, None] % 32 >= 16) & (p[:, None] % 4 == h)).astype(np.float32))
    put("eps", EPS)
    put("quart", ((p % 4) * 2)[:, None])
    put("cap", np.where(p[None, :] <= p[:, None], 3e38, -3e38))
    masks = np.zeros((P, NL + 1, P), np.int32)
    for i, s in enumerate(LEVELS):
        same = p[:, None] // (2 * s) == p[None, :] // (2 * s)
        masks[:, i] = same & (p[:, None] % (2 * s) < s) & (p[None, :] % (2 * s) >= s)
    masks[:, NL] = np.eye(P)
    pick = np.zeros((24, NB, P), np.float32)
    for b in range(NB):
        pick[16 + b, b] = 1.0
    return c, masks.reshape(P, -1), pick.reshape(24, -1)


def plan():
    n = [f"xT{k}" for k in range(KD)]
    n += [f"cq{m}" for m in range(3)]
    n += [f"tok{i}" for i in range(NT)] + ["kr", "ssq"]
    n += [f"q{m}" for m in range(2)] + ["kp"] + [f"k{m}" for m in range(2)]
    n += [f"v{i}" for i in range(2 * NT)]
    n += [f"g{m}" for m in range(4)]
    n += [f"ck{j}" for j in range(3)]
    for hh in range(2):
        n += [f"qn{2 * hh}", f"qn{2 * hh + 1}", f"qp{hh}"]
    n += ["sw0", "sw1"]
    n += [f"kn{h}" for h in range(4)] + [f"vm{i}" for i in range(NT)] + ["wuk0", "wuk1", "qlat", "snew"]
    for u in range(NT * MH + 2):
        n += [f"S{u}"] if u < NT * MH else []
        n += [f"PT{u - 1}"] if 1 <= u <= NT * MH else []
        n += [f"OM{u - 2}"] if u >= 2 else []
    while len(n) % 4:
        n.append(f"-{len(n)}")
    n += [f"cache{i}" if i % 2 == 0 or i < 2 * NB else f"-cache{i}" for i in range(4 * NB)]
    n += ["mt", "lg0", "lg1", "mx", "lg2", "lg3", "den", "lg4"] + [f"b{c}" for c in range(NT)]
    for lv in range(NL + 1):
        for c in range(NT):
            if c < 4 or lv == NL or LEVELS[lv] <= 8:
                n += [f"G{lv}.{c}"]
        n += [f"vb{b}" for b in NEW_STATES[lv]]
        n += [("rb", "osum", "ol", "omd")[lv]] if lv < 4 else []
    n += ["os"]
    for c in range(NT + 1):
        n += [f"kt{c}", f"s{c}"] if c < NT else []
        n += [f"o{c - 1}"] if c else []
        n += ["ot"] if c == 1 else []
    n += [f"ssg{h}" for h in range(4)]
    n += [f"wo{m}" for m in range(4)] + [f"hT{m}" for m in range(4)]
    for m in range(4, KD):
        n += [f"wo{m}", f"hT{m}"]
    n += ["ssf"]
    while len(n) % 4:
        n.append(f"-{len(n)}")
    n += [f"ffn{i}" for i in range(2 * KF)]
    n += [f"dn{i}" for i in range(KD)]
    n += ["y0", "ssy"] + [f"y{i}" for i in range(1, NT)]
    return {name: i for i, name in enumerate(n)}


PLAN = plan()
IDLE = {v for k, v in PLAN.items() if k[0] == "-"}

BLOCKS = [[("w_in", 0, KD, C_CQ, 256)], [("w_in", 0, KD, C_CQ + 256, 128)], [("w_in", 0, KD, C_CKV, 256)],
          [("w_in", 0, KD, C_KPE, ROPE), ("w_in", 0, KD, C_GR, P - ROPE)],
          [("w_in", 0, KD, C_Q, 256)], [("w_in", 0, KD, C_K, 256)],
          [("w_in", 0, KD, C_V, 256)], [("w_in", 0, KD, C_V + 256, 256)],
          [("w_in", 0, KD, C_G, 256)], [("w_in", 0, KD, C_G + 256, 256)],
          *[[("w_uq", 0, 3, 384 * x + c, w) for c, w in ((0, 128), (192, 128), (128, 64), (320, 64))] for x in range(2)],
          [("w_ukv", 0, 2, 0, 1024)]]
B_UQ, B_UKV, B_OUT = 10, 12, 13
BLOCKS += [[("w_out", 0, KD, 256 * m, 256)] for m in range(4)]
B_FFN = len(BLOCKS)
B_DOWN = B_FFN + 2 * (DFF // 256)
DPARTS = [(0, 8), (8, 8), (16, 6)]


SIGNALS = ["E_done", "Qall_clear", "Qall_done", "ckhi_done", "cklo_done", "clear_done", "ctok_done", "d2_done",
           "decay_done", "diff_done", "diffp_done", "dn_part", "eb_done", "fe_done", "gated", "ge_done", "hhi_done",
           "hlo_done", "kd_done", "kr_done", "kr_pad", "kt_done", "lga_done", "lgs_done", "lgt_clear", "lgt_done",
           "lw_done", "m_done", "mc_done", "mexp_done", "mixhi_done", "mixlo_done", "ml_done", "msk_loaded",
           "nhi_done", "nlo_done", "nm_done", "nmax_done", "og_done", "omdhi_done", "omhi_done", "pad_done",
           "pick_loaded", "pn_done", "prod_done", "ps_clear", "ps_done", "pt_done", "pti_loaded", "pv_done",
           "qc_done", "qd_clear", "qd_done", "qk_done", "qn_done", "qnhi_done", "qnlo_done", "qpe_done", "rexp_done",
           "rk_done", "rs_done", "rsg_done", "sc_done", "selw_done", "sqf_done", "sqg_done", "sqs_done", "sqy_done",
           "ssk_done", "ssx2_done", "ssx_done", "stat_clear", "states_loaded", "sumf_done", "sumy_done", "tf_done",
           "wexp_done", "wuv_kept", "x2_loaded", "xhi_done", "xn_done", "yT_done", "y_half", "y_out"]
SIGNALS += [f"kc_loaded{i}" for i in range(4)]

LAST = {0: "cq1", 1: "cq2", 2: "tok4", 3: "kr", 4: "q1", 5: "k1", 6: "v4", 7: "v9", 8: "g1", 9: "g3", 10: "qp0",
        11: "qp1", 12: "vm4", 13: "wo1", 14: "wo3", 15: "wo5", 16: "wo7", 17: "ffn1", 18: "ffn3"}

def reads(n):
    return sum(m not in IDLE for m in range(n % 4, n, 4))


def last_g(c):
    return f"G{NL}.{c}"


def last_of_level(lv):
    return f"G{lv}.{4 if lv == NL or LEVELS[lv] <= 8 else 3}"


def fills(name):
    return sum(v <= PLAN[name] and k[0] != "-" and not k.startswith("cache") for k, v in PLAN.items())


LOADS = []
for _n in range(B_DOWN + 12):
    _k = len(BLOCKS[_n]) if _n < B_FFN else 1
    LOADS.append(_k + (LOADS[_n - 2] if _n >= 2 else 0))


def hybrid_decode_kernel(nc, ins, outs):
    (x_prompt, x_sample, cache_ckv, cache_kpe, state_gla, page_table, meta_tokens, norm_mix, w_in, w_gk, b_gk,
     gla_norm, q_norm, kv_norm, w_uq, w_ukv, w_out, norm_ffn, w_gate, w_up, w_down, norm_final,
     c_all, c_masks, c_pick) = ins
    y_prompt, y_sample, ckv_p, kpe_p, gla_p, ckv_s, kpe_s, gla_s = outs
    weights = {"w_in": w_in[0], "w_uq": w_uq[0], "w_ukv": w_ukv[0], "w_out": w_out[0], "w_gate": w_gate[0],
               "w_up": w_up[0], "w_down": w_down[0]}
    with ExitStack() as ctx:
        top = [0]
        arena_bytes = 212000
        nc_base = nc.sbuf_base
        ctx.enter_context(nc.sbuf_tensor("arena", [P, arena_bytes // 4], F32))
        arena_at = -(-nc_base // 32) * 32

        def sb(name, shape, dt=F32, at=None):
            n = 4
            for d in shape[1:]:
                n *= d
            off = top[0] if at is None else at
            if at is None:
                top[0] = -(-(off + n) // 32) * 32
            assert off + n <= arena_bytes, (name, off, n)
            return nc.alloc_sbuf_tensor_at(name, shape, dt, offset=arena_at + off)

        xhi = sb("xhi", [P, KD, TPAD], F32R)
        xlo = sb("xlo", [P, KD, TPAD], F32R)
        wraw_at = top[0]
        wraw = [sb(f"wraw{i}", [P, 2048]) for i in range(2)]
        whi_at = top[0]
        whi = [sb(f"whi{i}", [P, 2048], F32R) for i in range(2)]
        wlo = [sb(f"wlo{i}", [P, 2048], F32R) for i in range(2)]
        cst_at = top[0]
        cst = sb("cst", [P, NCONST])
        nrm = sb("nrm", [P, 3 * KD + 4])
        keep = top[0]
        hT = sb("hT", [P, KD, T])
        gq = sb("gq", [P, 2, T], at=keep)
        gk = sb("gk", [P, 2, T], at=keep + 8 * T)
        gT = sb("gT", [P, 4, T], at=keep + 16 * T)
        hid_at = top[0]
        stat = sb("stat", [P, 64])
        vtok = sb("vtok", [P, NT, 512])
        grT = sb("grT", [32, T])
        x2_at = top[0]
        Qall = sb("Qall", [P, NB, NBLK * 32])
        wuv = sb("wuv", [P, 2, 4, 128])
        cks = sb("cks", [P, 2, NB])
        qlT = sb("qlT", [P, 2, 4, NB])
        fin_at = top[0]
        fin = sb("fin", [P, 640])
        el_at = top[0]
        el = sb("el", [P, 2, NT])
        eb = sb("eb", [P, 2, NB])
        wgk = sb("wgk", [32, 256])
        W0 = top[0]
        X = sb("X", [P, NT, D], at=W0)
        cq = sb("cq", [P, 3, T], at=W0)
        knT = sb("knT", [P, 4, T], at=W0)
        a = W0 + 16 * T
        qnhi = sb("qnhi", [P, 3, T], F32R, at=a)
        qnlo = sb("qnlo", [P, 3, T], F32R, at=a + 12 * T)
        vm = sb("vm", [P, NT, 512], at=a)
        a += 24 * T
        ctok = sb("ctok", [P, NT, 384], at=a)
        a += NT * 384 * 4
        kpT = sb("kpT", [P, T], at=a)
        a += 4 * T
        ckhi = sb("ckhi", [P, 2, TPAD], F32R, at=a)
        cklo = sb("cklo", [P, 2, TPAD], F32R, at=a + 8 * TPAD)
        krT = sb("krT", [ROPE, TPAD], at=a)
        rp = [sb(f"rp{i}", [P, NT, ROPE], at=a + 8 * TPAD + 4 * TPAD * i) for i in range(2)]
        pr = [sb(f"pr{i}", [P, NP], at=a + 4 * NP * i) for i in range(2)]
        pt = [sb(f"pt{i}", [P, NT, P], at=a + 8 * NP + 4 * NT * P * i) for i in range(2)]
        a += 16 * TPAD
        qnT = sb("qnT", [P, 4, T], at=a)
        a += 16 * T
        qpe = sb("qpe", [P, 2, T], at=a)
        a += 8 * T
        sqs = sb("sqs", [P, 3, T], at=a - 24 * T)
        rsb = sb("rsb", [P, T], at=a)
        kvn = sb("kvn", [P, KVL], at=a + 4 * T)
        a += 4 * T + 4 * KVL
        prod = sb("prod", [P, 3, 4, NB], at=a + 832)
        scr = sb("scr", [P, D], at=a + 1216)
        wukT = sb("wukT", [P, 4, 256], at=a + 1216)
        KC = [sb(f"KC{i}", [P, UNITS * KVL], at=whi_at + 16384 * i if i < 2 else W0 + 16384 * (i - 2)) for i in range(4)]
        KP = [sb(f"KP{i}", [P, UNITS * ROPE], at=4 * KD * TPAD + 4096 * i if i < 2 else W0 + 32768 + 4096 * (i - 2))
              for i in range(4)]
        b0 = W0 + 40960
        KT = [sb("KT0", [P, UNITS, 8, 32], at=b0), sb("KT1", [P, UNITS, 8, 32], at=wraw_at)]
        KTp = [[sb(f"KTp{i}{y}", [P, UNITS // 2, 2, 32], at=at) for y, at in enumerate(ats)] for i, ats in
               enumerate(((b0 + 16384, b0 + 18432), (b0 + 20480, 4 * KD * TPAD + 8192)))]
        assert b0 + 22528 <= arena_bytes
        Oall = sb("Oall", [P, NB, KVL], at=0)
        b1 = cst_at + 4 * CC["cosf"][0]
        assert 6400 <= 8 * T + 8 * NT * ROPE
        PS = [sb(f"PS{i}", [P, UNITS, 32], at=b1 + 2048 * i) for i in range(2)]
        Pc = sb("Pc", [P, P], at=b1 + 4096)
        Pt = sb("Pt", [P, 4, 32], at=b1 + 4608)
        Qc = [sb("Qc0", [P, NBLK * 32], at=b1 + 5120), sb("Qc1", [P, NBLK * 32], at=4 * NB * KVL)]
        sn8, mx8, w8, den8, r8, wn8 = (fin[0:NB, 4 * i:4 * i + 4] for i in range(6))
        mexp, rexp, wx8 = fin[0:NB, 24:152], fin[0:NB, 324:452], fin[0:NB, 152:184]
        Mc, Lc, Wc = (fin[:, o:o + 16].rearrange("p (e b) -> p e b", e=2) for o in (184, 200, 216))
        wvb, ML, mc = fin[:, 232:264], fin[:, 264:312], fin[:, 312:324]
        idx = sb("idx", [P, NB, CHUNKS], I32, at=fin_at + 4 * 456)
        pti = sb("pti", [P, NB], I32, at=fin_at + 4 * 472)
        icur = [sb(f"icur{i}", [P, 1], I32, at=fin_at + 32 * (60 + i)) for i in range(4)]
        selw = sb("selw", [P, NB, 32], at=x2_at)
        osb = sb("osb", [P, 2, KVL], at=x2_at + 1024)
        olat = sb("olat", [P, 2, NB * 4], at=x2_at + 3072)
        otmp = sb("otmp", [P, 2, NB * 4], at=x2_at + 3328)
        a = W0
        lgs = sb("lgs", [P, NT, 256], at=a)
        a += NT * 256 * 4
        bT = sb("bT", [P, 2, T], at=a)
        a += 8 * T
        Ee = [sb(f"Ee{i}", [P, 2, NP], at=a + 8 * NP * i) for i in range(2)]
        QD = [sb(f"QD{i}", [P, 2, 2 * NP], at=whi_at + 16384 * i) for i in range(2)]
        kt = [sb(f"kt{i}", [P, 2, NP], at=a + 8 * NP * (5, 2)[i]) for i in range(2)]
        qe = sb("qe", [P, 2, NP], at=a + 24 * NP)
        qd = sb("qd", [P, NB, 2, 32], at=a + 32 * NP)
        od = sb("od", [P, 2, 2, P], at=a + 32 * NP + 2048)
        oT = sb("oT", [P, 4, T], at=a)
        lgt = sb("lgt", [P, NT, 256], at=a)
        a += 48 * NP
        at_at = a
        AT = sb("AT", [P, NT, 4, P], at=a)
        a += NT * 4 * P * 4
        msk = sb("msk", [P, NL + 1, P], I32, at=a)
        a += 4 * P * (NL + 1)
        Sst = [sb("Sst0", [P, 2, P], at=a), sb("Sst1", [P, 2, P], at=cst_at + 4 * CC["cosf"][0] + 4096)]
        a += 8 * P
        states = sb("states", [P, NB, 2, P], at=a)
        a += 8 * NB * P
        ktok = sb("ktok", [P, 2, P], at=a)
        a += 8 * P
        pick = sb("pick", [24, NB, P], at=cst_at + 4 * CC["cosf"][0])
        X2 = [sb(f"X2_{i}", [P, D], at=x2_at + 4 * D * i if i < 4 else a) for i in range(NT)]
        assert x2_at + 16 * D <= el_at
        sqg = [sb(f"sqg{i}", [P, T], at=W0 + 4 * T * i) for i in range(4)]
        rsg = [sb(f"rsg{i}", [P, T], at=at_at + 4 * T * i) for i in range(4)]
        sqf = sb("sqf", [P, KD, T], at=W0 + 20480)
        rsf = sb("rsf", [P, T], at=W0)
        tf = [sb(f"tf{i}", [P, T], at=W0 + 4 * T * (1 + i)) for i in range(2)]
        hhi = sb("hhi", [P, KF, T], F32R, at=hid_at)
        hlo = sb("hlo", [P, KF, T], F32R, at=hid_at + 4 * KF * T)
        f0 = cst_at + 4 * CC["cosf"][0]
        fe = [sb(f"fe{i}", [P, T], at=f0 + 4 * T * i) for i in range(2)]
        sqy = sb("sqy", [P, KD, T], at=0)
        yT = sb("yT", [P, KD, T], at=4 * KD * TPAD)
        rsy = sb("rsy", [P, T], at=hid_at)
        ysb = [sb(f"ysb{i}", [P, D], at=hid_at + 4 * T + 4 * D * i) for i in range(NT)]

        pairs = [ctx.enter_context(nc.psum_tensor(f"pair{i}", [P, 1024], F32)) for i in range(4)]

        def sem(name):
            return ctx.enter_context(nc.semaphore(name))

        pe_done = sem("pe_done")
        pair_free = [sem(f"pair_free{i}") for i in range(4)]
        w_loaded = [sem(f"w_loaded{i}") for i in range(2)]
        w_hi, w_lo = sem("w_hi"), sem("w_lo")
        x_loaded = [sem(f"x_loaded{i}") for i in range(NT)]
        c_loaded, n_loaded, small_loaded = sem("c_loaded"), sem("n_loaded"), sem("small_loaded")
        out_done = sem("out_done")
        dve_chain, act_chain, pool_chain = sem("dve_chain"), sem("act_chain"), sem("pool_chain")
        signals = {name: sem(name) for name in SIGNALS}

        def S(name):
            return signals[name]

        block = ctx.enter_context(nc.Block())

        def C(name, rows=P):
            return cst[0:rows, CC[name][0]:CC[name][1]]

        ident, ones = C("ident"), C("ones")

        def halves(ap):
            return ap[:, :].rearrange("p (a t) -> p a t", a=2)[:, :, 0:TH]

        def split2(ap):
            return ap.rearrange("p (a t) -> p a t", a=2)

        def block_size(n):
            return BLOCKS[n][0][2] * sum(p[4] for p in BLOCKS[n]) if n < B_FFN else 256 * KD

        def view(bufs, n, k=None):
            k = k or BLOCKS[n][0][2]
            w = sum(p[4] for p in BLOCKS[n]) if n < B_FFN else 256
            return bufs[n % 2][:, 0:k * w].rearrange("p (k n) -> p k n", n=w)

        @block.sync
        def _(sp):
            def load_x(dst, sems):
                for i in range(NT):
                    if i == 0:
                        sp.dma_start(dst[0][0:NMETA, :], meta_tokens).then_inc(sems[0], 16)
                        sp.dma_start(dst[0][NMETA:P, :], x_prompt[0, 0:P - NMETA, :]).then_inc(sems[0], 16)
                    elif i < 4:
                        sp.dma_start(dst[i], x_prompt[0, P * i - NMETA:P * (i + 1) - NMETA, :]).then_inc(sems[i], 16)
                    else:
                        sp.dma_start(dst[4][0:NMETA, :], x_prompt[0, SEQ - NMETA:SEQ, :]).then_inc(sems[4], 16)
                        sp.dma_start(dst[4][NMETA:NMETA + NB, :], x_sample[:, 0, :]).then_inc(sems[4], 16)

            load_x([X[:, i, :] for i in range(NT)], x_loaded)
            sp.dma_start(cst[:, :], c_all).then_inc(c_loaded, 16)

            def load_block(n):
                if n >= 2:
                    sp.wait_ge(w_lo, n - 1)
                if n == B_UKV + 2:
                    sp.wait_ge(pe_done, fills("wuk1"))
                    sp.wait_ge(S("wuv_kept"), 1)
                c0 = 0
                w = sum(p[4] for p in BLOCKS[n])
                k = BLOCKS[n][0][2]
                for name, k0, kk, col, cols in BLOCKS[n]:
                    dst = wraw[n % 2][:, 0:k * w].rearrange("p (k n) -> p k n", n=w)[:, :, c0:c0 + cols]
                    src = weights[name][P * k0:P * (k0 + kk), col:col + cols].rearrange("(k p) n -> p k n", p=P)
                    sp.dma_start(dst, src).then_inc(w_loaded[n % 2], 16)
                    c0 += cols

            for n in range(B_UKV):
                load_block(n)
                if n == 7:
                    for width, dst_p, dst_s, col in ((KVL, ckv_p, ckv_s, 0), (ROPE, kpe_p, kpe_s, KVL)):
                        for i in range(NT):
                            sp.wait_ge(S("ctok_done"), i + 1 if col == 0 else NT + 1)
                            r = min(TT[i], NP - P * i)
                            sp.dma_start(dst_p[0, 0, P * i:P * i + r, :], ctok[0:r, i, col:col + width]).then_inc(out_done, 16)
                        sp.dma_start(dst_s[0, :, 0, :], ctok[r:r + NB, NT - 1, col:col + width]).then_inc(out_done, 16)
            load_block(B_UKV)
            sp.wait_ge(S("pv_done"), CHUNKS * NB)
            sp.dma_start(msk[:, :, :].rearrange("p a b -> p (a b)"), c_masks).then_inc(S("msk_loaded"), 16)
            for b in range(NB):
                for pp in range(2):
                    sp.dma_start(states[:, b, pp, :], state_gla[0, b, 2 * pp:2 * pp + 2].rearrange("a k v -> (a k) v")
                                 ).then_inc(S("states_loaded"), 16)
            load_block(B_OUT)
            load_block(B_OUT + 1)
            sp.dma_start(pick[:, :, :].rearrange("p a b -> p (a b)"), c_pick).then_inc(S("pick_loaded"), 16)
            sp.wait_ge(pair_free[PLAN["omd"] % 4], reads(PLAN["omd"]) + 1)
            load_x([t[:, :] for t in X2], [S("x2_loaded")] * NT)
            sp.wait_ge(pair_free[PLAN["vb7"] % 4], reads(PLAN["vb7"]) + 1)
            for b in range(NB):
                for pp in range(2):
                    sp.dma_start(gla_s[0, b, 2 * pp:2 * pp + 2].rearrange("a k v -> (a k) v"), states[:, b, pp, :]
                                 ).then_inc(out_done, 16)
            sp.wait_ge(pair_free[PLAN["s4"] % 4], reads(PLAN["s4"]) + 1)
            for pp in range(2):
                sp.dma_start(gla_p[0, 0, 2 * pp:2 * pp + 2].rearrange("a k v -> (a k) v"), Sst[(NT - 1) % 2][:, pp, :]).then_inc(out_done, 16)
            load_block(B_OUT + 2)
            load_block(B_OUT + 3)
            with sp.Fori(0, DFF // 256) as j:
                for s, name in ((0, "w_gate"), (1, "w_up")):
                    slot = (B_FFN + s) % 2
                    sp.wait_ge(w_lo, (B_FFN + s - 1) + 2 * j)
                    src = weights[name].rearrange("(k p) n -> p k n", p=P)[:, :, bass.ds(256 * j, 256)]
                    sp.dma_start(wraw[slot][:, :].rearrange("p (k n) -> p k n", n=256), src).then_inc(w_loaded[slot], 16)
            with sp.Fori(0, 2) as j:
                for cb in range(2):
                    for q, (k0, kk) in enumerate(DPARTS):
                        n = B_DOWN + 3 * cb + q
                        sp.wait_ge(w_lo, (n - 1) + 6 * j)
                        src = weights["w_down"][P * k0:P * (k0 + kk), :].rearrange("(k p) n -> p k n", p=P)[:, :, bass.ds(512 * j + 256 * cb, 256)]
                        sp.dma_start(wraw[n % 2][:, 0:256 * kk].rearrange("p (k n) -> p k n", n=256), src).then_inc(w_loaded[n % 2], 16)
            for i in range(NT):
                sp.wait_ge(pair_free[PLAN[f"y{i}"] % 4], reads(PLAN[f"y{i}"]) + 1)
                y = ysb[i]
                if i == 0:
                    sp.dma_start(y_prompt[0, 0:P - NMETA, :], y[NMETA:P, :]).then_inc(S("y_out"), 16)
                elif i < 4:
                    sp.dma_start(y_prompt[0, P * i - NMETA:P * (i + 1) - NMETA, :], y[:, :]).then_inc(S("y_out"), 16)
                else:
                    sp.dma_start(y_prompt[0, SEQ - NMETA:SEQ, :], y[0:NMETA, :]).then_inc(S("y_out"), 16)
                    sp.dma_start(y_sample[:, 0, :], y[NMETA:NMETA + NB, :]).then_inc(S("y_out"), 16)
            sp.wait_ge(S("y_out"), 16 * (NT + 1))
            sp.wait_ge(out_done, 16 * (12 + 2 + 16))

        @block.gpsimd
        def _(pool):
            g = nc.gpsimd
            chain = [0]

            def link(ins):
                chain[0] += 1
                ins.then_inc(pool_chain, 1)
                pool.wait_ge(pool_chain, chain[0])

            with nc.allow_non_contiguous_dma("vectors by feature"):
                for j, v in enumerate((norm_mix[0], norm_ffn[0], norm_final)):
                    pool.dma_start(nrm[:, KD * j:KD * j + KD], v.rearrange("(k p) -> p k", p=P)).then_inc(n_loaded, 16)
                pool.dma_start(nrm[:, 3 * KD:3 * KD + 3], q_norm[0].rearrange("(k p) -> p k", p=P)).then_inc(n_loaded, 16)
                pool.dma_start(nrm[:, 3 * KD + 3:3 * KD + 4], gla_norm[0].rearrange("(k p) -> p k", p=P)).then_inc(n_loaded, 16)
                link(g.memset(wgk[:, :], 0.0))
                pool.dma_start(wgk[0:RANK, :], w_gk[0]).then_inc(small_loaded, 16)
                pool.dma_start(wgk[RANK:RANK + 1, :], b_gk).then_inc(small_loaded, 16)
                pool.dma_start(kvn[:, :], kv_norm[0].partition_broadcast(P)).then_inc(small_loaded, 16)
            with nc.allow_non_contiguous_dma("page table"):
                for q in range(4):
                    pool.dma_start(pti[q:P:4, :], page_table.rearrange("b n -> n b")).then_inc(S("pti_loaded"), 16)
            g.memset(xhi[:, :, T:TPAD].bitcast(F32), 0.0).then_inc(S("pad_done"), 1)
            g.memset(xlo[:, :, T:TPAD].bitcast(F32), 0.0).then_inc(S("pad_done"), 1)
            g.memset(grT[:, :], 1.0).then_inc(S("pad_done"), 1)
            g.memset(Qall[:, :, :], 0.0).then_inc(S("Qall_clear"), 1)
            pool.wait_ge(w_loaded[B_UKV % 2], 16 * LOADS[B_UKV])
            ins = g.tensor_copy(wuv[:, :, :, :], wraw[B_UKV % 2][:, :].rearrange("p (k h n) -> p k h n", k=2, h=4)[:, :, :, NOPE:256])
            ins.then_inc(S("wuv_kept"), 1)
            pool.wait_ge(S("wuv_kept"), 1)
            pool.wait_ge(S("pti_loaded"), 64)
            link(g.tensor_scalar(idx[:, :, 0], pti[:, :], 8.0, C("quart"), ALU.mult, ALU.add))
            link(g.tensor_scalar(idx[:, :, 1], idx[:, :, 0], 1.0, 0.0, ALU.add, ALU.add))
            ckv_rows = cache_ckv[0].rearrange("n (s k) r -> (n s) (k r)", k=UNITS)
            kpe_rows = cache_kpe[0].rearrange("n (s k) r -> (n s) (k r)", k=UNITS)

            def gather(n):
                x = n % 4
                if n == 0:
                    pool.wait_ge(pe_done, fills("vm4"))
                if n == 2:
                    pool.wait_ge(pair_free[PLAN["OM19"] % 4], reads(PLAN["OM19"]) + 1)
                    pool.wait_ge(out_done, 16 * 12)
                if n >= 4:
                    pool.wait_ge(S("pv_done"), n - 3)
                    pool.wait_ge(S("kt_done"), n - 3)
                link(g.tensor_copy(icur[x][:, :], idx[:, n // 2, n % 2:n % 2 + 1]))
                g.indirect_dma_start(KC[x][:, :], None, ckv_rows, bass.IndirectOffsetOnAxis(icur[x][:, 0:1], 0)).then_inc(S(f"kc_loaded{x}"), 16)
                g.indirect_dma_start(KP[x][:, :], None, kpe_rows, bass.IndirectOffsetOnAxis(icur[x][:, 0:1], 0)).then_inc(S(f"kc_loaded{x}"), 16)

            pool.wait_ge(S("qpe_done"), 1)
            g.memset(PS[0][:, :, :], 0.0).then_inc(S("ps_clear"), 1)
            g.memset(PS[1][:, :, :], 0.0).then_inc(S("ps_clear"), 1)
            for n in range(CHUNKS * NB):
                gather(n)
            pool.wait_ge(S("pv_done"), CHUNKS * NB)
            for x in range(4):
                pool.wait_ge(S(f"kc_loaded{x}"), 32 * CHUNKS * NB // 4)
            for t in (QD[0][:, :, :], QD[1][:, :, :], AT[:, :, :, :]):
                g.memset(t, 0.0).then_inc(S("clear_done"), 1)
            pool.wait_ge(S("clear_done"), 3)

            def differences(lv):
                s = LEVELS[lv]
                n = 512 if s > 8 else NP
                nb = n // (2 * s)
                if lv >= 2:
                    pool.wait_ge(S("qk_done"), lv - 1)
                for q in range(2):
                    bb = bT[:, q, 0:n].rearrange("p (n a s) -> p n a s", a=2, s=s)
                    ee = Ee[lv % 2][:, q, 0:n].rearrange("p (n a s) -> p n a s", a=2, s=s)
                    mid = bb[:, :, 0, s - 1:s].broadcast_to([P, nb, s])
                    g.tensor_tensor(ee[:, :, 0, :], mid, bb[:, :, 0, :], ALU.subtract).then_inc(S("diffp_done"), 1)
                    pool.wait_ge(S("diffp_done"), 2 * lv + q + 1)

            for c in range(NT):
                pool.wait_ge(pair_free[PLAN[f"b{c}"] % 4], reads(PLAN[f"b{c}"]) + 1)
            differences(0)
            for lv in range(NL):
                n = 512 if LEVELS[lv] > 8 else NP
                if lv + 1 < NL:
                    differences(lv + 1)
                pool.wait_ge(S("E_done"), lv + 1)
                if lv >= 2:
                    pool.wait_ge(pe_done, fills(last_of_level(lv - 2)))
                g.tensor_tensor(kt[lv % 2][:, :, 0:n], gk[:, :, 0:n], Ee[lv % 2][:, :, 0:n], ALU.mult).then_inc(S("kd_done"), 1)
                pool.wait_ge(S("kd_done"), lv + 1)

        @block.tensor
        def _(pe):
            mm = nc.tensor.matmul

            def take(name):
                n = PLAN[name]
                if n >= 4:
                    pe.wait_ge(pair_free[n % 4], reads(n))
                return pairs[n % 4]

            def evacuated(name):
                pe.wait_ge(pair_free[PLAN[name] % 4], reads(PLAN[name]) + 1)

            def use(n):
                pe.wait_ge(w_lo, n + 1)

            def done(ins):
                ins.then_inc(pe_done, 1)

            def dense(ps, h, l, wcols, k_of, hi, lo, first=True, last=True):
                ins = None
                for half in range(2):
                    out = ps[:, 512 * half:512 * half + TH]
                    tok = slice(TH * half, TH * half + TH)
                    for j, kx in enumerate(k_of):
                        mm(out, wcols(h, j), hi[:, kx, tok], start=first and j == 0, stop=False)
                        mm(out, wcols(h, j), lo[:, kx, tok], start=False, stop=False)
                        ins = mm(out, wcols(l, j), hi[:, kx, tok], start=False, stop=last and j == len(k_of) - 1)
                return ins

            def two_layers(ps, n, part):
                h, l = view(whi, n, KD), view(wlo, n, KD)
                for k in range(KD):
                    part(k)
                    for m in range(2):
                        for half in range(2):
                            out = ps[m][:, 512 * half:512 * half + TH]
                            tok = slice(TH * half, TH * half + TH)
                            c = slice(P * m, P * m + P)
                            mm(out, h[:, k, c], xhi[:, k, tok], start=k == 0, stop=False)
                            mm(out, h[:, k, c], xlo[:, k, tok], start=False, stop=False)
                            ins = mm(out, l[:, k, c], xhi[:, k, tok], start=False, stop=k == KD - 1)
                        if k == KD - 1:
                            done(ins)

            def cols(c):
                return lambda ap, j: ap[:, j, c:c + P]

            def layer(name, n, c, K, hi, lo):
                done(dense(take(name), view(whi, n), view(wlo, n), cols(c), list(range(K)), hi, lo))

            def by_token(out, i, n, K, wcols, hi, lo):
                h, l = view(whi, n), view(wlo, n)
                tok = slice(P * i, P * i + P)
                ins = None
                for j in range(K):
                    mm(out, hi[:, j, tok], wcols(h, j), start=j == 0, stop=False)
                    mm(out, lo[:, j, tok], wcols(h, j), start=False, stop=False)
                    ins = mm(out, hi[:, j, tok], wcols(l, j), start=False, stop=j == K - 1)
                return ins

            def ones_sum(ps, src):
                ins = None
                for half in range(2):
                    for k, s in enumerate(src):
                        ins = mm(ps[:, 512 * half:512 * half + TH], ones, s[:, TH * half:TH * half + TH],
                                 start=k == 0, stop=k == len(src) - 1)
                return ins

            pe.wait_ge(c_loaded, 16)
            pe.wait_ge(S("xn_done"), NT)
            for k in range(KD):
                ps = take(f"xT{k}")
                for i in range(NT):
                    ins = nc.tensor.transpose(ps[:, P * i:P * i + TT[i]], X[0:TT[i], i, P * k:P * k + P],
                                              C("ident", TT[i])[:, 0:TT[i]])
                done(ins)
            pe.wait_ge(S("pad_done"), 3)
            use(0)
            two_layers([take("cq0"), take("cq1")], 0, lambda k: evacuated(f"xT{k}"))
            use(1)
            layer("cq2", 1, 0, KD, xhi, xlo)
            use(2)
            for i in range(NT):
                done(by_token(take(f"tok{i}")[:, 0:KVL], i, 2, KD, lambda a, j: a[:, j, :], xhi, xlo))
            use(3)
            layer("kr", 3, 0, KD, xhi, xlo)
            pe.wait_ge(S("sqs_done"), 3)
            done(ones_sum(take("ssq"), [sqs[:, k, :] for k in range(3)]))
            for n, name in ((4, "q"), (5, "k")):
                use(n)
                for m in range(2):
                    layer(f"{name}{m}", n, P * m, KD, xhi, xlo)
                if n == 4:
                    ps = take("kp")
                    evacuated("kr")
                    for i in range(NT):
                        ins = nc.tensor.transpose(ps[:, ROPE * i:ROPE * i + ROPE], krT[:, P * i:P * i + P], C("ident", ROPE)[:, 0:ROPE])
                    done(ins)
            for x in range(2):
                use(6 + x)
                for i in range(NT):
                    done(by_token(take(f"v{NT * x + i}")[:, 0:256], i, 6 + x, KD, lambda a, j: a[:, j, :], xhi, xlo))
            for m in range(4):
                if m % 2 == 0:
                    use(8 + m // 2)
                layer(f"g{m}", 8 + m // 2, P * (m % 2), KD, xhi, xlo)
            pe.wait_ge(S("ctok_done"), NT + 1)
            for j in range(3):
                ps = take(f"ck{j}")
                for i in range(NT):
                    ins = nc.tensor.transpose(ps[:, P * i:P * i + TT[i]], ctok[0:TT[i], i, P * j:P * j + P],
                                              C("ident", TT[i])[:, 0:TT[i]])
                done(ins)
            pe.wait_ge(S("qnlo_done"), 1)
            for hh in range(2):
                n = B_UQ + hh
                use(n)
                for x in range(2):
                    layer(f"qn{2 * hh + x}", n, P * x, 3, qnhi, qnlo)
                done(dense(take(f"qp{hh}"), view(whi, n), view(wlo, n), cols(2 * P), list(range(3)), qnhi, qnlo))
            for hh in range(2):
                ps = take(f"sw{hh}")
                evacuated(f"qp{hh}")
                for half in range(2):
                    ins = mm(ps[:, 512 * half:512 * half + TH], C("swap"), qpe[:, hh, TH * half:TH * half + TH], start=True, stop=True)
                done(ins)
            use(B_UKV)
            pe.wait_ge(S("cklo_done"), 2)
            for h in range(MH):
                layer(f"kn{h}", B_UKV, 256 * h, 2, ckhi, cklo)
            for i in range(NT):
                ps = take(f"vm{i}")
                done(by_token(ps[:, 0:512].rearrange("p (h v) -> p h v", h=4), i, B_UKV, 2,
                              lambda a, j: a[:, j, :].rearrange("p (h c) -> p h c", h=4)[:, :, NOPE:256], ckhi, cklo))
            raw = wraw[B_UKV % 2][:, :].rearrange("p (k h c) -> p k h c", k=2, h=4)
            for x in range(2):
                ps = take(f"wuk{x}")
                for y in range(2):
                    for rh in range(2):
                        o = P * (2 * y + rh)
                        ins = nc.tensor.transpose(ps[:, o:o + P], raw[:, rh, 2 * x + y, 0:NOPE], ident)
                done(ins)
            ps = take("qlat")
            evacuated("qn3")
            evacuated("wuk1")
            for rh in range(2):
                for h in range(4):
                    o = 32 * rh + 8 * h
                    ins = mm(ps[:, o:o + 8], wukT[:, h, P * rh:P * rh + P], qnT[:, h, NP:T], start=True, stop=True)
            done(ins)
            ps = take("snew")
            pe.wait_ge(S("prod_done"), 1)
            for h in range(4):
                for x in range(3):
                    ins = mm(ps[0:NB, h:h + 1], prod[:, x, h, :], ones[:, 0:1], start=x == 0, stop=x == 2)
            done(ins)
            U = NT * MH
            for u in range(U + 2):
                if u < U:
                    qb, h = divmod(u, MH)
                    a, q0, nq = h % 2, P * qb, min(P, NP - P * qb)
                    nk = min(q0 + P, NP)
                    ps = take(f"S{u}")
                    for k0, k1 in ((0, min(nk, 512)), (512, nk)):
                        if k1 > k0:
                            mm(ps[0:nq, k0:k1], qnT[:, h, q0:q0 + nq], knT[:, h, k0:k1], start=True, stop=False)
                            ins = mm(ps[0:nq, k0:k1], qpe[64 * a:64 * a + 64, h // 2, q0:q0 + nq], kpT[64 * a:64 * a + 64, k0:k1],
                                     start=False, stop=True)
                    done(ins)
                if 1 <= u <= U:
                    v = u - 1
                    qb, h = divmod(v, MH)
                    nq = min(P, NP - P * qb)
                    ps = take(f"PT{v}")
                    pe.wait_ge(S("pn_done"), v + 1)
                    for kb in range(min(qb + 1, 4)):
                        ins = nc.tensor.transpose(ps[:, P * kb:P * kb + nq], pr[v % 2][0:nq, P * kb:P * kb + P], C("ident", nq)[:, 0:nq])
                    if qb == 4:
                        ins = mm(ps[0:16, 512:528], pr[v % 2][0:16, 512:528], C("ident", 16)[:, 0:16], start=True, stop=True)
                    done(ins)
                if u >= 2:
                    v = u - 2
                    qb, h = divmod(v, MH)
                    nq = min(P, NP - P * qb)
                    ps = take(f"OM{v}")
                    evacuated(f"PT{v}")
                    for kb in range(qb + 1):
                        nk = min(P, NP - P * kb)
                        ins = mm(ps[:, 0:nq], vm[0:nk, kb, P * h:P * h + P], pt[v % 2][0:nk, kb, 0:nq], start=kb == 0, stop=kb == qb)
                    done(ins)
            base = PLAN["cache0"]

            def cache_scores(j, x):
                p = 2 * (x % 2)
                pe.wait_ge(S("kt_done"), 4 * j + x + 1)
                pe.wait_ge(pair_free[p], reads(base + p) + 2 * j + x // 2)
                if x % 2 == 0:
                    pe.wait_ge(S("qc_done"), 2 * j + x // 2 + 1)
                for c in range(NBLK):
                    for t in range(NG):
                        u = 4 * (t % 2)
                        kk = KT[(x + 1) % 2][:, 4 * t:4 * t + 4, c, :] if c < 8 else KTp[(x + 1) % 2][t // 2][:, u:u + 4, c - 8, :]
                        ins = mm(pairs[p][32 * t:32 * t + 32, 0:P], Qc[x // 2][:, 32 * c:32 * c + 32], kk, start=c == 0, stop=c == NBLK - 1)
                ins.then_inc(S("sc_done"), 1)

            def cache_values(j, x):
                p = 1 + 2 * (x // 2)
                if x % 2 == 0:
                    pe.wait_ge(pair_free[p], reads(base + p) + j)
                pe.wait_ge(S("ps_done"), 2 * (4 * j + x + 1))
                for y in range(4):
                    for t in range(NG):
                        unit = 4 * t + y
                        ins = mm(pairs[p][32 * t:32 * t + 32, 0:KVL], PS[x % 2][:, unit, :], KC[x][:, KVL * unit:KVL * unit + KVL],
                                 start=x % 2 == 0 and y == 0, stop=x % 2 == 1 and y == 3)
                ins.then_inc(S("pv_done"), 1)

            cache_scores(0, 0)
            with pe.Fori(0, NB // 2 - 1) as j:
                for x in range(4):
                    cache_scores(j + (x + 1) // 4, (x + 1) % 4)
                    cache_values(j, x)
            for x in range(4):
                if x < 3:
                    cache_scores(NB // 2 - 1, x + 1)
                cache_values(NB // 2 - 1, x)
            def gates(i):
                done(mm(take(f"lg{i}")[0:TT[i], 0:256], grT[0:RANK + 1, P * i:P * i + TT[i]], wgk[0:RANK + 1, :], start=True, stop=True))

            def gate_sums(c):
                ps = take(f"b{c}")
                pe.wait_ge(S("lgs_done"), c + 1)
                tri = C("ucum") if c < 4 else C("ucum4", TT[4])
                for q in range(2):
                    ins = mm(ps[:, 512 * q:512 * q + TT[c]], lgs[0:TT[c], c, P * q:P * q + P], tri, start=True, stop=True)
                done(ins)

            ps = take("mt")
            pe.wait_ge(S("mc_done"), 1)
            for e in range(2):
                ins = mm(ps[0:NB, P * e:P * e + P], Mc[:, e, :], ident, start=True, stop=True)
            done(ins)
            gates(0)
            gates(1)
            ps = take("mx")
            pe.wait_ge(S("mexp_done"), 1)
            done(mm(ps[:, 0:NB], mexp, C("ident", NB)[:, 0:NB], start=True, stop=True))
            gates(2)
            gates(3)
            ps = take("den")
            pe.wait_ge(S("lw_done"), 1)
            for e in range(2):
                ins = mm(ps[0:NB, 0:4], Lc[:, e, :], C("sell"), start=e == 0, stop=e == 1)
            done(ins)
            gates(4)
            gate_sums(0)
            gate_sums(1)
            gate_sums(2)
            gate_sums(3)
            gate_sums(4)
            def cache_sum(step):
                if step == 0:
                    ps = take("rb")
                    pe.wait_ge(S("rexp_done"), 1)
                    mm(ps[:, 0:NB], rexp, C("ident", NB)[:, 0:NB], start=True, stop=True)
                    done(mm(ps[:, 512:544], C("ones", NB), wx8, start=True, stop=True))
                if step == 1:
                    ps = take("osum")
                    pe.wait_ge(S("selw_done"), 1)
                    for b in range(NB):
                        r, o = 32 * (b % 4), 512 * (b // 4)
                        ins = mm(ps[r:r + 32, o:o + KVL], selw[:, b, :], Oall[:, b, :], start=True, stop=True)
                    done(ins)
                if step == 2:
                    ps = take("ol")
                    evacuated("osum")
                    for y in range(2):
                        for rh in range(2):
                            o = 512 * y + P * rh
                            ins = nc.tensor.transpose(ps[:, o:o + P], osb[:, y, P * rh:P * rh + P], ident)
                    done(ins)
                if step == 3:
                    ps = take("omd")
                    evacuated("ol")
                    for h in range(4):
                        for rh in range(2):
                            ins = mm(ps[:, 8 * h:8 * h + 8], wuv[:, rh, h, :], olat[:, rh, 8 * h:8 * h + 8], start=rh == 0, stop=rh == 1)
                    done(ins)

            for lv in range(NL + 1):
                if lv < NL:
                    pe.wait_ge(S("qk_done"), lv + 1)
                    pe.wait_ge(S("kd_done"), lv + 1)
                for c in range(NT):
                    if f"G{lv}.{c}" in PLAN:
                        n = min(P, NP - P * c)
                        ps = take(f"G{lv}.{c}")
                        if lv < NL:
                            for q in range(2):
                                ins = mm(ps[0:n, 512 * q:512 * q + 2 * n], kt[lv % 2][:, q, P * c:P * c + n],
                                         QD[lv % 2][:, q, 2 * P * c:2 * P * c + 2 * n], start=True, stop=True)
                        else:
                            for h in (0, 2, 1, 3):
                                a, q = h % 2, h // 2
                                ins = mm(ps[0:n, 512 * a + P * q:512 * a + P * q + n], gk[64 * a:64 * a + 64, q, P * c:P * c + n],
                                         gq[64 * a:64 * a + 64, q, P * c:P * c + n], start=True, stop=True)
                        done(ins)
                for b in NEW_STATES[lv]:
                    ps = take(f"vb{b}")
                    if b == 0:
                        pe.wait_ge(S("pick_loaded"), 16)
                    done(mm(ps[:, 0:512], pick[:, b, :], vtok[0:24, 4, :], start=True, stop=True))
                if lv < 4:
                    cache_sum(lv)
            ps = take("os")
            for b in range(NB - 4, NB):
                evacuated(f"vb{b}")
            pe.wait_ge(S("qd_done"), 1)
            for q in range(2):
                for y in range(2):
                    for b in range(4):
                        o = 256 * y + P * q
                        ins = mm(ps[32 * b:32 * b + 32, o:o + P], qd[:, 4 * y + b, q, :], states[:, 4 * y + b, q, :], start=True, stop=True)
            done(ins)
            ke = kt[(NL + 1) % 2]
            pe.wait_ge(S("qk_done"), NL + 1)
            for c in range(NT + 1):
                if c < NT:
                    n = min(P, NP - P * c)
                    ps = take(f"kt{c}")
                    for q in range(2):
                        ins = mm(ps[0:n, P * q:P * q + P], ke[:, q, P * c:P * c + n], ident, start=True, stop=True)
                    done(ins)
                    ps = take(f"s{c}")
                    evacuated(f"kt{c}")
                    for h in range(4):
                        a, q = h % 2, h // 2
                        ins = mm(ps[64 * a:64 * a + 64, P * q:P * q + P], ktok[0:n, q, 64 * a:64 * a + 64], vtok[0:n, c, P * h:P * h + P],
                                 start=True, stop=True)
                    done(ins)
                if c:
                    v = c - 1
                    n = min(P, NP - P * v)
                    ps = take(f"o{v}")
                    if v == 0:
                        evacuated(last_g(NT - 1))
                    else:
                        evacuated(f"s{v - 1}")
                    for h in (0, 2, 1, 3):
                        a, q = h % 2, h // 2
                        out = ps[:, 512 * a + P * q:512 * a + P * q + n]
                        ins = mm(out, vtok[0:n, v, P * h:P * h + P], AT[0:n, v, 2 * a + q, 0:n], start=True, stop=v == 0)
                        if v:
                            ins = mm(out, Sst[(v - 1) % 2][64 * a:64 * a + 64, q, :], qe[64 * a:64 * a + 64, q, P * v:P * v + n], start=False, stop=True)
                    done(ins)
                if c == 1:
                    ps = take("ot")
                    evacuated("os")
                    for y in range(2):
                        for q in range(2):
                            o = 256 * y + P * q
                            ins = nc.tensor.transpose(ps[:, o:o + P], od[:, y, q, :], ident)
                    done(ins)
            for h in range(4):
                ps = take(f"ssg{h}")
                pe.wait_ge(S("sqg_done"), h + 1)
                done(ones_sum(ps, [sqg[h]]))
            def out_proj(m, part):
                n = B_OUT + m // 2
                h, l = view(whi, n), view(wlo, n)
                k0 = 4 if part == 0 else 0
                cut = lambda ap, j: ap[:, k0 + j, P * (m % 2):P * (m % 2) + P]
                return dense(pairs[PLAN[f"wo{m}"] % 4], h, l, cut, list(range(k0, k0 + 4)), xhi, xlo, first=part == 0, last=part == 1)

            def residual(m):
                ps = take(f"hT{m}")
                for i in range(NT):
                    ins = nc.tensor.transpose(ps[:, P * i:P * i + TT[i]], X2[i][0:TT[i], P * m:P * m + P], C("ident", TT[i])[:, 0:TT[i]])
                done(ins)

            for m in range(4):
                if m % 2 == 0:
                    use(B_OUT + m // 2)
                take(f"wo{m}")
                out_proj(m, 0)
            pe.wait_ge(S("mixlo_done"), 4)
            for m in range(4):
                done(out_proj(m, 1))
            pe.wait_ge(S("x2_loaded"), 16 * (NT + 2))
            for m in range(4):
                residual(m)
            for m in range(4, KD):
                if m % 2 == 0:
                    use(B_OUT + m // 2)
                take(f"wo{m}")
                out_proj(m, 0)
                done(out_proj(m, 1))
                residual(m)
            ps = take("ssf")
            pe.wait_ge(S("sumf_done"), KD - 1)
            done(ones_sum(ps, [sqf[:, 0, :]]))
            base = PLAN["ffn0"]
            with pe.Fori(0, DFF // 256) as j:
                for s in range(2):
                    n = B_FFN + s
                    pe.wait_ge(w_lo, n + 1 + 2 * j)
                    for m in range(2):
                        pe.wait_ge(pair_free[2 * s + m], reads(base + 2 * s + m) + j)
                    two_layers(pairs[2 * s:2 * s + 2], n, lambda k: pe.wait_ge(S("nlo_done"), k + 1) if s == 0 else None)
            base = PLAN["dn0"]
            with pe.Fori(0, 2) as j:
                for cb in range(2):
                    for q, (k0, kk) in enumerate(DPARTS):
                        n = B_DOWN + 3 * cb + q
                        pe.wait_ge(w_lo, n + 1 + 6 * j)
                        pe.wait_ge(S("hlo_done"), k0 + kk)
                        for m in range(2):
                            p = 2 * cb + m
                            if q == 0:
                                pe.wait_ge(pair_free[p], reads(base + p) + j)
                            ins = dense(pairs[p], view(whi, n, kk), view(wlo, n, kk), cols(P * m), list(range(k0, k0 + kk)), hhi, hlo,
                                        first=q == 0, last=q == 2)
                            if q == 2:
                                done(ins)
                        if q < 2:
                            ins.then_inc(S("dn_part"), 1)
            pe.wait_ge(S("yT_done"), KD)
            for i in range(NT + 1):
                if i == 1:
                    ps = take("ssy")
                    pe.wait_ge(S("sumy_done"), KD - 1)
                    for t in range(NT):
                        ins = mm(ps[0:TT[t], t:t + 1], sqy[:, 0, P * t:P * t + TT[t]], ones[:, 0:1], start=True, stop=True)
                    done(ins)
                if i < NT:
                    ps = take(f"y{i}")
                    for k in range(KD):
                        ins = nc.tensor.transpose(ps[0:TT[i], P * k:P * k + P], yT[:, k, P * i:P * i + TT[i]], ident)
                    done(ins)

        @block.scalar
        def _(act):
            f = nc.scalar.activation
            chain = [0]

            def link(ins):
                chain[0] += 1
                ins.then_inc(act_chain, 1)
                act.wait_ge(act_chain, chain[0])

            def ready(name):
                act.wait_ge(pe_done, fills(name))
                return pairs[PLAN[name] % 4]

            def free(ins, name):
                ins.then_inc(pair_free[PLAN[name] % 4], 1)

            def hi(n, size=None):
                act.wait_ge(w_loaded[n % 2], 16 * LOADS[n])
                if n >= 2:
                    act.wait_ge(pe_done, fills(LAST[n - 2]))
                size = size or block_size(n)
                f(whi[n % 2][:, 0:size], wraw[n % 2][:, 0:size], ACT.Copy).then_inc(w_hi, 1)

            act.wait_ge(S("stat_clear"), 1)
            for n, i in enumerate((0, 2, 4)):
                act.wait_ge(x_loaded[i], 32 if i in (0, 4) else 16)
                f(scr[0:TT[i], :], X[0:TT[i], i, :], ACT.Square, accum_out=stat[0:TT[i], i:i + 1]).then_inc(S("ssx_done"), 1)
                act.wait_ge(S("ssx_done"), n + 1)
            act.wait_ge(c_loaded, 16)
            act.wait_ge(S("ssx2_done"), 2)
            link(f(stat[:, 0:NT], stat[:, 0:NT], ACT.Ln, scale=1.0 / D, bias=C("eps")))
            f(stat[:, 8:8 + NT], stat[:, 0:NT], ACT.Exp, scale=-0.5).then_inc(S("rs_done"), 1)
            act.wait_ge(S("rs_done"), 1)
            for i in (3, 4):
                f(X[0:TT[i], i, :], X[0:TT[i], i, :], ACT.Copy, scale=stat[0:TT[i], 8 + i:9 + i]).then_inc(S("xn_done"), 1)
            hi(0)
            act.wait_ge(n_loaded, 16 * 5)
            act.wait_ge(S("pad_done"), 3)
            for k in range(KD):
                ps = ready(f"xT{k}")
                f(xhi[:, k, 0:T], ps[:, 0:T], ACT.Copy, scale=nrm[:, k:k + 1]).then_inc(S("xhi_done"), 1)
                if k == 5:
                    hi(1)
            for m in range(3):
                if m == 2:
                    hi(2)
                act.wait_ge(pair_free[PLAN[f"cq{m}"] % 4], reads(PLAN[f"cq{m}"]) + 1)
                f(sqs[:, m, :], cq[:, m, :], ACT.Square).then_inc(S("sqs_done"), 1)
            hi(3)
            for i in range(NT):
                ps = ready(f"tok{i}")
                f(scr[:, 0:KVL], ps[:, 0:KVL], ACT.Square, accum_out=stat[:, 16 + i:17 + i]).then_inc(S("ssk_done"), 1)
                act.wait_ge(S("ssk_done"), i + 1)
            hi(4)
            act.wait_ge(S("kr_pad"), 1)
            for half in range(2):
                ins = f(krT[:, TH * half:TH * half + TH], ready("kr")[0:ROPE, 512 * half:512 * half + TH], ACT.Copy)
            ins.then_inc(S("kr_done"), 1)
            hi(5)
            link(f(stat[:, 24:24 + NT], stat[:, 16:16 + NT], ACT.Ln, scale=1.0 / KVL, bias=C("eps")))
            f(stat[:, 24:24 + NT], stat[:, 24:24 + NT], ACT.Exp, scale=-0.5).then_inc(S("rk_done"), 1)
            ps = ready("ssq")
            link(f(split2(rsb[:, :]), halves(ps), ACT.Ln, scale=1.0 / QL, bias=C("eps")))
            ins = f(rsb[:, :], rsb[:, :], ACT.Exp, scale=-0.5)
            free(ins, "ssq")
            act.wait_ge(S("qn_done"), 1)
            f(qnhi[:, :, :], cq[:, :, :], ACT.Copy).then_inc(S("qnhi_done"), 1)
            for m in range(2):
                free(f(split2(gq[:, m, :]), halves(ready(f"q{m}")), ACT.Copy, scale=DK ** -0.5), f"q{m}")
            hi(6)
            for m in range(2):
                free(f(split2(gk[:, m, :]), halves(ready(f"k{m}")), ACT.Copy), f"k{m}")
            hi(7)
            for x in range(2):
                for i in range(NT):
                    free(f(vtok[:, i, 256 * x:256 * x + 256], ready(f"v{NT * x + i}")[:, 0:256], ACT.Copy), f"v{NT * x + i}")
                hi(8 + x)
            for m in range(4):
                f(split2(gT[:, m, :]), halves(ready(f"g{m}")), ACT.Exp, scale=-1.0).then_inc(S("ge_done"), 1)
                if m == 1:
                    hi(10)
            hi(11)
            for j in range(2):
                f(ckhi[:, j, 0:T], ready(f"ck{j}")[:, 0:T], ACT.Copy).then_inc(S("ckhi_done"), 1)
            for hh in range(2):
                for x in range(2):
                    free(f(split2(qnT[:, 2 * hh + x, :]), halves(ready(f"qn{2 * hh + x}")), ACT.Copy), f"qn{2 * hh + x}")
                free(f(split2(qpe[:, hh, :]), halves(ready(f"qp{hh}")), ACT.Copy), f"qp{hh}")
                if hh == 0:
                    hi(12)
            for h in range(MH):
                free(f(split2(knT[:, h, :]), halves(ready(f"kn{h}")), ACT.Copy), f"kn{h}")
            for x in range(2):
                free(f(wukT[:, 2 * x:2 * x + 2, :].rearrange("p a b -> p (a b)"), ready(f"wuk{x}")[:, 0:512], ACT.Copy), f"wuk{x}")
            U = NT * MH
            for u in range(U + 2):
                if u < U:
                    qb = u // MH
                    nq, nk = min(P, NP - P * qb), min(P * qb + P, NP)
                    s = 32 + 4 * (u % 2)
                    ps = ready(f"S{u}")
                    act.wait_ge(S("nmax_done"), u + 1)
                    if u >= 2:
                        act.wait_ge(pe_done, fills(f"PT{u - 2}"))
                    free(f(pr[u % 2][0:nq, 0:nk], ps[0:nq, 0:nk], ACT.Exp, scale=SCALE, bias=stat[0:nq, s + 1:s + 2],
                           accum_out=stat[0:nq, s + 2:s + 3]), f"S{u}")
                if 1 <= u <= U:
                    v = u - 1
                    qb = v // MH
                    nq = min(P, NP - P * qb)
                    ps = ready(f"PT{v}")
                    if v >= 2:
                        act.wait_ge(pe_done, fills(f"OM{v - 2}"))
                    nb = min(qb + 1, 4)
                    ins = f(pt[v % 2][:, 0:nb, 0:nq], ps[:, 0:P * nb].rearrange("p (k q) -> p k q", q=P)[:, :, 0:nq], ACT.Copy)
                    if qb == 4:
                        ins = f(pt[v % 2][0:16, 4, 0:16], ps[0:16, 512:528], ACT.Copy)
                    free(ins, f"PT{v}")
                if u >= 2:
                    v = u - 2
                    qb, h = divmod(v, MH)
                    nq = min(P, NP - P * qb)
                    f(xhi[:, 4 + h, P * qb:P * qb + nq], ready(f"OM{v}")[:, 0:nq], ACT.Copy).then_inc(S("omhi_done"), 1)
            act.wait_ge(S("Qall_done"), NG * NG)
            act.wait_ge(S("ps_clear"), 2)

            def queries(b, x):
                f(Qc[x][:, :], Qall[:, bass.ds(b, 1), :].rearrange("p a n -> p (a n)"), ACT.Copy).then_inc(S("qc_done"), 1)

            def cache_softmax(j, x, more=True):
                n = 4 * j + x
                act.wait_ge(S("nm_done"), n + 1)
                f(Pc[:, :], pairs[2 * (x % 2)][:, 0:P], ACT.Exp, scale=SCALE, bias=mc[:, 4 + x:5 + x],
                  accum_out=mc[:, 8 + x:9 + x]).then_inc(pair_free[2 * (x % 2)], 1)
                if x % 2 == 0 and more:
                    queries(2 * j + x // 2 + 1, (x // 2 + 1) % 2)
                act.wait_ge(S("pt_done"), n + 1)
                for t in (0, 1):
                    for gg in range(NG):
                        at = 16 * (x % 2) + 4 * gg
                        ins = f(PS[x % 2][32 * gg:32 * gg + 32, 4 * t:4 * t + 4, at:at + 4], Pt[32 * t:32 * t + 32, :, 4 * gg:4 * gg + 4], ACT.Copy)
                ins.then_inc(S("ps_done"), 1)
                if x % 2 == 1:
                    act.wait_ge(S("pv_done"), n + 1)
                    p = 1 + 2 * (x // 2)
                    f(Oall[:, bass.ds(2 * j + x // 2, 1), :].rearrange("p a n -> p (a n)"), pairs[p][:, 0:KVL], ACT.Copy).then_inc(pair_free[p], 1)

            queries(0, 0)
            with act.Fori(0, NB // 2 - 1) as j:
                for x in range(4):
                    cache_softmax(j, x)
            for x in range(4):
                cache_softmax(NB // 2 - 1, x, more=x < 2)
            def gate_abs(i):
                if i == NT - 1:
                    act.wait_ge(S("lgt_clear"), 1)
                f(lgt[0:TT[i], i, :], ready(f"lg{i}")[0:TT[i], 0:256], ACT.Abs).then_inc(S("lga_done"), 1)

            act.wait_ge(S("d2_done"), 1)
            f(w8, w8, ACT.Exp, scale=SCALE).then_inc(S("wexp_done"), 1)
            gate_abs(0)
            gate_abs(1)
            act.wait_ge(pair_free[PLAN["mx"] % 4], reads(PLAN["mx"]) + 1)
            f(Wc, Wc, ACT.Exp, scale=SCALE).then_inc(S("wexp_done"), 1)
            for i in (2, 3, 4):
                gate_abs(i)
            act.wait_ge(S("lga_done"), NT)
            link(f(lgt[:, :, :], lgt[:, :, :], ACT.Exp, scale=-1.0))
            f(lgt[:, :, :], lgt[:, :, :], ACT.Ln, bias=1.0).then_inc(S("lgt_done"), 1)
            for c in range(NT):
                ps = ready(f"b{c}")
                free(f(bT[:, :, P * c:P * c + TT[c]], ps[:, :].rearrange("p (q t) -> p q t", q=2)[:, :, 0:TT[c]], ACT.Copy), f"b{c}")
            for c in range(NT):
                act.wait_ge(pair_free[PLAN[f"b{c}"] % 4], reads(PLAN[f"b{c}"]) + 1)
            f(eb[:, :, :], bT[:, :, NP:T], ACT.Exp).then_inc(S("eb_done"), 1)
            f(el[:, :, 0:4], bT[:, :, P - 1:4 * P:P], ACT.Exp)
            f(el[:, :, 4:5], bT[:, :, NP - 1:NP], ACT.Exp).then_inc(S("eb_done"), 1)
            for lv in range(NL):
                n = 512 if LEVELS[lv] > 8 else NP
                act.wait_ge(S("diff_done"), lv + 1)
                act.wait_ge(S("diffp_done"), 2 * lv + 2)
                f(Ee[lv % 2][:, :, 0:n], Ee[lv % 2][:, :, 0:n], ACT.Exp).then_inc(S("E_done"), 1)
                if lv == 4:
                    f(xhi[:, 4:8, NP:T], ready("omd")[:, 0:32].rearrange("p (h b) -> p h b", h=4), ACT.Copy).then_inc(S("omdhi_done"), 1)
                if lv == 1:
                    act.wait_ge(S("eb_done"), 2)
                    act.wait_ge(S("states_loaded"), 16 * 2 * NB)
                    for b in range(NB):
                        for q in range(2):
                            ins = f(states[:, b, q, :], states[:, b, q, :], ACT.Copy, scale=eb[:, q, b:b + 1])
                    ins.then_inc(S("decay_done"), 1)
            act.wait_ge(S("qk_done"), NL - 1)
            act.wait_ge(S("kd_done"), NL - 1)
            f(Ee[NL % 2][:, :, :], bT[:, :, 0:NP], ACT.Exp).then_inc(S("E_done"), 1)
            act.wait_ge(S("diff_done"), NL + 1)
            f(Ee[(NL + 1) % 2][:, :, :], Ee[(NL + 1) % 2][:, :, :], ACT.Exp).then_inc(S("E_done"), 1)
            act.wait_ge(S("qk_done"), NL + 1)
            hi(13)
            hi(14)
            free(f(od[:, :, :, :].rearrange("p y q v -> p (y q v)"), ready("os")[:, 0:512], ACT.Copy), "os")
            for c in range(NT + 1):
                if c < NT:
                    n = min(P, NP - P * c)
                    ps = ready(f"kt{c}")
                    if c:
                        act.wait_ge(pe_done, fills(f"s{c - 1}"))
                    free(f(ktok[0:n, :, :], ps[0:n, 0:256].rearrange("p (q d) -> p q d", q=2), ACT.Copy), f"kt{c}")
                if c:
                    v = c - 1
                    n = min(P, NP - P * v)
                    ps = ready(f"o{v}")
                    free(f(oT[:, :, P * v:P * v + n].rearrange("p (q a) t -> p a q t", a=2),
                           ps[:, :].rearrange("p (a q t) -> p a q t", a=2, q=4)[:, :, 0:2, 0:n], ACT.Copy), f"o{v}")
                if c == 1:
                    ps = ready("ot")
                    for y in range(2):
                        src = ps[:, 256 * y:256 * y + 256].rearrange("p (q t c) -> p q c t", q=2, t=4)[:, :, 0:2, :]
                        ins = f(oT[:, :, NP + 4 * y:NP + 4 * y + 4].rearrange("p (q a) t -> p q a t", a=2), src, ACT.Copy)
                    free(ins, "ot")
            act.wait_ge(pair_free[PLAN["o4"] % 4], reads(PLAN["o4"]) + 1)
            act.wait_ge(pair_free[PLAN["ot"] % 4], reads(PLAN["ot"]) + 1)
            for h in range(4):
                f(sqg[h][:, :], oT[:, h, :], ACT.Square).then_inc(S("sqg_done"), 1)
            link(f(rsg[0][0:1, 0:1], ones[0:1, 0:1], ACT.Ln))
            for h in range(4):
                free(f(split2(rsg[h][:, :]), halves(ready(f"ssg{h}")), ACT.Ln, scale=1.0 / DV, bias=C("eps")), f"ssg{h}")
            for h in range(4):
                act.wait_ge(pair_free[PLAN[f"ssg{h}"] % 4], reads(PLAN[f"ssg{h}"]) + 1)
                f(rsg[h][:, :], rsg[h][:, :], ACT.Exp, scale=-0.5).then_inc(S("rsg_done"), 1)
            for h in range(4):
                act.wait_ge(S("og_done"), h + 1)
                f(xhi[:, h, 0:T], oT[:, h, :], ACT.Copy).then_inc(S("mixhi_done"), 1)
            act.wait_ge(S("mixlo_done"), 4)

            def take_out(m):
                free(f(split2(hT[:, m, :]), halves(ready(f"wo{m}")), ACT.Copy), f"wo{m}")

            def square(m):
                act.wait_ge(pair_free[PLAN[f"hT{m}"] % 4], reads(PLAN[f"hT{m}"]) + 1)
                f(sqf[:, m, :], hT[:, m, :], ACT.Square).then_inc(S("sqf_done"), 1)

            for m in range(4):
                take_out(m)
                if m % 2 == 1:
                    hi(15 + m // 2)
            for m in range(4):
                square(m)
            for m in range(4, KD):
                take_out(m)
                if m == 6:
                    hi(17)
                square(m)
            link(f(rsf[0:1, 0:1], ones[0:1, 0:1], ACT.Ln))
            hi(18)
            ps = ready("ssf")
            link(f(split2(rsf[:, :]), halves(ps), ACT.Ln, scale=1.0 / D, bias=C("eps")))
            free(f(rsf[:, :], rsf[:, :], ACT.Exp, scale=-0.5), "ssf")
            for k in range(KD):
                act.wait_ge(S("tf_done"), k + 1)
                f(xhi[:, k, 0:T], tf[k % 2][:, :], ACT.Copy).then_inc(S("nhi_done"), 1)
            act.wait_ge(out_done, 16 * (12 + 2 + 16))
            base = PLAN["ffn0"]
            with act.Fori(0, DFF // 256) as j:
                for m in range(2):
                    act.wait_ge(pe_done, fills("ffn0") + 4 * j + m)
                    if m == 0:
                        act.wait_ge(w_lo, B_FFN + 2 + 2 * j)
                    f(split2(fe[m][:, :]), halves(pairs[m]), ACT.Exp, scale=-1.0).then_inc(S("fe_done"), 1)
                for s in range(2):
                    if s == 1:
                        for m in range(2):
                            act.wait_ge(pair_free[2 + m], reads(base + 2 + m) + 1 + j)
                            f(hhi[:, bass.ds(2 * j + m, 1), :].rearrange("p a t -> p (a t)"), fe[m][:, :], ACT.Copy).then_inc(S("hhi_done"), 1)
                    n = B_FFN + s
                    act.wait_ge(pe_done, fills("ffn0") + 4 * j + 2 * s + 1)
                    act.wait_ge(w_loaded[n % 2], 16 * (LOADS[n] + 1) + 16 * j)
                    f(whi[n % 2][:, :], wraw[n % 2][:, :], ACT.Copy).then_inc(w_hi, 1)
            for cb in range(4):
                for q in range(3):
                    n = B_DOWN + 3 * cb + q + 2
                    if n < B_DOWN + 12:
                        if q < 2:
                            act.wait_ge(S("dn_part"), 2 * cb + q + 1)
                        else:
                            act.wait_ge(pe_done, fills(f"dn{2 * cb + 1}"))
                        act.wait_ge(w_loaded[n % 2], 16 * LOADS[n])
                        size = 256 * DPARTS[(q + 2) % 3][1]
                        f(whi[n % 2][:, 0:size], wraw[n % 2][:, 0:size], ACT.Copy).then_inc(w_hi, 1)
                for m in (2 * cb, 2 * cb + 1):
                    act.wait_ge(pair_free[PLAN[f"dn{m}"] % 4], reads(PLAN[f"dn{m}"]) + 1)
                    if m == 0:
                        act.wait_ge(pe_done, fills("dn0"))
                    f(sqy[:, m, :], hT[:, m, :], ACT.Square).then_inc(S("sqy_done"), 1)
                    f(yT[:, m, :], hT[:, m, :], ACT.Copy, scale=nrm[:, 2 * KD + m:2 * KD + m + 1]).then_inc(S("yT_done"), 1)
            link(f(rsy[0:1, 0:1], ones[0:1, 0:1], ACT.Ln))
            ps = ready("ssy")
            link(f(rsy[:, 0:4], ps[:, 0:4], ACT.Ln, scale=1.0 / D, bias=C("eps")))
            link(f(rsy[0:TT[4], 4:5], ps[0:TT[4], 4:5], ACT.Ln, scale=1.0 / D, bias=C("eps", TT[4])))
            link(f(rsy[:, 0:4], rsy[:, 0:4], ACT.Exp, scale=-0.5))
            free(f(rsy[0:TT[4], 4:5], rsy[0:TT[4], 4:5], ACT.Exp, scale=-0.5), "ssy")
            act.wait_ge(pair_free[PLAN["ssy"] % 4], reads(PLAN["ssy"]) + 1)
            for i in range(NT):
                f(ysb[i][0:TT[i], 0:512], ready(f"y{i}")[0:TT[i], 0:512], ACT.Copy, scale=rsy[0:TT[i], i:i + 1]).then_inc(S("y_half"), 1)

        @block.vector
        def _(dve):
            v_ = nc.vector
            tt, ts, stt = v_.tensor_tensor, v_.tensor_scalar, v_.scalar_tensor_tensor
            chain = [0]

            def link(ins):
                chain[0] += 1
                ins.then_inc(dve_chain, 1)
                dve.wait_ge(dve_chain, chain[0])

            def ready(name):
                dve.wait_ge(pe_done, fills(name))
                return pairs[PLAN[name] % 4]

            def free(ins, name):
                ins.then_inc(pair_free[PLAN[name] % 4], 1)

            def lo(n):
                dve.wait_ge(w_hi, n + 1)
                size = block_size(n)
                tt(wlo[n % 2][:, 0:size], wraw[n % 2][:, 0:size], whi[n % 2][:, 0:size].bitcast(F32), ALU.subtract).then_inc(w_lo, 1)

            def rest(out, value, high):
                return tt(out, value, high.bitcast(F32), ALU.subtract)

            v_.memset(stat[:, :], 1.0).then_inc(S("stat_clear"), 1)
            dve.wait_ge(S("stat_clear"), 1)
            xsq = sqs[:, 0:2, :].rearrange("p a t -> p (a t)")[:, 0:D]
            for i in (1, 3):
                dve.wait_ge(x_loaded[i], 16)
                link(tt(xsq, X[:, i, :], X[:, i, :], ALU.mult))
                v_.reduce_sum(stat[:, i:i + 1], xsq, AX).then_inc(S("ssx2_done"), 1)
                dve.wait_ge(S("ssx2_done"), i // 2 + 1)
            dve.wait_ge(S("rs_done"), 1)
            for i in (0, 1, 2):
                ts(X[0:TT[i], i, :], X[0:TT[i], i, :], stat[0:TT[i], 8 + i:9 + i], None, ALU.mult).then_inc(S("xn_done"), 1)
            lo(0)
            dve.wait_ge(n_loaded, 16 * 5)
            for k in range(KD):
                dve.wait_ge(S("xhi_done"), k + 1)
                ps = ready(f"xT{k}")
                free(stt(xlo[:, k, 0:T], ps[:, 0:T], nrm[:, k:k + 1], xhi[:, k, 0:T].bitcast(F32), ALU.mult, ALU.subtract), f"xT{k}")
            lo(1)
            v_.memset(ckhi[:, :, T:TPAD].bitcast(F32), 0.0).then_inc(S("kr_pad"), 1)
            v_.memset(cklo[:, :, T:TPAD].bitcast(F32), 0.0)
            for m in range(3):
                if m == 2:
                    lo(2)
                free(v_.tensor_copy(split2(cq[:, m, :]), halves(ready(f"cq{m}"))), f"cq{m}")
            lo(3)
            dve.wait_ge(small_loaded, 16 * 3)
            for i in range(NT):
                ps = ready(f"tok{i}")
                dve.wait_ge(S("ssk_done"), i + 1)
                free(v_.tensor_copy(ctok[:, i, 0:KVL], ps[:, 0:KVL]), f"tok{i}")
            lo(4)
            ps = ready("kr")
            dve.wait_ge(S("kr_done"), 1)
            dve.wait_ge(S("pad_done"), 3)
            free(v_.tensor_copy(split2(grT[0:RANK, :]), halves(ps)[ROPE:ROPE + RANK]), "kr")
            lo(5)
            dve.wait_ge(S("rk_done"), 1)
            for i in range(NT):
                dve.wait_ge(pair_free[PLAN[f"tok{i}"] % 4], reads(PLAN[f"tok{i}"]) + 1)
                stt(ctok[:, i, 0:KVL], ctok[:, i, 0:KVL], stat[:, 24 + i:25 + i], kvn[:, :], ALU.mult, ALU.mult).then_inc(S("ctok_done"), 1)
            dve.wait_ge(pair_free[PLAN["ssq"] % 4], reads(PLAN["ssq"]) + 1)
            for m in range(3):
                ins = stt(cq[:, m, :], cq[:, m, :], nrm[:, 3 * KD + m:3 * KD + m + 1], rsb[:, :], ALU.mult, ALU.mult)
            ins.then_inc(S("qn_done"), 1)
            dve.wait_ge(S("qnhi_done"), 1)
            rest(qnlo[:, :, :], cq[:, :, :], qnhi[:, :, :]).then_inc(S("qnlo_done"), 1)
            ps = ready("kp")
            kv = ps[:, 0:NT * ROPE].rearrange("p (i d) -> p i d", d=ROPE)
            cos, sin = (C(x).rearrange("p (i d) -> p i d", d=ROPE) for x in ("cosk", "sink"))
            tt(rp[0][:, :, :], kv, cos, ALU.mult)
            tt(rp[1][:, :, 0:HALF], kv[:, :, HALF:ROPE], sin[:, :, 0:HALF], ALU.mult)
            free(tt(rp[1][:, :, HALF:ROPE], kv[:, :, 0:HALF], sin[:, :, HALF:ROPE], ALU.mult), "kp")
            dve.wait_ge(pair_free[PLAN["kp"] % 4], reads(PLAN["kp"]) + 1)
            for c in (256, 320):
                ins = tt(ctok[:, :, c:c + ROPE], rp[0][:, :, :], rp[1][:, :, :], ALU.add)
            ins.then_inc(S("ctok_done"), 1)
            for n in (6, 7, 8, 9):
                lo(n)
            for m in range(4):
                if m == 1:
                    lo(10)
                dve.wait_ge(S("ge_done"), m + 1)
                link(ts(gT[:, m, :], gT[:, m, :], 1.0, None, ALU.add))
                link(v_.reciprocal(gT[:, m, :], gT[:, m, :]))
                free(tt(split2(gT[:, m, :]), split2(gT[:, m, :]), halves(ready(f"g{m}")), ALU.mult), f"g{m}")
            lo(11)
            for j in range(3):
                ps = ready(f"ck{j}")
                if j < 2:
                    dve.wait_ge(S("ckhi_done"), j + 1)
                    rest(cklo[:, j, 0:T], ps[:, 0:T], ckhi[:, j, 0:T]).then_inc(S("cklo_done"), 1)
                    free(v_.tensor_copy(cks[:, j, :], ps[:, NP:T]), f"ck{j}")
                else:
                    free(v_.tensor_copy(kpT[:, :], ps[:, 0:T]), f"ck{j}")
            lo(12)
            for hh in range(2):
                ps = ready(f"sw{hh}")
                free(tt(split2(rsb[:, :]), halves(ps), split2(C("sinf")), ALU.mult), f"sw{hh}")
                link(tt(qpe[:, hh, :], qpe[:, hh, :], C("cosf"), ALU.mult))
                dve.wait_ge(pair_free[PLAN[f"sw{hh}"] % 4], reads(PLAN[f"sw{hh}"]) + 1)
                ins = tt(qpe[:, hh, :], qpe[:, hh, :], rsb[:, :], ALU.add)
                if hh == 0:
                    link(ins)
            ins.then_inc(S("qpe_done"), 1)
            for i in range(NT):
                free(v_.tensor_copy(vm[:, i, :], ready(f"vm{i}")[:, 0:512]), f"vm{i}")
            ps = ready("qlat")
            v_.tensor_copy(qlT[:, :, :, :], ps[:, 0:64].rearrange("p (r h b) -> p r h b", r=2, h=4)).then_inc(pair_free[PLAN["qlat"] % 4], 1)
            dve.wait_ge(pair_free[PLAN["qlat"] % 4], reads(PLAN["qlat"]) + 1)
            for rh in range(2):
                tt(prod[:, rh, :, :], qlT[:, rh, :, :], cks[:, rh:rh + 1, :].broadcast_to([P, 4, NB]), ALU.mult)
            dve.wait_ge(S("qpe_done"), 1)
            link(v_.memset(prod[:, 2, :, :], 0.0))
            for a in range(2):
                r = slice(64 * a, 64 * a + 64)
                ins = tt(prod[r, 2, a:4:2, :], qpe[r, :, NP:T], kpT[r, NP:T].unsqueeze(1).broadcast_to([64, 2, NB]), ALU.mult)
            ins.then_inc(S("prod_done"), 1)
            free(v_.tensor_copy(sn8, ready("snew")[0:NB, 0:4]), "snew")
            def cache_queries(y, gg):
                rows = slice(32 * gg, 32 * gg + 32)

                def twice(at, step):
                    return Qall[rows, :, at - at % 32:at - at % 32 + 32].rearrange("p b (d c) -> p b d c", d=2)[:, :, :, at % 16:at % 16 + 3 if step == 2 else at % 16 + 4:step]

                for rh in range(2):
                    src = qlT[32 * y:32 * y + 32, rh, :, :].rearrange("p h b -> p b h").unsqueeze(2).broadcast_to([32, NB, 2, 4])
                    v_.tensor_copy(twice(32 * (4 * rh + y) + 4 * gg, 1), src)
                aa, e = divmod(y, 2)
                src = qpe[64 * aa + 32 * e:64 * aa + 32 * e + 32, :, NP:T].rearrange("p q b -> p b q").unsqueeze(2).broadcast_to([32, NB, 2, 2])
                v_.tensor_copy(twice(32 * (8 + e) + 4 * gg + aa, 2), src).then_inc(S("Qall_done"), 1)

            dve.wait_ge(S("Qall_clear"), 1)

            def cache_keys(j, x):
                dve.wait_ge(S(f"kc_loaded{x}"), 32 + 32 * j)
                v_.transpose(KT[(x + 1) % 2][:, :, :, :].rearrange("p u c j -> p (u c j)").bitcast(U32), KC[x][:, :].bitcast(U32))
                for y in range(2):
                    ins = v_.transpose(KTp[(x + 1) % 2][y][:, :, :, :].rearrange("p u c j -> p (u c j)").bitcast(U32),
                                       KP[x][:, 512 * y:512 * y + 512].bitcast(U32))
                ins.then_inc(S("kt_done"), 1)

            U = NT * MH
            for u in range(U + 2):
                if u < U:
                    qb = u // MH
                    q0, nq, nk = P * qb, min(P, NP - P * qb), min(P * qb + P, NP)
                    s = 32 + 4 * (u % 2)
                    ps = ready(f"S{u}")
                    link(tt(ps[0:nq, q0:nk], ps[0:nq, q0:nk], C("cap", nq)[:, 0:nq], ALU.min))
                    link(v_.reduce_max(stat[0:nq, s:s + 1], ps[0:nq, 0:nk], AX))
                    ts(stat[0:nq, s + 1:s + 2], stat[0:nq, s:s + 1], -SCALE, None, ALU.mult).then_inc(S("nmax_done"), 1)
                    dve.wait_ge(pair_free[PLAN[f"S{u}"] % 4], reads(PLAN[f"S{u}"]) + 1)
                    link(v_.reciprocal(stat[0:nq, s + 3:s + 4], stat[0:nq, s + 2:s + 3]))
                    ts(pr[u % 2][0:nq, 0:nk], pr[u % 2][0:nq, 0:nk], stat[0:nq, s + 3:s + 4], None, ALU.mult).then_inc(S("pn_done"), 1)
                if u >= 2:
                    v = u - 2
                    qb, h = divmod(v, MH)
                    nq = min(P, NP - P * qb)
                    dve.wait_ge(S("omhi_done"), v + 1)
                    ins = rest(xlo[:, 4 + h, P * qb:P * qb + nq], ready(f"OM{v}")[:, 0:nq], xhi[:, 4 + h, P * qb:P * qb + nq])
                    free(ins, f"OM{v}")
                if u < NG * NG:
                    cache_queries(*divmod(u, NG))
                if u == 12:
                    cache_keys(0, 0)
            dve.wait_ge(out_done, 16 * 12)
            dve.wait_ge(S("ps_clear"), 2)

            def cache_max(j, x):
                n = 4 * j + x
                dve.wait_ge(S("sc_done"), n + 1)
                v_.reduce_max(mc[:, x:x + 1], pairs[2 * (x % 2)][:, 0:P], AX).then_inc(S("m_done"), 1)
                dve.wait_ge(S("m_done"), n + 1)
                ts(mc[:, 4 + x:5 + x], mc[:, x:x + 1], -SCALE, None, ALU.mult).then_inc(S("nm_done"), 1)

            def cache_probs(j, x):
                n = 4 * j + x
                p = 2 * (x % 2)
                dve.wait_ge(pair_free[p], reads(PLAN["cache0"] + p) + 2 * j + x // 2 + 1)
                v_.transpose(Pt[:, :, :].rearrange("p u j -> p (u j)").bitcast(U32), Pc[:, :].bitcast(U32)).then_inc(S("pt_done"), 1)
                dve.wait_ge(S("pt_done"), n + 1)
                for t in (2, 3):
                    for gg in range(NG):
                        at = 16 * (x % 2) + 4 * gg
                        ins = v_.tensor_copy(PS[x % 2][32 * gg:32 * gg + 32, 4 * t:4 * t + 4, at:at + 4], Pt[32 * t:32 * t + 32, :, 4 * gg:4 * gg + 4])
                ins.then_inc(S("ps_done"), 1)
                if x == 3:
                    v_.tensor_copy(ML[:, bass.ds(12 * j, 12)], mc).then_inc(S("ml_done"), 1)
                    dve.wait_ge(S("ml_done"), j + 1)

            with dve.Fori(0, NB // 2 - 1) as j:
                for x in range(4):
                    cache_keys(j + (x + 1) // 4, (x + 1) % 4)
                    cache_max(j, x)
                    cache_probs(j, x)
            for x in range(4):
                if x < 3:
                    cache_keys(NB // 2 - 1, x + 1)
                cache_max(NB // 2 - 1, x)
                cache_probs(NB // 2 - 1, x)
            dve.wait_ge(S("pv_done"), CHUNKS * NB)
            v_.memset(selw[:, :, :], 0.0)
            v_.memset(lgt[:, NT - 1, :], 0.0).then_inc(S("lgt_clear"), 1)

            def gate_min(i):
                dve.wait_ge(S("lga_done"), i + 1)
                r = TT[i]
                free(ts(lgs[0:r, i, :], ready(f"lg{i}")[0:r, 0:256], 0.0, None, ALU.min), f"lg{i}")

            mlv = ML.rearrange("p (j k b e) -> p k e j b", j=NB // 2, k=3, b=2)
            for e in range(2):
                v_.tensor_copy(Mc[:, e, :].rearrange("p (j b) -> p j b", b=2), mlv[:, 0, e])
                ins = v_.tensor_copy(Lc[:, e, :].rearrange("p (j b) -> p j b", b=2), mlv[:, 2, e])
            ins.then_inc(S("mc_done"), 1)
            free(v_.reduce_max(mx8, ready("mt")[0:NB, 0:2 * P].rearrange("p (x h) -> p h x", h=4), AX), "mt")
            dve.wait_ge(pair_free[PLAN["mt"] % 4], reads(PLAN["mt"]) + 1)
            link(tt(mx8, mx8, sn8, ALU.max))
            tt(w8, sn8, mx8, ALU.subtract).then_inc(S("d2_done"), 1)
            v_.tensor_copy(mexp.rearrange("p (x h) -> p x h", h=4), mx8.unsqueeze(1).broadcast_to([NB, 32, 4])).then_inc(S("mexp_done"), 1)
            gate_min(0)
            gate_min(1)
            dve.wait_ge(S("mexp_done"), 1)
            ready("mx")
            free(tt(Wc, Mc, pairs[PLAN["mx"] % 4][:, 0:NB].unsqueeze(1).broadcast_to([P, 2, NB]), ALU.subtract), "mx")
            dve.wait_ge(pair_free[PLAN["mx"] % 4], reads(PLAN["mx"]) + 1)
            gate_min(2)
            gate_min(3)
            dve.wait_ge(S("wexp_done"), 2)
            tt(Lc, Lc, Wc, ALU.mult).then_inc(S("lw_done"), 1)
            gate_min(4)
            free(tt(den8, ready("den")[0:NB, 0:4], w8, ALU.add), "den")
            dve.wait_ge(pair_free[PLAN["den"] % 4], reads(PLAN["den"]) + 1)
            link(v_.reciprocal(r8, den8))
            link(tt(wn8, w8, r8, ALU.mult))
            v_.tensor_copy(rexp.rearrange("p (x h) -> p x h", h=4), r8.unsqueeze(1).broadcast_to([NB, 32, 4]))
            tt(wx8.rearrange("p (h b) -> p h b", h=4), wn8.unsqueeze(2).broadcast_to([NB, 4, NB]),
               C("ident", NB)[:, 0:NB].unsqueeze(1).broadcast_to([NB, 4, NB]), ALU.mult).then_inc(S("rexp_done"), 1)
            dve.wait_ge(S("lgt_done"), 1)
            for i in range(NT):
                dve.wait_ge(pair_free[PLAN[f"lg{i}"] % 4], reads(PLAN[f"lg{i}"]) + 1)
                r = TT[i]
                tt(lgs[0:r, i, :], lgs[0:r, i, :], lgt[0:r, i, :], ALU.subtract).then_inc(S("lgs_done"), 1)
            dve.wait_ge(S("msk_loaded"), 16)
            for c in range(NT):
                dve.wait_ge(pair_free[PLAN[f"b{c}"] % 4], reads(PLAN[f"b{c}"]) + 1)

            def differences(lv):
                s = LEVELS[lv]
                n = 512 if s > 8 else NP
                nb = n // (2 * s)
                if lv >= 2:
                    dve.wait_ge(S("qk_done"), lv - 1)
                    dve.wait_ge(S("kd_done"), lv - 1)
                for q in range(2):
                    bb = bT[:, q, 0:n].rearrange("p (n a s) -> p n a s", a=2, s=s)
                    ee = Ee[lv % 2][:, q, 0:n].rearrange("p (n a s) -> p n a s", a=2, s=s)
                    mid = bb[:, :, 0, s - 1:s].broadcast_to([P, nb, s])
                    ins = tt(ee[:, :, 1, :], bb[:, :, 1, :], mid, ALU.subtract)
                ins.then_inc(S("diff_done"), 1)

            def keep_scores(lv):
                for c in range(NT):
                    if f"G{lv}.{c}" in PLAN:
                        n = min(P, NP - P * c)
                        ps = ready(f"G{lv}.{c}")
                        out = AT[0:n, c, :, 0:n].rearrange("p (a q) t -> p a q t", a=2)
                        if lv < NL:
                            data = ps[0:n, :].rearrange("p (q x) -> p q x", q=2)[:, :, 0:2 * n].rearrange("p q (a t) -> p a q t", a=2)
                        else:
                            data = ps[0:n, :].rearrange("p (a q t) -> p a q t", a=2, q=4)[:, :, 0:2, 0:n]
                        mask = msk[0:n, lv:lv + 1, 0:n].unsqueeze(1).broadcast_to([n, 2, 2, n])
                        free(v_.copy_predicated(out, mask.bitcast(U32), data), f"G{lv}.{c}")
                if lv == 0:
                    dve.wait_ge(S("decay_done"), 1)
                for b in NEW_STATES[lv]:
                    ps = ready(f"vb{b}")
                    for h in range(4):
                        a, q = h % 2, h // 2
                        r = slice(64 * a, 64 * a + 64)
                        ins = stt(states[r, b, q, :], ps[r, P * h:P * h + P], gk[r, q, NP + b:NP + b + 1], states[r, b, q, :], ALU.mult, ALU.add)
                    free(ins, f"vb{b}")

            def cache_sum(step):
                if step == 0:
                    ps = ready("rb")
                    link(tt(Wc, Wc, ps[:, 0:NB].unsqueeze(1).broadcast_to([P, 2, NB]), ALU.mult))
                    for e, sel in ((0, "sell"), (1, "selo")):
                        o = selw[:, :, 0:4] if e == 0 else otmp[:, 0, :].rearrange("p (b h) -> p b h", h=4)
                        ins = tt(o, Wc[:, e, :].unsqueeze(2).broadcast_to([P, NB, 4]), C(sel).unsqueeze(1).broadcast_to([P, NB, 4]), ALU.mult)
                    link(ins)
                    tt(selw[:, :, 0:4], selw[:, :, 0:4], otmp[:, 0, :].rearrange("p (b h) -> p b h", h=4), ALU.add).then_inc(S("selw_done"), 1)
                    free(v_.tensor_copy(wvb, ps[:, 512:544]), "rb")
                if step == 1:
                    free(v_.tensor_copy(osb[:, :, :], split2(ready("osum")[:, :])[:, :, 0:KVL]), "osum")
                    dve.wait_ge(S("selw_done"), 1)
                    dve.wait_ge(pair_free[PLAN["rb"] % 4], reads(PLAN["rb"]) + 1)
                    for rh in range(2):
                        ins = tt(otmp[:, rh, :].rearrange("p (h b) -> p h b", h=4), cks[:, rh:rh + 1, :].broadcast_to([P, 4, NB]),
                                 wvb.rearrange("p (h b) -> p h b", h=4), ALU.mult)
                    link(ins)
                if step == 2:
                    ps = ready("ol")
                    for rh in range(2):
                        for y in range(2):
                            o = 512 * y + P * rh
                            src = ps[:, o:o + P].rearrange("p (b h) -> p h b", b=4)[:, 0:4, :]
                            ins = tt(olat[:, rh, :].rearrange("p (h b) -> p h b", h=4)[:, :, 4 * y:4 * y + 4], src,
                                     otmp[:, rh, :].rearrange("p (h b) -> p h b", h=4)[:, :, 4 * y:4 * y + 4], ALU.add)
                    free(ins, "ol")
                if step == 3:
                    dve.wait_ge(S("omdhi_done"), 1)
                    ps = ready("omd")
                    rest(xlo[:, 4:8, NP:T], ps[:, 0:32].rearrange("p (h b) -> p h b", h=4), xhi[:, 4:8, NP:T]).then_inc(pair_free[PLAN["omd"] % 4], 1)
                    v_.memset(qd[:, :, :, :], 0.0).then_inc(S("qd_clear"), 1)
                    dve.wait_ge(S("qd_clear"), 1)
                    for a in range(2):
                        r = slice(64 * a, 64 * a + 64)
                        ins = v_.tensor_copy(qd[r, :, :, a], gq[r, :, NP:T].rearrange("p q b -> p b q"))
                    ins.then_inc(S("qd_done"), 1)

            differences(0)
            dve.wait_ge(S("clear_done"), 3)
            for lv in range(NL):
                n = 512 if LEVELS[lv] > 8 else NP
                if lv + 1 < NL:
                    differences(lv + 1)
                dve.wait_ge(S("E_done"), lv + 1)
                if lv >= 2:
                    dve.wait_ge(pe_done, fills(last_of_level(lv - 2)))
                for a in range(2):
                    r = slice(64 * a, 64 * a + 64)
                    out = QD[lv % 2][r, :, 0:1024].rearrange("p q (c a t) -> p q c a t", a=2, t=P)[:, :, :, a, :]
                    by_chunk = lambda x: x[r, :, 0:512].rearrange("p q (c t) -> p q c t", t=P)
                    ins = tt(out, by_chunk(gq), by_chunk(Ee[lv % 2]), ALU.mult)
                    if n == NP:
                        ins = tt(QD[lv % 2][r, :, 1024 + 16 * a:1040 + 16 * a], gq[r, :, 512:NP], Ee[lv % 2][r, :, 512:NP], ALU.mult)
                ins.then_inc(S("qk_done"), 1)
                if lv:
                    keep_scores(lv - 1)
                    if lv <= 4:
                        cache_sum(lv - 1)
            dve.wait_ge(S("qk_done"), NL)
            dve.wait_ge(S("kd_done"), NL)
            for c in range(NT):
                n = min(P, NP - P * c)
                e = P * c + n
                ins = tt(Ee[(NL + 1) % 2][:, :, P * c:e], bT[:, :, e - 1:e].broadcast_to([P, 2, n]), bT[:, :, P * c:e], ALU.subtract)
            ins.then_inc(S("diff_done"), 1)
            dve.wait_ge(S("E_done"), NL + 1)
            tt(qe[:, :, :], gq[:, :, 0:NP], Ee[NL % 2][:, :, :], ALU.mult)
            keep_scores(NL - 1)
            dve.wait_ge(S("E_done"), NL + 2)
            dve.wait_ge(pe_done, fills(last_of_level(NL - 1)))
            tt(kt[(NL + 1) % 2][:, :, :], gk[:, :, 0:NP], Ee[(NL + 1) % 2][:, :, :], ALU.mult).then_inc(S("qk_done"), 1)
            keep_scores(NL)
            lo(13)
            lo(14)
            dve.wait_ge(S("eb_done"), 2)
            for c in range(NT):
                ps = ready(f"s{c}")
                if c == 0:
                    free(v_.tensor_copy(Sst[0][:, :, :], ps[:, 0:256].rearrange("p (q v) -> p q v", q=2)), f"s{c}")
                    continue
                if c >= 2:
                    dve.wait_ge(pe_done, fills(f"o{c - 1}"))
                dve.wait_ge(pair_free[PLAN[f"s{c - 1}"] % 4], reads(PLAN[f"s{c - 1}"]) + 1)
                for q in range(2):
                    ins = stt(Sst[c % 2][:, q, :], Sst[(c - 1) % 2][:, q, :], el[:, q, c:c + 1], ps[:, P * q:P * q + P], ALU.mult, ALU.add)
                free(ins, f"s{c}")
            for h in range(4):
                dve.wait_ge(S("sqg_done"), h + 1)
                stt(oT[:, h, :], oT[:, h, :], nrm[:, 3 * KD + 3:3 * KD + 4], gT[:, h, :], ALU.mult, ALU.mult).then_inc(S("gated"), 1)
            for h in range(4 + 1):
                if h < 4:
                    dve.wait_ge(S("rsg_done"), h + 1)
                    dve.wait_ge(S("gated"), h + 1)
                    tt(oT[:, h, :], oT[:, h, :], rsg[h][:, :], ALU.mult).then_inc(S("og_done"), 1)
                if h:
                    dve.wait_ge(S("mixhi_done"), h)
                    rest(xlo[:, h - 1, 0:T], oT[:, h - 1, :], xhi[:, h - 1, 0:T]).then_inc(S("mixlo_done"), 1)
            def add_square(sq, squared, summed, m):
                dve.wait_ge(squared, m + 1)
                if m >= 2:
                    dve.wait_ge(summed, m - 1)
                tt(sq[:, 0, :], sq[:, 0, :], sq[:, m, :], ALU.add).then_inc(summed, 1)

            lo(15)
            for m in range(KD):
                if m in (2, 6):
                    lo(16 + m // 4)
                ps = ready(f"hT{m}")
                dve.wait_ge(pair_free[PLAN[f"wo{m}"] % 4], reads(PLAN[f"wo{m}"]) + 1)
                free(tt(hT[:, m, :], hT[:, m, :], ps[:, 0:T], ALU.add), f"hT{m}")
                if m >= 2:
                    add_square(sqf, S("sqf_done"), S("sumf_done"), m - 1)
            add_square(sqf, S("sqf_done"), S("sumf_done"), KD - 1)
            lo(18)
            dve.wait_ge(pair_free[PLAN["ssf"] % 4], reads(PLAN["ssf"]) + 1)
            for k in range(KD + 1):
                if k < KD:
                    if k >= 2:
                        dve.wait_ge(S("nlo_done"), k - 1)
                    stt(tf[k % 2][:, :], hT[:, k, :], nrm[:, KD + k:KD + k + 1], rsf[:, :], ALU.mult, ALU.mult).then_inc(S("tf_done"), 1)
                if k:
                    dve.wait_ge(S("nhi_done"), k)
                    rest(xlo[:, k - 1, 0:T], tf[(k - 1) % 2][:, :], xhi[:, k - 1, 0:T]).then_inc(S("nlo_done"), 1)
            dve.wait_ge(out_done, 16 * (12 + 2 + 16))
            base = PLAN["ffn0"]
            per = 4
            c0 = chain[0]
            with dve.Fori(0, DFF // 256) as j:
                def sigmoid(m):
                    dve.wait_ge(S("fe_done"), 2 * j + m + 1)
                    ts(fe[m][:, :], fe[m][:, :], 1.0, None, ALU.add).then_inc(dve_chain, 1)
                    dve.wait_ge(dve_chain, c0 + per * j + 2 * m + 1)
                    v_.reciprocal(fe[m][:, :], fe[m][:, :]).then_inc(dve_chain, 1)
                    dve.wait_ge(dve_chain, c0 + per * j + 2 * m + 2)
                    tt(split2(fe[m][:, :]), split2(fe[m][:, :]), halves(pairs[m]), ALU.mult).then_inc(pair_free[m], 1)

                def next_lo(s):
                    n = B_FFN + s
                    dve.wait_ge(w_hi, n + 3 + 2 * j)
                    tt(wlo[n % 2][:, :], wraw[n % 2][:, :], whi[n % 2][:, :].bitcast(F32), ALU.subtract).then_inc(w_lo, 1)

                sigmoid(0)
                next_lo(0)
                sigmoid(1)
                for m in range(2):
                    dve.wait_ge(pe_done, fills("ffn0") + 4 * j + 2 + m)
                    dve.wait_ge(pair_free[m], reads(base + m) + 1 + j)
                    tt(split2(fe[m][:, :]), split2(fe[m][:, :]), halves(pairs[2 + m]), ALU.mult).then_inc(pair_free[2 + m], 1)
                for m in range(2):
                    dve.wait_ge(S("hhi_done"), 2 * j + m + 1)
                    rest(hlo[:, bass.ds(2 * j + m, 1), :].rearrange("p a t -> p (a t)"), fe[m][:, :],
                         hhi[:, bass.ds(2 * j + m, 1), :].rearrange("p a t -> p (a t)")).then_inc(S("hlo_done"), 1)
                next_lo(1)
            chain[0] = c0 + per * (DFF // 256)
            for cb in range(4):
                for q in range(3):
                    n = B_DOWN + 3 * cb + q + 2
                    if n < B_DOWN + 12:
                        dve.wait_ge(w_hi, n + 1)
                        size = 256 * DPARTS[(q + 2) % 3][1]
                        tt(wlo[n % 2][:, 0:size], wraw[n % 2][:, 0:size], whi[n % 2][:, 0:size].bitcast(F32), ALU.subtract).then_inc(w_lo, 1)
                for m in (2 * cb, 2 * cb + 1):
                    free(tt(split2(hT[:, m, :]), split2(hT[:, m, :]), halves(ready(f"dn{m}")), ALU.add), f"dn{m}")
                    if m >= 2:
                        add_square(sqy, S("sqy_done"), S("sumy_done"), m - 1)
            add_square(sqy, S("sqy_done"), S("sumy_done"), KD - 1)
            dve.wait_ge(pair_free[PLAN["ssy"] % 4], reads(PLAN["ssy"]) + 1)
            for i in range(NT):
                dve.wait_ge(S("y_half"), i + 1)
                ps = ready(f"y{i}")
                free(ts(ysb[i][0:TT[i], 512:D], ps[0:TT[i], 512:D], rsy[0:TT[i], i:i + 1], None, ALU.mult), f"y{i}")


_INS = ["x_prompt", "x_sample", "cache_ckv", "cache_kpe", "state_gla", "page_table", "meta_tokens", "norm_mix", "w_in",
        "w_gk", "b_gk", "gla_norm", "q_norm", "kv_norm", "w_uq", "w_ukv", "w_out", "norm_ffn", "w_gate", "w_up", "w_down",
        "norm_final"]
_OUTS = [(1, SEQ, D), (NB, 1, D), (1, 1, NP, KVL), (1, 1, NP, ROPE), (1, 1, GH, DK, DV), (1, NB, 1, KVL), (1, NB, 1, ROPE),
         (1, NB, GH, DK, DV)]


def kernel(**inputs):
    import concourse.bacc as bacc
    from concourse.bass_utils import run_bass_kernel_spmd

    nc = bacc.Bacc("TRN2", target_bir_lowering=False, num_devices=1)
    arrays, ins = {}, []
    shaped = dict(zip(("c_all", "c_masks", "c_pick"), constants()))
    for name in _INS + list(shaped):
        a = np.ascontiguousarray(inputs[name] if name in inputs else shaped[name])
        arrays[f"in_{name}"] = a
        ins.append(nc.dram_tensor(f"in_{name}", a.shape, mybir.dt.from_np(a.dtype), kind="ExternalInput").ap())
    outs = [nc.dram_tensor(f"out_{i}", s, F32, kind="ExternalOutput").ap() for i, s in enumerate(_OUTS)]
    hybrid_decode_kernel(nc, ins, outs)
    r = run_bass_kernel_spmd(nc, [arrays], core_ids=[0])
    return tuple(r.results[0][f"out_{i}"] for i in range(len(_OUTS)))
```
